# Optimizing a Trainium2 kernel written in Bass

```python
import math
import jax, jax.numpy as jnp
from jax import lax
import numpy as np

D_MODEL = 1024
BATCH = 1
SEQ = 256
DEPTH = 2

GRID_W = 64
CTX_LEN = 256
N_MIXERS = 3
N_MOD = 9
FFN_HIDDEN = 256 * ((8 * D_MODEL + 767) // 768)
FFN_RESIDUAL = 0.5
DN_HEAD_DIM = 128
DN_HEADS = D_MODEL // DN_HEAD_DIM
DN_CONV = 5
DN_CHUNK = 64
SWA_HEAD_DIM = 64
SWA_HEADS = D_MODEL // SWA_HEAD_DIM
SWA_KV_HEADS = SWA_HEADS // 4
WINDOW = 128
ATTN_BLOCK = 128
RET_HEADS = 4
RET_QK_DIM = D_MODEL // RET_HEADS
RET_V_DIM = 2 * RET_QK_DIM
RET_CHUNK = 128
ROPE_BASE = 10000.0
EPS = 1e-6


def _rms_norm(x, gain):
    xf = x.astype(jnp.float32)
    y = xf * lax.rsqrt(jnp.mean(xf * xf, axis=-1, keepdims=True) + EPS)
    return (y * gain.astype(jnp.float32)).astype(x.dtype)

def _head_group_norm(x, gain):
    xf = x.astype(jnp.float32)
    mu = jnp.mean(xf, axis=-1, keepdims=True)
    var = jnp.mean(jnp.square(xf - mu), axis=-1, keepdims=True)
    return ((xf - mu) * lax.rsqrt(var + EPS) * gain.astype(jnp.float32)).astype(x.dtype)

def _l2_normalize(x):
    xf = x.astype(jnp.float32)
    return (xf * lax.rsqrt(jnp.sum(xf * xf, axis=-1, keepdims=True) + EPS)).astype(x.dtype)

def _modulated_norm(h, gain, shift, scale):
    return _rms_norm(h, gain) * (1.0 + scale) + shift

def _swiglu(h, w1, w2):
    a, b = jnp.split(h @ w1, 2, axis=-1)
    return (jax.nn.silu(a) * b) @ w2

def _rotary_tables(positions, n_freq):
    inv = ROPE_BASE ** (-jnp.arange(n_freq, dtype=jnp.float32) / n_freq)
    ang = jnp.concatenate([p.astype(jnp.float32)[:, None] * inv[None, :] for p in positions], axis=-1)
    return jnp.cos(ang), jnp.sin(ang)

def _rope(x, cos, sin):
    x1, x2 = jnp.split(x, 2, axis=-1)
    c = cos[:, None, :].astype(x.dtype)
    s = sin[:, None, :].astype(x.dtype)
    return jnp.concatenate([x1 * c - x2 * s, x1 * s + x2 * c], axis=-1)

def _short_conv(x, w):
    k = w.shape[0]
    return lax.conv_general_dilated(x, w[:, None, :], window_strides=(1,), padding=[(k // 2, k // 2)],
                                    dimension_numbers=('NWC', 'WIO', 'NWC'), feature_group_count=x.shape[-1])

def _join(a_ctx, a_lat, reverse):
    if reverse:
        a_ctx, a_lat = jnp.flip(a_ctx, 1), jnp.flip(a_lat, 1)
    return jnp.concatenate([a_ctx, a_lat], axis=1)

def _both_dirs(a_ctx, a_lat):
    return jnp.concatenate([_join(a_ctx, a_lat, False), _join(a_ctx, a_lat, True)], axis=0)

def _split_dirs(o, n_batch, ctx_len):
    of, ob = o[:n_batch], o[n_batch:]
    return (of[:, :ctx_len], of[:, ctx_len:], jnp.flip(ob[:, :ctx_len], 1), jnp.flip(ob[:, ctx_len:], 1))

def _to_chunks(a, size):
    n, t, h = a.shape[:3]
    a = a.astype(jnp.float32).reshape((n, t // size, size, h) + a.shape[3:])
    return jnp.moveaxis(a, 3, 1)

def _from_chunks(a):
    n, h, nc, c = a.shape[:4]
    return jnp.moveaxis(a, 1, 3).reshape((n, nc * c, h) + a.shape[4:])

def _gated_delta_chunked(q, k, v, g, beta):
    out_dtype = v.dtype
    n, t, h, dk = q.shape
    dv = v.shape[-1]
    q = _to_chunks(q, DN_CHUNK) * dk ** -0.5
    k = _to_chunks(k, DN_CHUNK)
    v = _to_chunks(v, DN_CHUNK)
    gc = jnp.cumsum(_to_chunks(g, DN_CHUNK), axis=-1)
    beta = _to_chunks(beta, DN_CHUNK)
    causal = jnp.tril(jnp.ones((DN_CHUNK, DN_CHUNK), bool))
    strict = jnp.tril(jnp.ones((DN_CHUNK, DN_CHUNK), bool), -1)
    decay = jnp.exp(jnp.where(causal, gc[..., :, None] - gc[..., None, :], -jnp.inf))
    kb = k * beta[..., None]
    lower = jnp.where(strict, jnp.einsum('nhcid,nhcjd->nhcij', kb, k) * decay, 0.0)
    rhs = jnp.concatenate([v * beta[..., None], kb * jnp.exp(gc)[..., None]], axis=-1)
    uw = lax.linalg.triangular_solve(lower, rhs, left_side=True, lower=True, unit_diagonal=True)
    u, w = uw[..., :dv], uw[..., dv:]
    qk = jnp.einsum('nhcid,nhcjd->nhcij', q, k) * decay
    qg = q * jnp.exp(gc)[..., None]
    g_last = gc[..., -1]
    kd = k * jnp.exp(g_last[..., None] - gc)[..., None]
    xs = tuple(jnp.moveaxis(a, 2, 0) for a in (u, w, qk, qg, kd, jnp.exp(g_last)))

    def step(state, inp):
        u_c, w_c, qk_c, qg_c, kd_c, a_c = inp
        v_new = u_c - jnp.einsum('nhik,nhkv->nhiv', w_c, state)
        o = jnp.einsum('nhik,nhkv->nhiv', qg_c, state) + jnp.einsum('nhij,nhjv->nhiv', qk_c, v_new)
        state = state * a_c[..., None, None] + jnp.einsum('nhjk,nhjv->nhkv', kd_c, v_new)
        return state, o

    _, o = lax.scan(step, jnp.zeros((n, h, dk, dv), jnp.float32), xs)
    return _from_chunks(jnp.moveaxis(o, 0, 2)).astype(out_dtype)

def _retention_log_decay():
    return jnp.log1p(-jnp.exp2(-5.0 - jnp.arange(RET_HEADS, dtype=jnp.float32)))

def _retention_chunked(q, k, v, log_gamma):
    out_dtype = v.dtype
    n, t, h, dk = q.shape
    dv = v.shape[-1]
    q = _to_chunks(q, RET_CHUNK)
    k = _to_chunks(k, RET_CHUNK) * dk ** -0.5
    v = _to_chunks(v, RET_CHUNK)
    pos = jnp.arange(RET_CHUNK, dtype=jnp.float32)
    lg = log_gamma[:, None]
    rel = pos[:, None] - pos[None, :]
    decay = jnp.exp(jnp.where(rel >= 0, lg[:, :, None] * rel, -jnp.inf))
    scores = jnp.einsum('nhcid,nhcjd->nhcij', q, k) * decay[:, None]
    o_intra = jnp.einsum('nhcij,nhcje->nhcie', scores, v)
    q_in = q * jnp.exp(lg * (pos + 1.0))[:, None, :, None]
    k_st = k * jnp.exp(lg * (RET_CHUNK - 1.0 - pos))[:, None, :, None]
    chunk_decay = jnp.exp(lg * RET_CHUNK)[:, :, None]

    def step(state, inp):
        q_c, k_c, v_c = inp
        o = jnp.einsum('nhid,nhde->nhie', q_c, state)
        state = state * chunk_decay + jnp.einsum('nhjd,nhje->nhde', k_c, v_c)
        return state, o

    xs = tuple(jnp.moveaxis(a, 2, 0) for a in (q_in, k_st, v))
    _, o_inter = lax.scan(step, jnp.zeros((n, h, dk, dv), jnp.float32), xs)
    return _from_chunks(o_intra + jnp.moveaxis(o_inter, 0, 2)).astype(out_dtype)

def _sink_softmax(logits, sink):
    sink_col = jnp.broadcast_to(sink.astype(jnp.float32)[None, :, :, None, None], logits.shape[:-1] + (1,))
    return jax.nn.softmax(jnp.concatenate([sink_col, logits], axis=-1), axis=-1)[..., 1:]

def _deltanet_mixer(hc, hx, w_in, conv_w, a_log, dt_bias, o_gain, w_out):
    n_batch, ctx_len = hx.shape[0], hc.shape[1]
    qkv_w = 3 * DN_HEADS * DN_HEAD_DIM
    z_w = DN_HEADS * DN_HEAD_DIM

    def project(h):
        n = h.shape[1]
        qkv, z, ab = jnp.split(h @ w_in, [qkv_w, qkv_w + z_w], axis=-1)
        qkv = jax.nn.silu(_short_conv(qkv, conv_w))
        q, k, v = [a.reshape(n_batch, n, DN_HEADS, DN_HEAD_DIM) for a in jnp.split(qkv, 3, axis=-1)]
        ab = ab.astype(jnp.float32).reshape(n_batch, n, 2, 2, DN_HEADS)
        g = -jnp.exp(a_log.astype(jnp.float32)) * jax.nn.softplus(ab[:, :, :, 0] + dt_bias.astype(jnp.float32))
        beta = jax.nn.sigmoid(ab[:, :, :, 1])
        return _l2_normalize(q), _l2_normalize(k), v, z.reshape(n_batch, n, DN_HEADS, DN_HEAD_DIM), g, beta

    qc, kc, vc, zc, gc, bc = project(hc)
    qx, kx, vx, zx, gx, bx = project(hx)
    g_all = jnp.concatenate([_join(gc[:, :, 0], gx[:, :, 0], False), _join(gc[:, :, 1], gx[:, :, 1], True)], axis=0)
    b_all = jnp.concatenate([_join(bc[:, :, 0], bx[:, :, 0], False), _join(bc[:, :, 1], bx[:, :, 1], True)], axis=0)
    o = _gated_delta_chunked(_both_dirs(qc, qx), _both_dirs(kc, kx), _both_dirs(vc, vx), g_all, b_all)
    ofc, ofx, obc, obx = _split_dirs(o, n_batch, ctx_len)

    def finish(o_f, o_b, z):
        y = _rms_norm(o_f + o_b, o_gain) * jax.nn.silu(z)
        return y.reshape(y.shape[0], y.shape[1], -1) @ w_out

    return finish(ofc, obc, zc), finish(ofx, obx, zx)

def _window_attention_mixer(hc, hx, w_qkv, q_gain, k_gain, sink, w_out, cos, sin):
    n_batch, n_tok = hx.shape[0], hx.shape[1]
    ctx_len = hc.shape[1]
    group = SWA_HEADS // SWA_KV_HEADS
    q_w = SWA_HEADS * SWA_HEAD_DIM
    kv_w = SWA_KV_HEADS * SWA_HEAD_DIM
    scale = SWA_HEAD_DIM ** -0.5
    sink_hg = sink.reshape(SWA_KV_HEADS, group)

    def project(h, rotate):
        n = h.shape[1]
        q, k, v = jnp.split(h @ w_qkv, [q_w, q_w + kv_w], axis=-1)
        q = _rms_norm(q.reshape(n_batch, n, SWA_HEADS, SWA_HEAD_DIM), q_gain)
        k = _rms_norm(k.reshape(n_batch, n, SWA_KV_HEADS, SWA_HEAD_DIM), k_gain)
        if rotate:
            q, k = _rope(q, cos, sin), _rope(k, cos, sin)
        q = (q * scale).reshape(n_batch, n, SWA_KV_HEADS, group, SWA_HEAD_DIM)
        return q, k, v.reshape(n_batch, n, SWA_KV_HEADS, SWA_HEAD_DIM)

    qc, kc, vc = project(hc, False)
    qx, kx, vx = project(hx, True)

    s_c = jnp.einsum('bqhgd,bkhd->bhgqk', qc, kc).astype(jnp.float32)
    p_c = _sink_softmax(s_c, sink_hg).astype(vc.dtype)
    oc = jnp.einsum('bhgqk,bkhd->bqhgd', p_c, vc).reshape(n_batch, ctx_len, q_w)

    span = ATTN_BLOCK + 2 * WINDOW
    pad = ((0, 0), (WINDOW, WINDOW), (0, 0), (0, 0))
    kp, vp = jnp.pad(kx, pad), jnp.pad(vx, pad)
    q_off = jnp.arange(ATTN_BLOCK)
    k_off = jnp.arange(span)

    def block(j):
        start = j * ATTN_BLOCK
        qb = lax.dynamic_slice_in_dim(qx, start, ATTN_BLOCK, axis=1)
        kb = lax.dynamic_slice_in_dim(kp, start, span, axis=1)
        vb = lax.dynamic_slice_in_dim(vp, start, span, axis=1)
        t_pos = start + q_off
        s_pos = start - WINDOW + k_off
        allowed = (jnp.abs(t_pos[:, None] - s_pos[None, :]) <= WINDOW) & (s_pos >= 0) & (s_pos < n_tok)
        s_ctx = jnp.einsum('bqhgd,bkhd->bhgqk', qb, kc).astype(jnp.float32)
        s_win = jnp.where(allowed, jnp.einsum('bqhgd,bkhd->bhgqk', qb, kb).astype(jnp.float32), -jnp.inf)
        p = _sink_softmax(jnp.concatenate([s_ctx, s_win], axis=-1), sink_hg).astype(vb.dtype)
        return (jnp.einsum('bhgqk,bkhd->bqhgd', p[..., :ctx_len], vc)
                + jnp.einsum('bhgqk,bkhd->bqhgd', p[..., ctx_len:], vb))

    ox = lax.map(block, jnp.arange(n_tok // ATTN_BLOCK))
    ox = jnp.moveaxis(ox, 0, 1).reshape(n_batch, n_tok, q_w)
    return oc @ w_out, ox @ w_out

def _retention_mixer(hc, hx, w_in, gn_gain, w_out, cos, sin):
    n_batch, ctx_len = hx.shape[0], hc.shape[1]
    qk_w = RET_HEADS * RET_QK_DIM
    v_w = RET_HEADS * RET_V_DIM

    def project(h):
        n = h.shape[1]
        q, k, v, gf, gb = jnp.split(h @ w_in, [qk_w, 2 * qk_w, 2 * qk_w + v_w, 2 * qk_w + 2 * v_w], axis=-1)
        hq = lambda a: a.reshape(n_batch, n, RET_HEADS, RET_QK_DIM)
        hv = lambda a: a.reshape(n_batch, n, RET_HEADS, RET_V_DIM)
        return hq(q), hq(k), hv(v), hv(gf), hv(gb)

    qc, kc, vc, gfc, gbc = project(hc)
    qx, kx, vx, gfx, gbx = project(hx)
    qx, kx = _rope(qx, cos, sin), _rope(kx, cos, sin)
    o = _retention_chunked(_both_dirs(qc, qx), _both_dirs(kc, kx), _both_dirs(vc, vx), _retention_log_decay())
    ofc, ofx, obc, obx = _split_dirs(o, n_batch, ctx_len)
    gain = gn_gain.reshape(2, RET_HEADS, RET_V_DIM)

    def finish(o_f, o_b, g_f, g_b):
        y = (jax.nn.silu(g_f) * _head_group_norm(o_f, gain[0]) + jax.nn.silu(g_b) * _head_group_norm(o_b, gain[1]))
        return y.reshape(y.shape[0], y.shape[1], -1) @ w_out

    return finish(ofc, obc, gfc, gbc), finish(ofx, obx, gfx, gbx)

def first_inputs(seed: int = 0) -> dict:
    key = jax.random.key(seed)
    ks = jax.random.split(key, 24)
    d, f = D_MODEL, FFN_HIDDEN
    n_dn, n_swa, n_ret = (len(range(kind, DEPTH, N_MIXERS)) for kind in range(N_MIXERS))

    def nrm(k, shape, std):
        return std * jax.random.normal(k, shape, jnp.float32)

    dn_in = 4 * DN_HEADS * DN_HEAD_DIM + 4 * DN_HEADS
    swa_in = (SWA_HEADS + 2 * SWA_KV_HEADS) * SWA_HEAD_DIM
    ret_v = RET_HEADS * RET_V_DIM
    ret_in = 2 * RET_HEADS * RET_QK_DIM + 3 * ret_v
    dt = jnp.exp(jax.random.uniform(ks[12], (n_dn, 2, DN_HEADS), jnp.float32, math.log(1e-3), math.log(1e-1)))
    return {
        "x": nrm(ks[0], (BATCH, SEQ, d), 1.0),
        "c": nrm(ks[1], (BATCH, d), 1.0),
        "ctx": nrm(ks[2], (BATCH, CTX_LEN, d), 1.0),
        "c_ctx": nrm(ks[3], (d,), 1.0),
        "ada_w": nrm(ks[4], (DEPTH, d, N_MOD * d), 0.5 * d ** -0.5),
        "ada_b": nrm(ks[5], (DEPTH, N_MOD * d), 0.02),
        "norm_g": 1.0 + nrm(ks[6], (DEPTH, 3, d), 0.02),
        "ffn_w1": nrm(ks[7], (DEPTH, 2, d, 2 * f), d ** -0.5),
        "ffn_w2": nrm(ks[8], (DEPTH, 2, f, d), f ** -0.5),
        "dn_w_in": nrm(ks[9], (n_dn, d, dn_in), d ** -0.5),
        "dn_conv": nrm(ks[10], (n_dn, DN_CONV, 3 * DN_HEADS * DN_HEAD_DIM), DN_CONV ** -0.5),
        "dn_a_log": jnp.log(jax.random.uniform(ks[11], (n_dn, 2, DN_HEADS), jnp.float32, 1.0, 16.0)),
        "dn_dt_bias": dt + jnp.log(-jnp.expm1(-dt)),
        "dn_o_gain": 1.0 + nrm(ks[13], (n_dn, DN_HEAD_DIM), 0.02),
        "dn_w_out": nrm(ks[14], (n_dn, DN_HEADS * DN_HEAD_DIM, d), (DN_HEADS * DN_HEAD_DIM) ** -0.5),
        "swa_w_qkv": nrm(ks[15], (n_swa, d, swa_in), d ** -0.5),
        "swa_q_gain": 1.0 + nrm(ks[16], (n_swa, SWA_HEAD_DIM), 0.02),
        "swa_k_gain": 1.0 + nrm(ks[17], (n_swa, SWA_HEAD_DIM), 0.02),
        "swa_sink": nrm(ks[18], (n_swa, SWA_HEADS), 1.0),
        "swa_w_out": nrm(ks[19], (n_swa, SWA_HEADS * SWA_HEAD_DIM, d), (SWA_HEADS * SWA_HEAD_DIM) ** -0.5),
        "ret_w_in": nrm(ks[20], (n_ret, d, ret_in), d ** -0.5),
        "ret_gn_gain": 1.0 + nrm(ks[21], (n_ret, 2, ret_v), 0.02),
        "ret_w_out": nrm(ks[22], (n_ret, ret_v, d), ret_v ** -0.5),
    }

def first_block(x, c, ctx, c_ctx, ada_w, ada_b, norm_g, ffn_w1, ffn_w2, dn_w_in, dn_conv, dn_a_log, dn_dt_bias,
              dn_o_gain, dn_w_out, swa_w_qkv, swa_q_gain, swa_k_gain, swa_sink, swa_w_out, ret_w_in, ret_gn_gain,
              ret_w_out):
    n_batch, n_tok, d = x.shape
    ROWS = n_tok // GRID_W
    rows = jnp.repeat(jnp.arange(ROWS), GRID_W)
    cols = jnp.tile(jnp.arange(GRID_W), ROWS)
    swa_cos, swa_sin = _rotary_tables((rows, cols), SWA_HEAD_DIM // 4)
    ret_cos, ret_sin = _rotary_tables((jnp.arange(n_tok),), RET_QK_DIM // 2)
    cond_x = jax.nn.silu(c)
    cond_c = jax.nn.silu(c_ctx)

    for i in range(DEPTH):
        kind, slot, last = i % N_MIXERS, i // N_MIXERS, i == DEPTH - 1
        mx = (cond_x @ ada_w[i] + ada_b[i]).reshape(n_batch, 3, 3, 1, d)
        mc = (cond_c @ ada_w[i] + ada_b[i]).reshape(3, 3, d)

        x = x + FFN_RESIDUAL * mx[:, 0, 2] * _swiglu(
            _modulated_norm(x, norm_g[i, 0], mx[:, 0, 0], mx[:, 0, 1]), ffn_w1[i, 0], ffn_w2[i, 0])
        ctx = ctx + FFN_RESIDUAL * mc[0, 2] * _swiglu(
            _modulated_norm(ctx, norm_g[i, 0], mc[0, 0], mc[0, 1]), ffn_w1[i, 0], ffn_w2[i, 0])

        hx = _modulated_norm(x, norm_g[i, 1], mx[:, 1, 0], mx[:, 1, 1])
        hc = _modulated_norm(ctx, norm_g[i, 1], mc[1, 0], mc[1, 1])
        if kind == 0:
            oc, ox = _deltanet_mixer(hc, hx, dn_w_in[slot], dn_conv[slot], dn_a_log[slot], dn_dt_bias[slot],
                                     dn_o_gain[slot], dn_w_out[slot])
        elif kind == 1:
            oc, ox = _window_attention_mixer(hc, hx, swa_w_qkv[slot], swa_q_gain[slot], swa_k_gain[slot],
                                             swa_sink[slot], swa_w_out[slot], swa_cos, swa_sin)
        else:
            oc, ox = _retention_mixer(hc, hx, ret_w_in[slot], ret_gn_gain[slot], ret_w_out[slot], ret_cos, ret_sin)
        x = x + mx[:, 1, 2] * ox

        x = x + FFN_RESIDUAL * mx[:, 2, 2] * _swiglu(
            _modulated_norm(x, norm_g[i, 2], mx[:, 2, 0], mx[:, 2, 1]), ffn_w1[i, 1], ffn_w2[i, 1])
        if not last:
            ctx = ctx + mc[1, 2] * oc
            ctx = ctx + FFN_RESIDUAL * mc[2, 2] * _swiglu(
                _modulated_norm(ctx, norm_g[i, 2], mc[2, 0], mc[2, 1]), ffn_w1[i, 1], ffn_w2[i, 1])
    return x


DEPTH_2 = 1

MEM_LEN = 256
NEG_INF = -1e30

CONV_DIM = D_MODEL
CONV_KERNEL = 31

SSD_INNER = 2 * D_MODEL
SSD_HEAD_DIM = 64
SSD_HEADS = SSD_INNER // SSD_HEAD_DIM
SSD_GROUPS = 4
SSD_STATE = 128
SSD_CONV = 4
SSD_CHUNK = 128
SSD_XBC = SSD_INNER + 2 * SSD_GROUPS * SSD_STATE

ATTN_HEADS = 16
ATTN_KV_HEADS = 4
ATTN_HEAD_DIM = 64
ATTN_DIM = ATTN_HEADS * ATTN_HEAD_DIM
ATTN_KV_DIM = ATTN_KV_HEADS * ATTN_HEAD_DIM
ATTN_WINDOW = 128

REL_BUCKETS = 32
REL_MAX_DIST = 128

XATTN_HEADS = 4
XATTN_HEAD_DIM = D_MODEL // XATTN_HEADS

N_BRANCH = 3
MLP_HIDDEN = 4 * D_MODEL

OFF_CONV = 0
OFF_Z = OFF_CONV + 2 * CONV_DIM
OFF_XBC = OFF_Z + SSD_INNER
OFF_DT = OFF_XBC + SSD_XBC
OFF_Q = OFF_DT + SSD_HEADS
OFF_K = OFF_Q + ATTN_DIM
OFF_V = OFF_K + ATTN_KV_DIM
OFF_GATE = OFF_V + ATTN_KV_DIM
IN_COLS = OFF_GATE + N_BRANCH * D_MODEL


def rms_norm(x, g):
    x32 = x.astype(jnp.float32)
    y = x32 * lax.rsqrt(jnp.mean(x32 * x32, axis=-1, keepdims=True) + EPS)
    return (y * g.astype(jnp.float32)).astype(x.dtype)

def layer_norm(x, g, b):
    x32 = x.astype(jnp.float32)
    mu = jnp.mean(x32, axis=-1, keepdims=True)
    xc = x32 - mu
    y = xc * lax.rsqrt(jnp.mean(xc * xc, axis=-1, keepdims=True) + EPS)
    return (y * g.astype(jnp.float32) + b.astype(jnp.float32)).astype(x.dtype)

def causal_depthwise_conv(x, w, b):
    k, c = w.shape
    y = lax.conv_general_dilated(
        x, w[:, None, :].astype(x.dtype), window_strides=(1,), padding=[(k - 1, 0)],
        dimension_numbers=("NWC", "WIO", "NWC"), feature_group_count=c)
    return y + b.astype(x.dtype)

def conformer_conv_branch(u, dw_w, dw_b, ln_g, ln_b):
    a, gate = jnp.split(u, 2, axis=-1)
    h = a * jax.nn.sigmoid(gate)
    h = causal_depthwise_conv(h, dw_w, dw_b)
    h = layer_norm(h, ln_g, ln_b)
    return jax.nn.silu(h)

def segsum_exp(a):
    t = a.shape[-1]
    cs = jnp.cumsum(a, axis=-1)
    diff = cs[..., :, None] - cs[..., None, :]
    mask = jnp.tril(jnp.ones((t, t), dtype=bool))
    return jnp.where(mask, jnp.exp(jnp.where(mask, diff, 0.0)), 0.0)

def ssd_chunked(x, dt, a, bm, cm):
    b, l, h, p = x.shape
    g, n = bm.shape[-2:]
    r = h // g
    q = SSD_CHUNK
    nc = l // q
    xdt = (x * dt[..., None].astype(x.dtype)).reshape(b, nc, q, g, r, p)
    bc = bm.reshape(b, nc, q, g, n)
    cc = cm.reshape(b, nc, q, g, n)
    da = (dt * a).reshape(b, nc, q, g, r).transpose(0, 1, 3, 4, 2)
    cs = jnp.cumsum(da, axis=-1)
    decay = segsum_exp(da).astype(x.dtype)
    cb = jnp.einsum("bcqgn,bcsgn->bcgqs", cc, bc)
    scores = cb[:, :, :, None] * decay
    y_diag = jnp.einsum("bcgrqs,bcsgrp->bcqgrp", scores, xdt)
    decay_to_end = jnp.exp(cs[..., -1:] - cs).astype(x.dtype)
    chunk_states = jnp.einsum("bcqgn,bcgrq,bcqgrp->bcgrpn", bc, decay_to_end, xdt)
    chunk_decay = jnp.exp(cs[..., -1])

    def step(state, inp):
        s_c, d_c = inp
        return state * d_c[..., None, None] + s_c, state

    init = jnp.zeros((b, g, r, p, n), jnp.float32)
    _, states_in = lax.scan(
        step, init,
        (jnp.moveaxis(chunk_states.astype(jnp.float32), 1, 0), jnp.moveaxis(chunk_decay, 1, 0)))
    states_in = jnp.moveaxis(states_in, 0, 1).astype(x.dtype)
    decay_from_start = jnp.exp(cs).astype(x.dtype)
    y_off = jnp.einsum("bcqgn,bcgrpn,bcgrq->bcqgrp", cc, states_in, decay_from_start)
    return (y_diag + y_off).reshape(b, l, h, p)

def ssd_branch(z, xbc, dt_raw, conv_w, conv_b, dt_bias, a_log, d_skip, norm_g):
    b, l, _ = xbc.shape
    xbc = jax.nn.silu(causal_depthwise_conv(xbc, conv_w, conv_b))
    xs = xbc[..., :SSD_INNER].reshape(b, l, SSD_HEADS, SSD_HEAD_DIM)
    bm = xbc[..., SSD_INNER:SSD_INNER + SSD_GROUPS * SSD_STATE].reshape(b, l, SSD_GROUPS, SSD_STATE)
    cm = xbc[..., SSD_INNER + SSD_GROUPS * SSD_STATE:].reshape(b, l, SSD_GROUPS, SSD_STATE)
    dt = jax.nn.softplus(dt_raw.astype(jnp.float32) + dt_bias.astype(jnp.float32))
    a = -jnp.exp(a_log.astype(jnp.float32))
    y = ssd_chunked(xs, dt, a, bm, cm) + xs * d_skip[:, None].astype(xs.dtype)
    y = y.reshape(b, l, SSD_INNER) * jax.nn.silu(z)
    y = rms_norm(y.reshape(b, l, SSD_GROUPS, SSD_INNER // SSD_GROUPS),
                 norm_g.reshape(SSD_GROUPS, SSD_INNER // SSD_GROUPS))
    return y.reshape(b, l, SSD_INNER)

def t5_band_bias(rel_table):
    qi = jnp.arange(ATTN_BLOCK)[:, None] + ATTN_BLOCK
    kj = jnp.arange(2 * ATTN_BLOCK)[None, :]
    dist = qi - kj
    max_exact = REL_BUCKETS // 2
    d = jnp.maximum(dist, 1).astype(jnp.float32)
    large = max_exact + (jnp.log(d / max_exact) / math.log(REL_MAX_DIST / max_exact)
                         * (REL_BUCKETS - max_exact)).astype(jnp.int32)
    large = jnp.minimum(large, REL_BUCKETS - 1)
    bucket = jnp.where(dist < max_exact, jnp.maximum(dist, 0), large)
    bias = jnp.transpose(rel_table[bucket], (2, 0, 1)).astype(jnp.float32)
    return bias, dist

def swa_branch(q, k, v, q_g, k_g, sinks, rel_bias, band_dist):
    b, l, _ = q.shape
    nb = l // ATTN_BLOCK
    r = ATTN_HEADS // ATTN_KV_HEADS
    q = rms_norm(q.reshape(b, l, ATTN_HEADS, ATTN_HEAD_DIM), q_g)
    k = rms_norm(k.reshape(b, l, ATTN_KV_HEADS, ATTN_HEAD_DIM), k_g)
    v = v.reshape(b, l, ATTN_KV_HEADS, ATTN_HEAD_DIM)

    def band(t):
        tp = jnp.pad(t, ((0, 0), (ATTN_BLOCK, 0), (0, 0), (0, 0)))
        prev = tp[:, :l].reshape(b, nb, ATTN_BLOCK, ATTN_KV_HEADS, ATTN_HEAD_DIM)
        cur = t.reshape(b, nb, ATTN_BLOCK, ATTN_KV_HEADS, ATTN_HEAD_DIM)
        return jnp.concatenate([prev, cur], axis=2)

    kb, vb = band(k), band(v)
    qb = q.reshape(b, nb, ATTN_BLOCK, ATTN_KV_HEADS, r, ATTN_HEAD_DIM)
    logits = jnp.einsum("bnqgrd,bnkgd->bngrqk", qb, kb).astype(jnp.float32) * (ATTN_HEAD_DIM ** -0.5)
    logits = logits + rel_bias.reshape(ATTN_KV_HEADS, r, ATTN_BLOCK, 2 * ATTN_BLOCK)
    key_pos = (jnp.arange(nb)[:, None] * ATTN_BLOCK - ATTN_BLOCK
               + jnp.arange(2 * ATTN_BLOCK)[None, :])
    in_window = (band_dist >= 0) & (band_dist < ATTN_WINDOW)
    mask = in_window[None] & (key_pos >= 0)[:, None, :]
    logits = jnp.where(mask[None, :, None, None], logits, NEG_INF)
    sink = sinks.astype(jnp.float32).reshape(ATTN_KV_HEADS, r)[None, None, :, :, None, None]
    m = jnp.maximum(jnp.max(logits, axis=-1, keepdims=True), sink)
    pexp = jnp.exp(logits - m)
    probs = pexp / (jnp.sum(pexp, axis=-1, keepdims=True) + jnp.exp(sink - m))
    out = jnp.einsum("bngrqk,bnkgd->bnqgrd", probs.astype(v.dtype), vb)
    return out.reshape(b, l, ATTN_DIM)

def memory_cross_attention(h, mem_h, w_q, w_kv, q_g, k_g, w_o):
    b, l, _ = h.shape
    m = mem_h.shape[1]
    q = rms_norm((h @ w_q).reshape(b, l, XATTN_HEADS, XATTN_HEAD_DIM), q_g)
    kv = mem_h @ w_kv
    k = rms_norm(kv[..., :D_MODEL].reshape(b, m, XATTN_HEADS, XATTN_HEAD_DIM), k_g)
    v = kv[..., D_MODEL:].reshape(b, m, XATTN_HEADS, XATTN_HEAD_DIM)
    logits = jnp.einsum("bqhd,bkhd->bhqk", q, k).astype(jnp.float32) * (XATTN_HEAD_DIM ** -0.5)
    probs = jax.nn.softmax(logits, axis=-1)
    out = jnp.einsum("bhqk,bkhd->bqhd", probs.astype(v.dtype), v).reshape(b, l, D_MODEL)
    return out @ w_o

def second_inputs(seed: int = 0) -> dict:
    key = jax.random.key(seed)
    ks = iter(jax.random.split(key, 48))
    f32 = jnp.float32
    L = DEPTH_2

    def nrm(shape, scale):
        return jax.random.normal(next(ks), shape, f32) * scale

    def gain(shape):
        return 1.0 + nrm(shape, 0.02)

    out_scale = (2.0 * DEPTH_2) ** -0.5
    dt0 = jnp.exp(jax.random.uniform(next(ks), (L, SSD_HEADS), f32, math.log(1e-3), math.log(1e-1)))
    return {
        "x": nrm((BATCH, SEQ, D_MODEL), 1.0),
        "mem": nrm((BATCH, MEM_LEN, D_MODEL), 1.0),
        "rel_table": nrm((REL_BUCKETS, ATTN_HEADS), 0.1),
        "norm_mix": gain((L, D_MODEL)),
        "w_in": nrm((L, D_MODEL, IN_COLS), D_MODEL ** -0.5),
        "gate_bias": nrm((L, N_BRANCH, D_MODEL), 0.01),
        "conv_dw_w": nrm((L, CONV_KERNEL, CONV_DIM), CONV_KERNEL ** -0.5),
        "conv_dw_b": nrm((L, CONV_DIM), 0.01),
        "conv_ln_g": gain((L, CONV_DIM)),
        "conv_ln_b": nrm((L, CONV_DIM), 0.01),
        "w_conv_out": nrm((L, CONV_DIM, D_MODEL), CONV_DIM ** -0.5),
        "ssd_conv_w": nrm((L, SSD_CONV, SSD_XBC), SSD_CONV ** -0.5),
        "ssd_conv_b": nrm((L, SSD_XBC), 0.01),
        "ssd_dt_bias": dt0 + jnp.log(-jnp.expm1(-dt0)),
        "ssd_A_log": jnp.log(jax.random.uniform(next(ks), (L, SSD_HEADS), f32, 1.0, 16.0)),
        "ssd_D": gain((L, SSD_HEADS)),
        "ssd_norm_g": gain((L, SSD_INNER)),
        "w_ssd_out": nrm((L, SSD_INNER, D_MODEL), SSD_INNER ** -0.5),
        "attn_q_norm": gain((L, ATTN_HEAD_DIM)),
        "attn_k_norm": gain((L, ATTN_HEAD_DIM)),
        "attn_sinks": nrm((L, ATTN_HEADS), 0.5),
        "w_attn_out": nrm((L, ATTN_DIM, D_MODEL), ATTN_DIM ** -0.5),
        "w_mix_out": nrm((L, D_MODEL, D_MODEL), out_scale * D_MODEL ** -0.5),
        "norm_xattn": gain((L, D_MODEL)),
        "norm_mem": gain((L, D_MODEL)),
        "w_xq": nrm((L, D_MODEL, D_MODEL), D_MODEL ** -0.5),
        "w_xkv": nrm((L, D_MODEL, 2 * D_MODEL), D_MODEL ** -0.5),
        "xattn_q_norm": gain((L, XATTN_HEAD_DIM)),
        "xattn_k_norm": gain((L, XATTN_HEAD_DIM)),
        "w_xo": nrm((L, D_MODEL, D_MODEL), out_scale * D_MODEL ** -0.5),
        "norm_mlp": gain((L, D_MODEL)),
        "w_mlp_up": nrm((L, D_MODEL, MLP_HIDDEN), D_MODEL ** -0.5),
        "w_mlp_down": nrm((L, MLP_HIDDEN, D_MODEL), out_scale * MLP_HIDDEN ** -0.5),
    }

def second_block(x, mem, rel_table, norm_mix, w_in, gate_bias, conv_dw_w, conv_dw_b, conv_ln_g,
              conv_ln_b, w_conv_out, ssd_conv_w, ssd_conv_b, ssd_dt_bias, ssd_A_log, ssd_D,
              ssd_norm_g, w_ssd_out, attn_q_norm, attn_k_norm, attn_sinks, w_attn_out, w_mix_out,
              norm_xattn, norm_mem, w_xq, w_xkv, xattn_q_norm, xattn_k_norm, w_xo, norm_mlp,
              w_mlp_up, w_mlp_down):
    b, l, _ = x.shape
    rel_bias, band_dist = t5_band_bias(rel_table)
    h = x
    for i in range(DEPTH_2):
        u = rms_norm(h, norm_mix[i])
        proj = u @ w_in[i]
        y_a = conformer_conv_branch(proj[..., OFF_CONV:OFF_Z], conv_dw_w[i], conv_dw_b[i],
                                    conv_ln_g[i], conv_ln_b[i]) @ w_conv_out[i]
        y_b = ssd_branch(proj[..., OFF_Z:OFF_XBC], proj[..., OFF_XBC:OFF_DT], proj[..., OFF_DT:OFF_Q],
                         ssd_conv_w[i], ssd_conv_b[i], ssd_dt_bias[i], ssd_A_log[i], ssd_D[i],
                         ssd_norm_g[i]) @ w_ssd_out[i]
        y_c = swa_branch(proj[..., OFF_Q:OFF_K], proj[..., OFF_K:OFF_V], proj[..., OFF_V:OFF_GATE],
                         attn_q_norm[i], attn_k_norm[i], attn_sinks[i], rel_bias, band_dist) @ w_attn_out[i]
        gates = jax.nn.sigmoid(proj[..., OFF_GATE:IN_COLS].reshape(b, l, N_BRANCH, D_MODEL)
                               + gate_bias[i].astype(proj.dtype))
        merged = gates[..., 0, :] * y_a + gates[..., 1, :] * y_b + gates[..., 2, :] * y_c
        h = h + merged @ w_mix_out[i]
        h = h + memory_cross_attention(rms_norm(h, norm_xattn[i]), rms_norm(mem, norm_mem[i]),
                                       w_xq[i], w_xkv[i], xattn_q_norm[i], xattn_k_norm[i], w_xo[i])
        u = rms_norm(h, norm_mlp[i])
        h = h + jnp.square(jax.nn.relu(u @ w_mlp_up[i])) @ w_mlp_down[i]
    return h


def setup_inputs(seed=0):
    out = dict(first_inputs(seed))
    for name, value in second_inputs(seed + 1).items():
        if name != "x":
            out[name + "_2"] = value
    return out


def reference(
    x, c, ctx, c_ctx, ada_w, ada_b, norm_g, ffn_w1, ffn_w2, dn_w_in, dn_conv, dn_a_log,
    dn_dt_bias, dn_o_gain, dn_w_out, swa_w_qkv, swa_q_gain, swa_k_gain, swa_sink, swa_w_out,
    ret_w_in, ret_gn_gain, ret_w_out, mem_2, rel_table_2, norm_mix_2, w_in_2, gate_bias_2,
    conv_dw_w_2, conv_dw_b_2, conv_ln_g_2, conv_ln_b_2, w_conv_out_2, ssd_conv_w_2,
    ssd_conv_b_2, ssd_dt_bias_2, ssd_A_log_2, ssd_D_2, ssd_norm_g_2, w_ssd_out_2, attn_q_norm_2,
    attn_k_norm_2, attn_sinks_2, w_attn_out_2, w_mix_out_2, norm_xattn_2, norm_mem_2, w_xq_2,
    w_xkv_2, xattn_q_norm_2, xattn_k_norm_2, w_xo_2, norm_mlp_2, w_mlp_up_2, w_mlp_down_2,
):
    x = first_block(
        x, c, ctx, c_ctx, ada_w, ada_b, norm_g, ffn_w1, ffn_w2, dn_w_in, dn_conv, dn_a_log,
        dn_dt_bias, dn_o_gain, dn_w_out, swa_w_qkv, swa_q_gain, swa_k_gain, swa_sink, swa_w_out,
        ret_w_in, ret_gn_gain, ret_w_out,
    )
    return second_block(
        x, mem_2, rel_table_2, norm_mix_2, w_in_2, gate_bias_2, conv_dw_w_2, conv_dw_b_2,
        conv_ln_g_2, conv_ln_b_2, w_conv_out_2, ssd_conv_w_2, ssd_conv_b_2, ssd_dt_bias_2,
        ssd_A_log_2, ssd_D_2, ssd_norm_g_2, w_ssd_out_2, attn_q_norm_2, attn_k_norm_2,
        attn_sinks_2, w_attn_out_2, w_mix_out_2, norm_xattn_2, norm_mem_2, w_xq_2, w_xkv_2,
        xattn_q_norm_2, xattn_k_norm_2, w_xo_2, norm_mlp_2, w_mlp_up_2, w_mlp_down_2,
    )


_drawn_inputs = setup_inputs


def setup_inputs(seed=0):
    import zlib

    import numpy as np

    out = dict(_drawn_inputs(seed))
    spreads = {}
    factors = {'norm_g': 5.744,
     'dn_o_gain': 8.0,
     'swa_q_gain': 8.0,
     'swa_k_gain': 8.0,
     'swa_sink': 8.0,
     'rel_table_2': 28.777,
     'norm_mix_2': 4.604,
     'gate_bias_2': 31.88,
     'conv_dw_b_2': 31.827,
     'conv_ln_g_2': 39.525,
     'conv_ln_b_2': 184.73,
     'ssd_conv_b_2': 32.759,
     'ssd_D_2': 200.0,
     'ssd_norm_g_2': 30.564,
     'attn_q_norm_2': 8.0,
     'attn_k_norm_2': 8.0,
     'attn_sinks_2': 200.0,
     'norm_xattn_2': 8.0,
     'norm_mem_2': 8.0,
     'xattn_q_norm_2': 8.0,
     'xattn_k_norm_2': 8.0,
     'norm_mlp_2': 14.176}
    for name, (base, spread) in spreads.items():
        noise = np.random.default_rng([zlib.crc32(name.encode()), seed]).standard_normal(out[name].shape)
        drawn = base * np.exp(spread * noise) if base else spread * noise
        out[name] = __import__('jax').numpy.asarray(drawn.astype(out[name].dtype))
    for name, factor in factors.items():
        out[name] = (out[name] * factor).astype(out[name].dtype)
    return out
```

```python
from contextlib import ExitStack, contextmanager
from itertools import count

import concourse.bass as bass
from concourse import mybir

F32 = mybir.dt.float32
ACT = mybir.ActivationFunctionType
ALU = mybir.AluOpType
AX_X = mybir.AxisListType.X

P = 128
D = 1024
KT = D // P
CTX, LAT = 256, 256
TOK = CTX + LAT
FFN = 2816
FT = FFN // P
EPS = 1e-6
BANK = 512
SEED = 2000


class Progress:

    def __init__(self, sem, steps, stage):
        self.sem, self.steps, self.stage = sem, steps, stage
        self.count, self.open = SEED, None

    def mark(self, name):
        self.count += 1
        key = (self.stage[0], name)
        assert self.steps.get(key, (self.count, 0))[0] == self.count, f"two steps are called {key}"
        self.steps.setdefault(key, (self.count, 0))
        if self.open is not None:
            self.open.append(key)
        return self.sem, 1

    def after(self, name, i=None, stage=None):
        key = (stage or self.stage[0], name)
        if key not in self.steps:
            assert not self.stage[1], f"nothing makes {key}"
            return self.sem, 1
        first, per_turn = self.steps[key]
        return self.sem, first if i is None or not per_turn else (first - per_turn) + (i + 1) * per_turn

    @contextmanager
    def turns(self, engine, times):
        start, self.open = self.count, []
        if times == 1:
            yield 0
        else:
            with engine.Fori(0, times) as i:
                yield i
        per_turn = self.count - start
        for key in self.open:
            self.steps[key] = (self.steps[key][0], per_turn)
        self.open, self.count = None, start + per_turn * times


def row(t, i):
    return t[:, bass.ds(i, 1), :].rearrange("p a n -> p (a n)")


class Kit:

    def __init__(self, nc, ctx, dram, steps, counted):
        self.nc, self.ctx, self.dram = nc, ctx, dram
        self.stage = ["start", counted]
        sem = lambda name: ctx.enter_context(nc.semaphore(name))
        self.PE, self.AC, self.DV, self.PO = (
            Progress(sem(name), steps.setdefault(name, {}), self.stage)
            for name in ("pe_done", "act_done", "dve_done", "pool_done"))
        self.landed = [sem("weights_landed_0"), sem("weights_landed_1")]
        self.landings = [0, 0]
        self.consts_landed = sem("consts_landed")
        self.stored = sem("stored")
        self.stores = 0
        f = lambda name, *shape: ctx.enter_context(nc.sbuf_tensor(name, [P, *shape], F32))
        self.W = f("weight_slots", 2, 4096)
        self.X = f("residual", KT, TOK)
        self.H = f("normed", KT, TOK)
        self.R = f("norm_r", 2, BANK)
        self.EPSC = f("eps", 1)
        self.banks = [ctx.enter_context(nc.psum_tensor(f"bank{b}", [P, BANK], F32)) for b in range(8)]
        self.ACC, self.AUX = self.banks[:4], self.banks[4:]
        self.upcoming = {}
        self.C = {}
        for name, a in dram.items():
            if name.startswith("c_"):
                self.C[name[2:]] = ctx.enter_context(nc.sbuf_tensor("k" + name, list(a.shape), F32))

    def open(self, name):
        self.stage[0] = name
        return self.nc.Block()



def load_unit(k, sp, weights, u, slot):
    n = weights.shape[2]
    sp.dma_start(k.W[:, slot, 0:n], weights[bass.ds(u, 1)].rearrange("a p n -> (a p) n")).then_inc(k.landed[slot], 16)


def stream(k, sp, weights, group, ahead, body=2):
    units = weights.shape[0]
    turns = units // body
    done = lambda s, i: k.PE.after(("acc", s * group + group - 1), i)
    for u in range(2, body):
        sp.wait_ge(*done(u - 2, 0))
        load_unit(k, sp, weights, u, u % 2)
    if turns == 2:
        for s in range(body):
            sp.wait_ge(*(done(body - 2 + s, 0) if s < 2 else done(s - 2, 1)))
            load_unit(k, sp, weights, body + s, s % 2)
    elif turns > 2:
        with sp.Fori(1, turns) as i:
            for s in range(body):
                sp.wait_ge(*(done(body - 2 + s, i - 1) if s < 2 else done(s - 2, i)))
                load_unit(k, sp, weights, i * body + s, s % 2)
    if ahead is not None:
        for s in range(2):
            sp.wait_ge(*done(body - 2 + s, turns - 1))
            load_unit(k, sp, ahead, s, s)


def weights_here(k, pe, s, i, body):
    pe.wait_ge(k.landed[s % 2], k.landings[s % 2] + 16 * (s // 2 + 1) + i * (16 * (body // 2)))


def close_stream(k, units):
    for s in range(2):
        k.landings[s] += 16 * (units // 2)


def linear(k, pe, weights, group, depth, rhs, tokens, evictor, body=2):
    n_tiles = body * group
    assert n_tiles % 4 == 0
    with k.PE.turns(pe, weights.shape[0] // body) as i:
        for s in range(body):
            weights_here(k, pe, s, i, body)
            for m in range(group):
                n = s * group + m
                e = evictor((n - 4) % n_tiles)
                pe.wait_ge(*(e.after(("ev", n - 4), i) if n >= 4 else e.after(("ev", n_tiles - 4 + n), i - 1)))
                for d in range(depth):
                    at = (m * depth + d) * P
                    mm = k.nc.tensor.matmul(k.ACC[n % 4][:, 0:tokens], k.W[:, s % 2, at:at + P], rhs(d),
                                            start=d == 0, stop=d == depth - 1)
                mm.then_inc(*k.PE.mark(("acc", n)))



def norm(k, name, src, dst, tokens, parts, squares):
    nc = k.nc
    with k.open(name) as block:
        @block.scalar
        def _(act):
            for d in range(KT):
                nc.scalar.activation(squares[:, d, 0:tokens], src(d), ACT.Square).then_inc(*k.AC.mark(("sq", d)))
            act.wait_ge(*k.PE.after("sum"))
            nc.scalar.activation(k.R[:, 0, 0:tokens], k.AUX[0][:, 0:tokens], ACT.Sqrt, scale=1.0 / D,
                                 bias=k.EPSC[:]).then_inc(*k.AC.mark("rms"))
            for d in range(KT):
                act.wait_ge(*k.DV.after(("x", d)))
                for n, (a, b, scale, shift) in enumerate(parts):
                    nc.scalar.activation(dst(d)[:, a:b], dst(d)[:, a:b], ACT.Identity, scale=scale(d),
                                         bias=shift(d) if shift else 0.0).then_inc(*k.AC.mark(("out", d, n)))

        @block.tensor
        def _(pe):
            for d in range(KT):
                pe.wait_ge(*k.AC.after(("sq", d)))
                mm = nc.tensor.matmul(k.AUX[0][:, 0:tokens], k.C["ones"][:], squares[:, d, 0:tokens],
                                      start=d == 0, stop=d == KT - 1)
            mm.then_inc(*k.PE.mark("sum"))

        @block.vector
        def _(dve):
            dve.wait_ge(*k.AC.after("rms"))
            nc.vector.reciprocal(k.R[:, 1, 0:tokens], k.R[:, 0, 0:tokens]).then_inc(*k.DV.mark("r"))
            dve.wait_ge(*k.DV.after("r"))
            for d in range(KT):
                nc.vector.tensor_tensor(dst(d), src(d), k.R[:, 1, 0:tokens], ALU.mult).then_inc(*k.DV.mark(("x", d)))



def start(k, ahead):
    nc = k.nc
    with k.open("start") as block:
        @block.sync
        def _(sp):
            n = 0
            for name, t in k.C.items():
                sp.dma_start(t[:], k.dram["c_" + name]).then_inc(k.consts_landed, 16)
                n += 16
            sp.dma_start(k.X[:], k.dram["tokens"]).then_inc(k.consts_landed, 16)
            for s in range(2):
                load_unit(k, sp, ahead, s, s)
            sp.wait_ge(k.consts_landed, n + 16)

        @block.tensor
        def _(pe):
            nc.tensor.nop().then_inc(k.PE.sem, SEED)

        @block.scalar
        def _(act):
            nc.scalar.nop().then_inc(k.AC.sem, SEED)

        @block.vector
        def _(dve):
            nc.vector.memset(k.EPSC[:], EPS).then_inc(k.DV.sem, SEED)

        @block.gpsimd
        def _(pool):
            nc.gpsimd.nop().then_inc(k.PO.sem, SEED)


def modulation(k, mod, gate, scale, ahead):
    nc, w = k.nc, k.dram["w_ada"]
    units, body, width = w.shape[0], 4, w.shape[2] // KT
    tiles = width // P
    cond = k.C["cond"]
    with k.open("modulation") as block:
        @block.sync
        def _(sp):
            stream(k, sp, w, 1, ahead, body)

        @block.scalar
        def _(act):
            nc.scalar.activation(cond[:], cond[:], ACT.Silu).then_inc(*k.AC.mark("silu"))
            with k.AC.turns(act, units // body) as i:
                for s in range(body):
                    act.wait_ge(*k.PE.after(("acc", s), i))
                    nc.scalar.activation(k.H[0:2, s, 0:width], k.ACC[s][0:2, 0:width], ACT.Copy).then_inc(*k.AC.mark(("ev", s)))

        @block.tensor
        def _(pe):
            pe.wait_ge(*k.AC.after("silu"))

            def turned(s, i):
                pe.wait_ge(*k.AC.after(("ev", s), i))
                pe.wait_ge(*k.DV.after(("mod", s), i - 1))
                for m in range(tiles):
                    mm = nc.tensor.matmul(k.AUX[s][:, 2 * m:2 * m + 2], k.H[0:2, s, m * P:(m + 1) * P],
                                          k.C["ident"][0:2, 0:2], start=True, stop=True)
                mm.then_inc(*k.PE.mark(("turned", s)))

            with k.PE.turns(pe, units // body) as i:
                for s in range(body):
                    weights_here(k, pe, s, i, body)
                    pe.wait_ge(*k.AC.after(("ev", s), i - 1))
                    for d in range(KT):
                        mm = nc.tensor.matmul(k.ACC[s][0:2, 0:width], cond[:, d, :],
                                              k.W[:, s % 2, d * width:(d + 1) * width], start=d == 0, stop=d == KT - 1)
                    mm.then_inc(*k.PE.mark(("acc", s)))
                    if s:
                        turned(s - 1, i)
                turned(body - 1, i)

        @block.vector
        def _(dve):
            with k.DV.turns(dve, units // body) as i:
                for s in range(body):
                    dve.wait_ge(*k.PE.after(("turned", s), i))
                    at = bass.ds((i * body + s) * (2 * tiles), 2 * tiles)
                    nc.vector.tensor_tensor(mod[:, at], k.AUX[s][:, 0:2 * tiles], k.C["ada_b"][:, at],
                                            ALU.add).then_inc(*k.DV.mark(("mod", s)))
            dve.wait_ge(*k.DV.after(("mod", body - 1), units // body - 1))
            m = mod[:].rearrange("p (l i j f) -> p l i j f", l=2, i=3, j=3)
            for l in range(2):
                for n in range(3):
                    nc.vector.scalar_tensor_tensor(scale[:, l, n, :], m[:, l, n, 1, :], 1.0, k.C["norm_g"][:, l, n, :],
                                                   ALU.add, ALU.mult).then_inc(*k.DV.mark(("scale", l, n)))
                    nc.vector.tensor_scalar(gate[:, l, n, :], m[:, l, n, 2, :], 1.0 if n == 1 else 0.5, None,
                                            ALU.mult).then_inc(*k.DV.mark(("gate", l, n)))
    close_stream(k, units)


def gated_residual(k, dve, n, at, first, gate):
    for c, (a, b) in enumerate(((0, CTX), (CTX, TOK))):
        if b <= first:
            continue
        x = row(k.X, at)[:, a:b]
        ins = k.nc.vector.scalar_tensor_tensor(x, k.ACC[n % 4][:, a - first:b - first], gate(at, c), x, ALU.mult, ALU.add)
        ins.then_inc(*k.DV.mark(("ev", n) if c == 1 else ("ev ctx", n)))


def gated_mlp(k, name, w1, w2, first, gate, hidden, silus, ahead):
    nc, tokens = k.nc, TOK - first
    with k.open(name + " up") as block:
        @block.sync
        def _(sp):
            stream(k, sp, w1, 2, w2)

        @block.tensor
        def _(pe):
            linear(k, pe, w1, 2, KT, lambda d: k.H[:, d, first:TOK], tokens, lambda n: k.DV if n % 2 else k.AC)

        @block.scalar
        def _(act):
            with k.AC.turns(act, FT // 2) as i:
                for s in range(2):
                    act.wait_ge(*k.PE.after(("acc", 2 * s), i))
                    act.wait_ge(*k.DV.after(("ev", 2 * s + 1), i - 1))
                    nc.scalar.activation(silus[:, s, 0:tokens], k.ACC[2 * s][:, 0:tokens],
                                         ACT.Silu).then_inc(*k.AC.mark(("ev", 2 * s)))

        @block.vector
        def _(dve):
            with k.DV.turns(dve, FT // 2) as i:
                for s in range(2):
                    dve.wait_ge(*k.PE.after(("acc", 2 * s + 1), i))
                    dve.wait_ge(*k.AC.after(("ev", 2 * s), i))
                    nc.vector.tensor_tensor(row(hidden, i * 2 + s)[:, 0:tokens], silus[:, s, 0:tokens],
                                            k.ACC[2 * s + 1][:, 0:tokens], ALU.mult).then_inc(*k.DV.mark(("ev", 2 * s + 1)))
    close_stream(k, w1.shape[0])
    with k.open(name + " down") as block:
        @block.sync
        def _(sp):
            stream(k, sp, w2, 1, ahead, body=4)

        @block.tensor
        def _(pe):
            linear(k, pe, w2, 1, FT, lambda d: hidden[:, d, 0:tokens], tokens, lambda n: k.DV, body=4)

        @block.vector
        def _(dve):
            with k.DV.turns(dve, KT // 4) as i:
                for n in range(4):
                    dve.wait_ge(*k.PE.after(("acc", n), i))
                    gated_residual(k, dve, n, i * 4 + n, first, gate)
    close_stream(k, w2.shape[0])



DN_HEADS = D // P
CHUNKS = TOK // P
LEVELS = 7
ORDER = ((0, 1, 2, 3), (1, 0, 3, 2))


def conv_silu(k, name, w, src, seqs, length, taps, mid, bias, out, convs, ahead):
    nc = k.nc
    width, tokens, turns = taps.shape[2], seqs * length, w.shape[0] // 2
    with k.open(name) as block:
        @block.sync
        def _(sp):
            stream(k, sp, w, 4, ahead)

        @block.tensor
        def _(pe):
            linear(k, pe, w, 4, KT, src, tokens, lambda n: k.DV)

        @block.vector
        def _(dve):
            with k.DV.turns(dve, turns) as i:
                for n in range(8):
                    x = k.ACC[n % 4][:, 0:tokens].rearrange("p (s t) -> p s t", s=seqs)
                    y = convs[:, n % 4, 0:tokens].rearrange("p (s t) -> p s t", s=seqs)
                    tap = lambda j: taps[:, bass.ds(i * 8 + n, 1), j:j + 1].rearrange("p a b -> p (a b)")
                    dve.wait_ge(*k.PE.after(("acc", n), i))
                    dve.wait_ge(*(k.AC.after(("silu", n - 4), i) if n >= 4 else k.AC.after(("silu", n + 4), i - 1)))
                    nc.vector.tensor_scalar(y, x, tap(mid), None, ALU.mult).then_inc(*k.DV.mark(("tap", n, mid)))
                    last = ("tap", n, mid)
                    others = [j for j in range(width) if j != mid]
                    for j in others:
                        shift = j - mid
                        a, b = max(0, -shift), length - max(0, shift)
                        dve.wait_ge(*k.DV.after(last, i))
                        last = ("ev", n) if j == others[-1] else ("tap", n, j)
                        nc.vector.scalar_tensor_tensor(y[:, :, a:b], x[:, :, a + shift:b + shift], tap(j),
                                                       y[:, :, a:b], ALU.mult, ALU.add).then_inc(*k.DV.mark(last))

        @block.scalar
        def _(act):
            with k.AC.turns(act, turns) as i:
                for n in range(8):
                    act.wait_ge(*k.DV.after(("ev", n), i))
                    nc.scalar.activation(row(out, i * 8 + n), convs[:, n % 4, 0:tokens], ACT.Silu,
                                         bias=bias[:, bass.ds(i * 8 + n, 1)] if bias is not None else 0.0
                                         ).then_inc(*k.AC.mark(("silu", n)))
    close_stream(k, w.shape[0])


def delta_gates(k, z, g, beta, gc, eg_neg, ekd, ea, tmp, ahead):
    nc, w = k.nc, k.dram["w_dn_z"]
    ab = k.AUX[0][:, 0:CHUNKS * 32].rearrange("p (x w h) -> p x w h", w=2, h=8)
    per_dir = lambda t, d: t[:].rearrange("p (c d) h -> p c d h", d=2)[:, :, d, :]
    sums, totals = k.AUX[1][:, 0:64], k.AUX[1][:, 64:128]
    flat = lambda t: t[:].rearrange("p a b -> p (a b)")
    with k.open("delta gates") as block:
        @block.sync
        def _(sp):
            stream(k, sp, w, 4, ahead)

        @block.tensor
        def _(pe):
            for c in range(CHUNKS):
                for d in range(KT):
                    mm = nc.tensor.matmul(k.AUX[0][:, c * 32:c * 32 + 32], k.H[:, d, c * P:(c + 1) * P],
                                          k.C["w_dn_ab"][:, d, :], start=d == 0, stop=d == KT - 1)
            mm.then_inc(*k.PE.mark("ab"))
            linear(k, pe, w, 4, KT, lambda d: k.H[:, d, :], TOK, lambda n: k.AC)
            pe.wait_ge(*k.DV.after("g"))
            for d in range(2):
                nc.tensor.matmul(sums[:, d * 32:d * 32 + 32], k.C["until"][:, d, :], per_dir(g, d), start=True, stop=True)
                mm = nc.tensor.matmul(totals[:, d * 32:d * 32 + 32], k.C["ones"][:], per_dir(g, d), start=True, stop=True)
            mm.then_inc(*k.PE.mark("sums"))

        @block.vector
        def _(dve):
            dve.wait_ge(*k.PE.after("ab"))
            nc.vector.tensor_tensor(tmp[:, 0], ab[:, :, 0, :], k.C["dn_dt_bias"][:], ALU.add).then_inc(*k.DV.mark("x"))
            dve.wait_ge(*k.DV.after("x"))
            nc.vector.scalar_tensor_tensor(tmp[:, 1], tmp[:, 0], -1.0, tmp[:, 0], ALU.mult, ALU.max).then_inc(*k.DV.mark("|x|"))
            dve.wait_ge(*k.AC.after("ln"))
            nc.vector.scalar_tensor_tensor(tmp[:, 3], tmp[:, 0], 0.0, tmp[:, 2], ALU.max, ALU.add).then_inc(*k.DV.mark("softplus"))
            dve.wait_ge(*k.DV.after("softplus"))
            nc.vector.scalar_tensor_tensor(g[:], tmp[:, 3], -1.0, k.C["dn_a_log"][:], ALU.mult, ALU.mult).then_inc(*k.DV.mark("g"))
            dve.wait_ge(*k.PE.after("sums"))
            nc.vector.tensor_copy(flat(gc), sums).then_inc(*k.DV.mark("gc"))
            dve.wait_ge(*k.DV.after("gc"))
            nc.vector.tensor_tensor(flat(ekd), totals, flat(gc), ALU.subtract).then_inc(*k.DV.mark("to end"))
            dve.wait_ge(*k.AC.after("eg"))
            nc.vector.tensor_scalar(flat(eg_neg), flat(eg_neg), -1.0, None, ALU.mult).then_inc(*k.DV.mark("-eg"))

        @block.scalar
        def _(act):
            act.wait_ge(*k.DV.after("|x|"))
            nc.scalar.activation(k.C["dn_a_log"][:], k.C["dn_a_log"][:], ACT.Exp).then_inc(*k.AC.mark("a"))
            nc.scalar.activation(tmp[:, 2], tmp[:, 1], ACT.Exp, scale=-1.0).then_inc(*k.AC.mark("exp"))
            act.wait_ge(*k.AC.after("exp"))
            nc.scalar.activation(tmp[:, 2], tmp[:, 2], ACT.Ln, bias=1.0).then_inc(*k.AC.mark("ln"))
            nc.scalar.activation(beta[:], ab[:, :, 1, :], ACT.Sigmoid).then_inc(*k.AC.mark("beta"))
            with k.AC.turns(act, 1):
                for n in range(8):
                    act.wait_ge(*k.PE.after(("acc", n)))
                    nc.scalar.activation(z[:, n, :], k.ACC[n % 4][:], ACT.Silu).then_inc(*k.AC.mark(("ev", n)))
            act.wait_ge(*k.DV.after("to end"))
            nc.scalar.activation(flat(eg_neg), sums, ACT.Exp).then_inc(*k.AC.mark("eg"))
            nc.scalar.activation(flat(ea), totals, ACT.Exp).then_inc(*k.AC.mark("ea"))
            nc.scalar.activation(flat(ekd), flat(ekd), ACT.Exp).then_inc(*k.AC.mark("ekd"))
    close_stream(k, w.shape[0])


def delta_heads(k, new, qkv, z, g, beta, gc, eg_neg, ekd, ea):
    nc, B = k.nc, k.banks
    head, kh, qh, vh = new("dn_squares", 2, TOK), new("dn_k", TOK), new("dn_q", TOK), new("dn_v", TOK)
    ktok, vtok = new("dn_ktok", CHUNKS, P), new("dn_vtok", CHUNKS, P)
    pair = lambda name, *shape: [new(f"dn_{name}{d}", *(shape or (CHUNKS, P))) for d in range(2)]
    gu, dec, egb, kd, Y = (pair(n) for n in "gu dec egb kd y".split())
    at, qkt, qg, kbg = ([k.H[:, 2 * n + d, :].rearrange("p (c t) -> p c t", c=CHUNKS) for d in range(2)]
                        for n in range(4))
    ps, wt, X = gu, dec, egb
    lm = [pair(f"lm{s}_") for s in range(2)]
    vnew, S = pair("vnew", P), pair("state", P)
    oh = new("dn_o", TOK)
    r = k.R
    C = k.C
    ck = lambda t, c: t[:, c * P:(c + 1) * P]
    tc = lambda t, c, d, i: t[:, c * 2 + d, bass.ds(i, 1)]
    td = lambda t, c, d, i: t[:, d * 4 + c, bass.ds(i, 1)]
    w4 = lambda t: t[:, :, :].rearrange("p c n -> p (c n)")
    wide = lambda m: m.unsqueeze(1).to_broadcast([P, CHUNKS, P])

    with k.open("delta heads") as block:
        @block.scalar
        def _(act):
            with k.AC.turns(act, DN_HEADS) as i:
                act.wait_ge(*k.PE.after("sum_o", i - 1))
                nc.scalar.activation(head[:, 0, :], row(qkv, i), ACT.Square).then_inc(*k.AC.mark("sq_q"))
                nc.scalar.activation(head[:, 1, :], row(qkv, i + 8), ACT.Square).then_inc(*k.AC.mark("sq_k"))
                nc.scalar.activation(vh[:], row(qkv, i + 16), ACT.Copy).then_inc(*k.AC.mark("vh"))
                act.wait_ge(*k.PE.after("sum_q", i))
                act.wait_ge(*k.DV.after("out", i - 1))
                nc.scalar.activation(r[:, 0, :], B[0][:], ACT.Sqrt, bias=k.EPSC[:]).then_inc(*k.AC.mark("norm_q"))
                act.wait_ge(*k.PE.after("sum_k", i))
                nc.scalar.activation(r[:, 1, :], B[1][:], ACT.Sqrt, bias=k.EPSC[:]).then_inc(*k.AC.mark("norm_k"))
                act.wait_ge(*k.PE.after("vT", i))
                nc.scalar.activation(w4(vtok), B[3][:], ACT.Copy).then_inc(*k.AC.mark("vtok"))
                act.wait_ge(*k.PE.after("kT", i))
                nc.scalar.activation(w4(ktok), B[2][:], ACT.Copy).then_inc(*k.AC.mark("ktok"))
                for d in range(2):
                    act.wait_ge(*k.PE.after(("gcb", d), i))
                    nc.scalar.activation(w4(egb[d]), B[6 + d][:], ACT.Exp).then_inc(*k.AC.mark(("egb", d)))
                    act.wait_ge(*k.DV.after(("dd", d, 3), i))
                    nc.scalar.activation(w4(dec[d]), w4(dec[d]), ACT.Exp).then_inc(*k.AC.mark(("dec", d)))
                for s in range(LEVELS):
                    for d in range(2 if s else 0):
                        act.wait_ge(*k.PE.after(("p", s, d), i))
                        nc.scalar.activation(w4(ps[d]), B[d][:], ACT.Copy).then_inc(*k.AC.mark(("ps", s, d)))
                    for d in range(2 if s < LEVELS - 1 else 0):
                        if s == 0:
                            act.wait_ge(*k.DV.after(("qg", d), i))
                        act.wait_ge(*k.PE.after(("yT", s, d), i))
                        nc.scalar.activation(w4(X[d]), B[2 + d][:], ACT.Copy).then_inc(*k.AC.mark(("x", s, d)))
                for d in range(2):
                    act.wait_ge(*k.PE.after(("wT", d), i))
                    nc.scalar.activation(w4(wt[d]), B[d][:], ACT.Copy).then_inc(*k.AC.mark(("wt", d)))
                act.wait_ge(*k.DV.after(("o", 3, 1), i))
                nc.scalar.activation(head[:, 0, :], oh[:], ACT.Square).then_inc(*k.AC.mark("sq_o"))
                act.wait_ge(*k.PE.after("sum_o", i))
                nc.scalar.activation(r[:, 0, :], B[0][:], ACT.Sqrt, scale=1.0 / P, bias=k.EPSC[:]).then_inc(*k.AC.mark("norm_o"))

        @block.tensor
        def _(pe):
            def four(bank, lhs, rhs, name):
                for c in range(CHUNKS):
                    mm = nc.tensor.matmul(ck(bank, c), lhs[:, c, :], rhs[:, c, :], start=True, stop=True)
                mm.then_inc(*k.PE.mark(name))

            with k.PE.turns(pe, DN_HEADS) as i:
                pe.wait_ge(*k.AC.after("sq_q", i))
                nc.tensor.matmul(B[0][:], C["ones"][:], head[:, 0, :], start=True, stop=True).then_inc(*k.PE.mark("sum_q"))
                pe.wait_ge(*k.AC.after("sq_k", i))
                nc.tensor.matmul(B[1][:], C["ones"][:], head[:, 1, :], start=True, stop=True).then_inc(*k.PE.mark("sum_k"))
                pe.wait_ge(*k.AC.after("vh", i))
                for c in range(CHUNKS):
                    mm = nc.tensor.transpose(ck(B[3], c), ck(vh, c), C["ident"][:])
                mm.then_inc(*k.PE.mark("vT"))
                for d in range(2):
                    pe.wait_ge(*k.DV.after(("gu", d, 3), i))
                    nc.tensor.matmul(B[6 + d][:], C["ones"][:], w4(gu[d]), start=True, stop=True).then_inc(*k.PE.mark(("gcb", d)))
                pe.wait_ge(*k.DV.after("kh", i))
                for c in range(CHUNKS):
                    mm = nc.tensor.transpose(ck(B[2], c), ck(kh, c), C["ident"][:])
                mm.then_inc(*k.PE.mark("kT"))
                for c in range(CHUNKS):
                    mm = nc.tensor.matmul(ck(B[4], c), ck(kh, c), ck(kh, c), start=True, stop=True)
                mm.then_inc(*k.PE.mark("kk"))
                for c in range(CHUNKS):
                    mm = nc.tensor.matmul(ck(B[5], c), ck(kh, c), ck(qh, c), start=True, stop=True)
                mm.then_inc(*k.PE.mark("kq"))
                for s in range(LEVELS):
                    for d in range(2 if s else 0):
                        pe.wait_ge(*k.PO.after(("lm", s, d), i))
                        pe.wait_ge(*k.AC.after(("x", s - 1, d), i))
                        four(B[d], lm[s % 2][d], X[d], ("p", s, d))
                    for d in range(2 if s else 0):
                        pe.wait_ge(*k.AC.after(("ps", s, d), i))
                        four(B[4 + d], ps[d], Y[d], ("dy", s, d))
                    for d in range(2 if s < LEVELS - 1 else 0):
                        if s:
                            pe.wait_ge(*k.DV.after(("y", s, d), i))
                        else:
                            pe.wait_ge(*k.PO.after(("y", d), i))
                            pe.wait_ge(*k.DV.after(("kd", 1, 3), i))
                        for c in range(CHUNKS):
                            mm = nc.tensor.transpose(ck(B[2 + d], c), Y[d][:, c, :], C["ident"][:])
                        mm.then_inc(*k.PE.mark(("yT", s, d)))
                for d in range(2):
                    pe.wait_ge(*k.DV.after(("y", LEVELS - 1, d), i))
                    four(B[d], kbg[d], Y[d], ("wT", d))
                for t in range(CHUNKS):
                    for d in range(2):
                        c = ORDER[d][t]
                        mm = nc.tensor.matmul(B[2 + d][:, 0:P], Y[d][:, c, :], vtok[:, c, :], start=True, stop=t == 0)
                        if t:
                            pe.wait_ge(*k.AC.after(("wt", d), i))
                            pe.wait_ge(*k.DV.after(("state", t - 1, d), i))
                            mm = nc.tensor.matmul(B[2 + d][:, 0:P], wt[d][:, c, :], S[d][:], start=False, stop=True)
                        mm.then_inc(*k.PE.mark(("vn", t, d)))
                    for d in range(2):
                        c = ORDER[d][t]
                        if t:
                            pe.wait_ge(*k.DV.after(("o", t - 1, d), i))
                            nc.tensor.matmul(B[4 + d][:, 0:P], S[d][:], qg[d][:, c, :], start=True, stop=False)
                        pe.wait_ge(*k.DV.after(("vnew", t, d), i))
                        nc.tensor.matmul(B[4 + d][:, 0:P], vnew[d][:], qkt[d][:, c, :], start=t == 0,
                                         stop=True).then_inc(*k.PE.mark(("o", t, d)))
                        if t < CHUNKS - 1:
                            nc.tensor.matmul(B[6 + d][:, 0:P], kd[d][:, c, :], vnew[d][:], start=True,
                                             stop=True).then_inc(*k.PE.mark(("ds", t, d)))
                pe.wait_ge(*k.AC.after("sq_o", i))
                nc.tensor.matmul(B[0][:], C["ones"][:], head[:, 0, :], start=True, stop=True).then_inc(*k.PE.mark("sum_o"))

        @block.gpsimd
        def _(pool):
            with k.PO.turns(pool, DN_HEADS) as i:
                for s in range(LEVELS):
                    for d in range(2):
                        pool.wait_ge(*k.DV.after(("at", d, 3), i))
                        if s >= 3:
                            pool.wait_ge(*k.PE.after(("p", s - 2, d), i))
                        if s == 2:
                            pool.wait_ge(*k.PO.after(("y", d), i))
                        nc.gpsimd.tensor_tensor(lm[s % 2][d][:], at[d], wide(C["level"][:, d * LEVELS + s, :]),
                                                ALU.mult).then_inc(*k.PO.mark(("lm", s, d)))
                    if s == 0:
                        for d in range(2):
                            pool.wait_ge(*k.PE.after(("vn", 3, d), i - 1))
                            pool.wait_ge(*k.PO.after(("lm", 0, d), i))
                            nc.gpsimd.tensor_tensor(Y[d][:], wide(C["ident"][:]), lm[0][d][:],
                                                    ALU.subtract).then_inc(*k.PO.mark(("y", d)))

        @block.vector
        def _(dve):
            with k.DV.turns(dve, DN_HEADS) as i:
                for d in range(2):
                    for c in range(CHUNKS):
                        nc.vector.tensor_scalar(gu[d][:, c, :], C["until"][:, d, :], tc(g, c, d, i), None,
                                                ALU.mult).then_inc(*k.DV.mark(("gu", d, c)))
                dve.wait_ge(*k.AC.after("norm_q", i))
                nc.vector.reciprocal(r[:, 0, :], r[:, 0, :]).then_inc(*k.DV.mark("r_q"))
                dve.wait_ge(*k.AC.after("norm_k", i))
                nc.vector.reciprocal(r[:, 1, :], r[:, 1, :]).then_inc(*k.DV.mark("r_k"))
                dve.wait_ge(*k.DV.after("r_q", i))
                nc.vector.scalar_tensor_tensor(qh[:], row(qkv, i), P ** -0.5, r[:, 0, :], ALU.mult,
                                               ALU.mult).then_inc(*k.DV.mark("qh"))
                dve.wait_ge(*k.DV.after("r_k", i))
                nc.vector.tensor_tensor(kh[:], row(qkv, i + 8), r[:, 1, :], ALU.mult).then_inc(*k.DV.mark("kh"))
                for d in range(2):
                    dve.wait_ge(*k.AC.after(("egb", d), i))
                    for c in range(CHUNKS):
                        nc.vector.scalar_tensor_tensor(dec[d][:, c, :], ck(B[6 + d], c), td(gc, c, d, i),
                                                       C["behind"][:, d, :], ALU.subtract,
                                                       ALU.add).then_inc(*k.DV.mark(("dd", d, c)))
                for d in range(2):
                    dve.wait_ge(*k.AC.after(("dec", d), i))
                    dve.wait_ge(*k.PE.after("kk", i))
                    for c in range(CHUNKS):
                        nc.vector.scalar_tensor_tensor(at[d][:, c, :], ck(B[4], c), tc(beta, c, d, i), dec[d][:, c, :],
                                                       ALU.mult, ALU.mult).then_inc(*k.DV.mark(("at", d, c)))
                for d in range(2):
                    dve.wait_ge(*k.PE.after("kq", i))
                    nc.vector.tensor_tensor(w4(qkt[d]), B[5][:], w4(dec[d]), ALU.mult).then_inc(*k.DV.mark(("qkt", d)))
                    dve.wait_ge(*k.AC.after(("egb", d), i))
                    nc.vector.tensor_tensor(w4(qg[d]), qh[:], w4(egb[d]), ALU.mult).then_inc(*k.DV.mark(("qg", d)))
                    dve.wait_ge(*k.AC.after("ktok", i))
                    for c in range(CHUNKS):
                        nc.vector.tensor_scalar(kbg[d][:, c, :], ktok[:, c, :], td(eg_neg, c, d, i), None,
                                                ALU.mult).then_inc(*k.DV.mark(("kbg", d, c)))
                        nc.vector.tensor_scalar(kd[d][:, c, :], ktok[:, c, :], td(ekd, c, d, i), None,
                                                ALU.mult).then_inc(*k.DV.mark(("kd", d, c)))
                for s in range(1, LEVELS):
                    for d in range(2):
                        dve.wait_ge(*k.PE.after(("dy", s, d), i))
                        nc.vector.tensor_tensor(w4(Y[d]), w4(Y[d]), B[4 + d][:], ALU.subtract).then_inc(*k.DV.mark(("y", s, d)))
                seen = set()
                for t in range(CHUNKS):
                    for d in range(2):
                        dve.wait_ge(*k.PE.after(("vn", t, d), i))
                        nc.vector.tensor_scalar(vnew[d][:], B[2 + d][:, 0:P], tc(beta, ORDER[d][t], d, i), None,
                                                ALU.mult).then_inc(*k.DV.mark(("vnew", t, d)))
                    for d in range(2):
                        c = ORDER[d][t]
                        dve.wait_ge(*k.PE.after(("o", t, d), i))
                        if c in seen:
                            dve.wait_ge(*k.DV.after(("o", ORDER[1 - d].index(c), 1 - d), i))
                            ins = nc.vector.tensor_tensor(ck(oh, c), ck(oh, c), B[4 + d][:, 0:P], ALU.add)
                        else:
                            ins = nc.vector.tensor_copy(ck(oh, c), B[4 + d][:, 0:P])
                            seen.add(c)
                        ins.then_inc(*k.DV.mark(("o", t, d)))
                        if t < CHUNKS - 1:
                            dve.wait_ge(*k.PE.after(("ds", t, d), i))
                            if t:
                                ins = nc.vector.scalar_tensor_tensor(S[d][:], S[d][:], td(ea, c, d, i), B[6 + d][:, 0:P],
                                                                     ALU.mult, ALU.add)
                            else:
                                ins = nc.vector.tensor_copy(S[d][:], B[6 + d][:, 0:P])
                            ins.then_inc(*k.DV.mark(("state", t, d)))
                dve.wait_ge(*k.AC.after("norm_o", i))
                nc.vector.reciprocal(r[:, 0, :], r[:, 0, :]).then_inc(*k.DV.mark("r_o"))
                dve.wait_ge(*k.DV.after("r_o", i))
                nc.vector.tensor_tensor(oh[:], oh[:], r[:, 0, :], ALU.mult).then_inc(*k.DV.mark("oh"))
                dve.wait_ge(*k.DV.after("oh", i))
                nc.vector.scalar_tensor_tensor(row(qkv, i), oh[:], C["dn_o_gain"][:], row(z, i), ALU.mult,
                                               ALU.mult).then_inc(*k.DV.mark("out"))


def to_residual(k, name, w, src, tokens, write, ahead):
    group = D // P // w.shape[0]
    depth = w.shape[2] // P // group
    body = max(2, 4 // group)
    with k.open(name) as block:
        @block.sync
        def _(sp):
            stream(k, sp, w, group, ahead, body)

        @block.tensor
        def _(pe):
            linear(k, pe, w, group, depth, src, tokens, lambda n: k.DV, body)

        @block.vector
        def _(dve):
            tiles = body * group
            with k.DV.turns(dve, KT // tiles) as i:
                for n in range(tiles):
                    dve.wait_ge(*k.PE.after(("acc", n), i))
                    write(dve, n, i * tiles + n, i)
    close_stream(k, w.shape[0])



HEAD = 64
Q_HEADS = [h for pair in range(2) for i in range(4) for h in (8 * pair + i, 8 * pair + 4 + i)]


def late_constants(k, new, names):
    with k.open("load " + names[0]) as block:
        @block.sync
        def _(sp):
            for name in names:
                a = k.dram["late_" + name]
                k.C[name] = new("k" + name, *a.shape[1:])
                sp.dma_start(k.C[name][0:a.shape[0]], a).then_inc(k.stored, 16)
            k.stores += 16 * len(names)
            sp.wait_ge(k.stored, k.stores)


def norm_heads(k, name, tiles, tokens, gain, ones, width, new, rope=False, softmax_scale=1.0, eps="eps"):
    nc = k.nc
    sq, r, t = new("nh_sq", sum(map(len, tiles)), tokens), new("nh_r", len(tiles), tokens), new("nh_t", 2, tokens)
    flat = [(g, n, tile) for g, group in enumerate(tiles) for n, tile in enumerate(group)]
    a, b = 1.0 / (width * softmax_scale ** 2), k.C[eps]
    with k.open(name) as block:
        @block.scalar
        def _(act):
            for m, (g, n, tile) in enumerate(flat):
                nc.scalar.activation(sq[:, m, :], tile, ACT.Square).then_inc(*k.AC.mark(("sq", m)))
            for g in range(len(tiles)):
                act.wait_ge(*k.PE.after(("sum", g)))
                nc.scalar.activation(r[:, g, :], k.ACC[g][:, 0:tokens], ACT.Sqrt, scale=a, bias=b[:, 0:1]).then_inc(*k.AC.mark(("rms", g)))

        @block.tensor
        def _(pe):
            for m, (g, n, tile) in enumerate(flat):
                pe.wait_ge(*k.AC.after(("sq", m)))
                mm = nc.tensor.matmul(k.ACC[g][:, 0:tokens], ones[:], sq[:, m, :], start=n == 0, stop=n == len(tiles[g]) - 1)
                if n == len(tiles[g]) - 1:
                    mm.then_inc(*k.PE.mark(("sum", g)))
            if rope:
                for m, (g, n, tile) in enumerate(flat):
                    pe.wait_ge(*k.DV.after(("n", m)))
                    nc.tensor.matmul(k.AUX[m][:, 0:tokens], k.C["rot"][:], tile, start=True, stop=True).then_inc(*k.PE.mark(("rot", m)))

        @block.vector
        def _(dve):
            for g in range(len(tiles)):
                dve.wait_ge(*k.AC.after(("rms", g)))
                nc.vector.reciprocal(r[:, g, :], r[:, g, :]).then_inc(*k.DV.mark(("r", g)))
            for m, (g, n, tile) in enumerate(flat):
                dve.wait_ge(*k.DV.after(("r", g)))
                nc.vector.scalar_tensor_tensor(tile, tile, gain(n), r[:, g, :], ALU.mult, ALU.mult).then_inc(*k.DV.mark(("n", m)))
            if rope:
                for m, (g, n, tile) in enumerate(flat):
                    dve.wait_ge(*k.PE.after(("rot", m)))
                    nc.vector.tensor_tensor(t[:, m, :], k.AUX[m][:, 0:tokens], k.C["sin"][:], ALU.mult).then_inc(*k.DV.mark(("s", m)))
                    nc.vector.tensor_tensor(tile, tile, k.C["cos"][:], ALU.mult).then_inc(*k.DV.mark(("c", m)))
                    dve.wait_ge(*k.DV.after(("c", m)))
                    nc.vector.tensor_tensor(tile, tile, t[:, m, :], ALU.add).then_inc(*k.DV.mark(("roped", m)))


def window_heads(k, name, pair, new, q, ks, v, o, gain, keys, mask, sink, rope):
    nc, C = k.nc, k.C
    sq, r, qn, qs, qr = (new("wh_" + n, LAT) for n in ("sq", "r", "qn", "qs", "qr"))
    sc, pt = new("wh_scores", 4, BANK), new("wh_pt", 2, BANK)
    cols = new("wh_cols", 8, 4)
    mx, nm, sums, es, tot, rt, sk = (cols[:, n, :] for n in range(7))
    bias = new("wh_bias", 2, 256) if mask is None else None
    combos = [(hh, b) for hh in range(2) for b in range(2)]
    n_keys = [keys[b][1] - keys[b][0] for hh, b in combos]
    half = lambda t, hh: t[hh * HEAD:(hh + 1) * HEAD]
    blk = lambda b: slice(b * P, (b + 1) * P)
    with k.open(name) as block:
        @block.scalar
        def _(act):
            def copy_p(x, i):
                act.wait_ge(*k.PE.after(("pT", x), i))
                if x >= 2:
                    act.wait_ge(*k.PE.after(("o", x - 2), i))
                nc.scalar.activation(pt[:, x % 2, 0:n_keys[x]], k.AUX[x % 2][:, 0:n_keys[x]], ACT.Copy).then_inc(*k.AC.mark(("pt", x)))

            with k.AC.turns(act, 4) as i:
                nc.scalar.activation(sq[:], row(q, pair * 4 + i), ACT.Square).then_inc(*k.AC.mark("sq"))
                if bias is not None:
                    act.wait_ge(*k.DV.after(("max", 3), i - 1))
                    b_in = sink[1][:, bass.ds((pair * 4 + i) * 2, 2), :]
                    nc.scalar.activation(bias[:], b_in, ACT.Copy).then_inc(*k.AC.mark("bias"))
                act.wait_ge(*k.PE.after("sum", i))
                nc.scalar.activation(r[:], k.AUX[3][:, 0:LAT], ACT.Sqrt, scale=1.0,
                                     bias=C["eps_width"][:, 0:1]).then_inc(*k.AC.mark("rms"))
                for x in range(4):
                    act.wait_ge(*k.DV.after(("nm", x), i))
                    nc.scalar.activation(sc[:, x, 0:n_keys[x]], sc[:, x, 0:n_keys[x]], ACT.Exp, bias=nm[:, x:x + 1],
                                         accum_out=sums[:, x:x + 1]).then_inc(*k.AC.mark(("exp", x)))
                    nc.scalar.activation(es[:, x:x + 1], sk[:, combos[x][0]:combos[x][0] + 1], ACT.Exp,
                                         bias=nm[:, x:x + 1]).then_inc(*k.AC.mark(("es", x)))
                    if x:
                        copy_p(x - 1, i)
                copy_p(3, i)
                act.wait_ge(*k.PE.after(("o", 3), i))
                nc.scalar.activation(row(o, pair * 4 + i)[:, 0:LAT], k.AUX[2][:, 0:LAT], ACT.Copy).then_inc(*k.AC.mark("ev"))

        @block.vector
        def _(dve):
            with k.DV.turns(dve, 4) as i:
                dve.wait_ge(*k.AC.after(("es", 3), i - 1))
                nc.vector.tensor_copy(sk[:, 0:2], sink[0][:, bass.ds((pair * 4 + i) * 2, 2)]).then_inc(*k.DV.mark("sink"))
                dve.wait_ge(*k.AC.after("rms", i))
                nc.vector.reciprocal(r[:], r[:]).then_inc(*k.DV.mark("r"))
                dve.wait_ge(*k.DV.after("r", i))
                nc.vector.scalar_tensor_tensor((qn if rope else qs)[:], row(q, pair * 4 + i), gain, r[:], ALU.mult,
                                               ALU.mult).then_inc(*k.DV.mark("qn" if rope else "qs"))
                if rope:
                    dve.wait_ge(*k.PE.after("rot", i))
                    nc.vector.tensor_tensor(qr[:], k.AUX[3][:, LAT:2 * LAT], C["sin"][:, CTX:TOK], ALU.mult).then_inc(*k.DV.mark("qr"))
                    nc.vector.tensor_tensor(qn[:], qn[:], C["cos"][:, CTX:TOK], ALU.mult).then_inc(*k.DV.mark("qc"))
                    dve.wait_ge(*k.DV.after("qc", i))
                    nc.vector.tensor_tensor(qs[:], qn[:], qr[:], ALU.add).then_inc(*k.DV.mark("qs"))
                dve.wait_ge(*k.DV.after("sink", i))
                if bias is not None:
                    dve.wait_ge(*k.AC.after("bias", i))
                for x, (hh, b) in enumerate(combos):
                    dve.wait_ge(*k.PE.after(("score", x), i))
                    nc.vector.memset(cols[:, 7, x:x + 1], 0.0).then_inc(*k.DV.mark(("scored", x)))
                    m = mask(b) if mask else bias[:, hh, 256 - n_keys[x]:256]
                    nc.vector.tensor_tensor_reduce(sc[:, x, 0:n_keys[x]], k.ACC[x][:, 0:n_keys[x]], m, 1.0, sk[:, hh:hh + 1],
                                                   ALU.add, ALU.max, mx[:, x:x + 1]).then_inc(*k.DV.mark(("max", x)))
                    dve.wait_ge(*k.DV.after(("max", x), i))
                    nc.vector.tensor_scalar(nm[:, x:x + 1], mx[:, x:x + 1], -1.0, None, ALU.mult).then_inc(*k.DV.mark(("nm", x)))
                for x in range(4):
                    dve.wait_ge(*k.AC.after(("es", x), i))
                    nc.vector.tensor_tensor(tot[:, x:x + 1], sums[:, x:x + 1], es[:, x:x + 1], ALU.add).then_inc(*k.DV.mark(("tot", x)))
                    dve.wait_ge(*k.DV.after(("tot", x), i))
                    nc.vector.reciprocal(rt[:, x:x + 1], tot[:, x:x + 1]).then_inc(*k.DV.mark(("rt", x)))
                    dve.wait_ge(*k.DV.after(("rt", x), i))
                    nc.vector.tensor_scalar(sc[:, x, 0:n_keys[x]], sc[:, x, 0:n_keys[x]], rt[:, x:x + 1], None,
                                            ALU.mult).then_inc(*k.DV.mark(("p", x)))

        @block.tensor
        def _(pe):
            def turn_p(x, i):
                pe.wait_ge(*k.DV.after(("p", x), i))
                if x >= 2:
                    pe.wait_ge(*k.AC.after(("pt", x - 2), i))
                for kt in range(n_keys[x] // P):
                    mm = nc.tensor.transpose(k.AUX[x % 2][:, blk(kt)], sc[:, x, blk(kt)], C["ident"][:])
                mm.then_inc(*k.PE.mark(("pT", x)))

            def output(x, i):
                hh, b = combos[x]
                pe.wait_ge(*k.AC.after(("pt", x), i))
                n = n_keys[x] // P
                at = (2 * pair + hh) * HEAD
                for kt in range(n):
                    mm = nc.tensor.matmul(half(k.AUX[2], hh)[:, blk(b)], v[:, keys[b][0] // P + kt, at:at + HEAD],
                                          pt[:, x % 2, blk(kt)], start=kt == 0, stop=kt == n - 1)
                mm.then_inc(*k.PE.mark(("o", x)))

            with k.PE.turns(pe, 4) as i:
                pe.wait_ge(*k.AC.after("sq", i))
                nc.tensor.matmul(k.AUX[3][:, 0:LAT], C["ones64"][:], sq[:], start=True, stop=True).then_inc(*k.PE.mark("sum"))
                if rope:
                    pe.wait_ge(*k.DV.after("qn", i))
                    nc.tensor.matmul(k.AUX[3][:, LAT:2 * LAT], C["rot"][:], qn[:], start=True, stop=True).then_inc(*k.PE.mark("rot"))
                pe.wait_ge(*k.DV.after("qs", i))
                for x, (hh, b) in enumerate(combos):
                    nc.tensor.matmul(k.ACC[x][:, 0:n_keys[x]], half(qs, hh)[:, blk(b)],
                                     half(ks, hh)[:, pair, keys[b][0]:keys[b][1]], start=True,
                                     stop=True).then_inc(*k.PE.mark(("score", x)))
                pe.wait_ge(*k.AC.after("ev", i - 1))
                turn_p(0, i)
                for x in range(1, 4):
                    turn_p(x, i)
                    output(x - 1, i)
                output(3, i)


def project(k, name, w, src, tokens, evict, ahead, group=4, engine=None):
    with k.open(name) as block:
        @block.sync
        def _(sp):
            stream(k, sp, w, group, ahead)

        @block.tensor
        def _(pe):
            linear(k, pe, w, group, KT, src, tokens, lambda n: k.AC)

        @block.scalar
        def _(act):
            with k.AC.turns(act, w.shape[0] // 2) as i:
                for n in range(2 * group):
                    act.wait_ge(*k.PE.after(("acc", n), i))
                    evict(act, n, i * (2 * group) + n).then_inc(*k.AC.mark(("ev", n)))
        if engine is not None:
            engine(block)
    close_stream(k, w.shape[0])


def project_kv(k, name, w, src, tokens, keys, v, ahead):
    nc = k.nc
    spots = tokens // P
    with k.open(name) as block:
        @block.sync
        def _(sp):
            for s in range(2):
                sp.wait_ge(*k.PE.after(("kv", s)))
                load_unit(k, sp, ahead, s, s)

        @block.tensor
        def _(pe):
            weights_here(k, pe, 0, 0, 2)
            for m in range(2):
                for d in range(KT):
                    at = (m * KT + d) * P
                    mm = nc.tensor.matmul(k.ACC[m][:, 0:tokens], k.W[:, 0, at:at + P], src(d), start=d == 0, stop=d == KT - 1)
            mm.then_inc(*k.PE.mark(("kv", 0)))
            weights_here(k, pe, 1, 0, 2)
            for t in range(spots):
                for d in range(KT):
                    mm = nc.tensor.matmul(k.AUX[t][:, 0:256], src(d)[:, t * P:(t + 1) * P], k.W[:, 1, d * 256:(d + 1) * 256],
                                          start=d == 0, stop=d == KT - 1)
            mm.then_inc(*k.PE.mark(("kv", 1)))

        @block.scalar
        def _(act):
            act.wait_ge(*k.PE.after(("kv", 0)))
            for m in range(2):
                nc.scalar.activation(keys[:, m, :], k.ACC[m][:, 0:tokens], ACT.Copy).then_inc(*k.AC.mark(("k", m)))

        @block.vector
        def _(dve):
            dve.wait_ge(*k.PE.after(("kv", 1)))
            for t in range(spots):
                nc.vector.tensor_copy(v[:, t, :], k.AUX[t][:, 0:256]).then_inc(*k.DV.mark(("v", t)))
    close_stream(k, 2)


def swa(k, new_in, modulated, gate, ahead):
    nc, w = k.nc, k.dram
    with ExitStack() as c:
        new = new_in(c)
        late_constants(k, new, ["cos", "sin", "window", "rot", "ones64", "swa_gains", "swa_sink", "eps_width", "eps"])
        q, keys, v = new("swa_q", KT, LAT), new("swa_k", 2, TOK), new("swa_v", 4, 256)
        with ExitStack() as cc:
            modulated(1, 1, new_in(cc)("squares", KT, TOK))
        copy = lambda act, n, at: nc.scalar.activation(row(q, at), k.ACC[n % 4][:, 0:LAT], ACT.Copy)
        project(k, "swa q", w["w_swa_q"], lambda d: k.H[:, d, CTX:TOK], LAT, copy, w["w_swa_kv"])
        project_kv(k, "swa kv", w["w_swa_kv"], lambda d: k.H[:, d, :], TOK, keys, v, w["w_swa_out"])
        gains = k.C["swa_gains"]
        with ExitStack() as cc:
            norm_heads(k, "swa keys", [[keys[:, 0, :]], [keys[:, 1, :]]], TOK, lambda n: gains[:, 1:2], k.C["ones64"],
                       HEAD, new_in(cc), rope=True)
        for pair in range(2):
            with ExitStack() as cc:
                window_heads(k, f"swa heads {pair}", pair, new_in(cc), q, keys, v, k.H, gains[:, 0:1],
                             [(0, TOK)] * 2, lambda b: k.C["window"][:, b, :], (k.C["swa_sink"],), True)
        to_residual(k, "swa out", w["w_swa_out"], lambda d: k.H[:, d, 0:LAT], LAT,
                    lambda dve, n, at, i: gated_residual(k, dve, n, at, CTX, gate), ahead)


def layout_swa(I, t):
    import numpy as np
    wq = I["swa_w_qkv"][0]
    order = np.concatenate([np.arange(h * HEAD, (h + 1) * HEAD) for h in Q_HEADS])
    t["w_swa_q"] = pack(wq[:, :1024][:, order], 4)
    t["w_swa_kv"] = pack_kv(wq[:, 1024:1280], wq[:, 1280:])
    t["w_swa_out"] = pack(I["swa_w_out"][0][order], 4)
    t["late_swa_gains"] = np.stack([np.tile(I[n][0], 2) for n in ("swa_q_gain", "swa_k_gain")], 1)
    t["late_swa_sink"] = rows(I["swa_sink"][0][Q_HEADS], 16)
    t["late_eps_width"] = np.full((P, 1), EPS * HEAD, np.float32)
    t["late_eps"] = np.full((P, 1), EPS, np.float32)


def pack_kv(wk, wv):
    import numpy as np
    return np.stack([pack(wk, 2)[0], wv.reshape(KT, P, 256).transpose(1, 0, 2).reshape(P, 2048)])



SSD_HEADS = 32
GROUPS = 4
INNER = 16
CONV = 31
SECOND_CONSTANTS = ["norm_mix", "gate_bias", "conv_dw_w", "conv_dw_b", "conv_ln_g", "conv_ln_b", "ssd_conv_w",
                    "ssd_conv_b", "w_dt", "ssd_dt_bias", "ssd_a_log", "ssd_d", "ssd_norm_g", "attn_gains",
                    "attn_sinks", "norm_xattn", "norm_mem", "xattn_gains", "norm_mlp", "ones64", "eps_width",
                    "eps", "eps_xattn"]


def long_conv(k, dve, first, count, x, y):
    nc, w = k.nc, k.C["conv_dw_w"]
    with k.DV.turns(dve, count) as i:
        at = i + first
        tap = lambda j: w[:, bass.ds(at, 1), j:j + 1].rearrange("p a b -> p (a b)")
        nc.vector.tensor_scalar(row(y, at), row(x, at), tap(CONV - 1), k.C["conv_dw_b"][:, bass.ds(at, 1)], ALU.mult,
                                ALU.add).then_inc(*k.DV.mark(("tap", CONV - 1)))
        for j in reversed(range(CONV - 1)):
            a = CONV - 1 - j
            dve.wait_ge(*k.DV.after(("tap", j + 1), i))
            nc.vector.scalar_tensor_tensor(row(y, at)[:, a:LAT], row(x, at)[:, 0:LAT - a], tap(j), row(y, at)[:, a:LAT],
                                           ALU.mult, ALU.add).then_inc(*k.DV.mark(("tap", j)))


def glu(k, w, src, out, sig, ahead):
    nc = k.nc
    with k.open("glu") as block:
        @block.sync
        def _(sp):
            stream(k, sp, w, 4, ahead)

        @block.tensor
        def _(pe):
            linear(k, pe, w, 4, KT, src, LAT, lambda n: k.AC if n % 2 else k.DV)

        @block.scalar
        def _(act):
            with k.AC.turns(act, 2) as i:
                for n in range(1, 8, 2):
                    act.wait_ge(*k.PE.after(("acc", n), i))
                    act.wait_ge(*k.DV.after(("ev", n - 1), i - 1))
                    nc.scalar.activation(sig[:, n // 2, :], k.ACC[n % 4][:, 0:LAT], ACT.Sigmoid).then_inc(*k.AC.mark(("ev", n)))

        @block.vector
        def _(dve):
            with k.DV.turns(dve, 2) as i:
                for n in range(0, 8, 2):
                    dve.wait_ge(*k.AC.after(("ev", n + 1), i))
                    nc.vector.tensor_tensor(row(out, i * 4 + n // 2), sig[:, n // 2, :], k.ACC[n % 4][:, 0:LAT],
                                            ALU.mult).then_inc(*k.DV.mark(("ev", n)))
    close_stream(k, w.shape[0])


def band_bias(k, new, biasm):
    nc = k.nc
    late_constants(k, new, ["bucket", "rel_table", "band"])
    by_dist = new("by_dist", 384)
    skew = nc.dram_tensor(f"skew{int(k.stage[1])}", [P, 16, 384], F32, kind="Internal").ap()
    with k.open("band bias") as block:
        @block.tensor
        def _(pe):
            nc.tensor.matmul(k.ACC[0][0:16, 0:384], k.C["rel_table"][0:32, :], k.C["bucket"][0:32, :], start=True,
                             stop=True).then_inc(*k.PE.mark("by_dist"))

        @block.scalar
        def _(act):
            act.wait_ge(*k.PE.after("by_dist"))
            nc.scalar.activation(by_dist[0:16, :], k.ACC[0][0:16, 0:384], ACT.Copy).then_inc(*k.AC.mark("by_dist"))

        @block.sync
        def _(sp):
            sp.wait_ge(*k.AC.after("by_dist"))
            sp.dma_start(skew.rearrange("i h x -> h i x"),
                         by_dist[0:16, :].unsqueeze(1).to_broadcast([16, P, 384])).then_inc(k.stored, 16)
            sp.wait_ge(k.stored, k.stores + 16)
            shifted = bass.AP(tensor=skew.tensor, offset=P - 1, ap=[[16 * 384 - 1, P], [384, 16], [1, 256]])
            sp.dma_start(biasm[:], shifted).then_inc(k.stored, 16)
            sp.wait_ge(k.stored, k.stores + 32)

        @block.vector
        def _(dve):
            dve.wait_ge(k.stored, k.stores + 32)
            nc.vector.tensor_tensor(biasm[:], biasm[:], k.C["band"][:].unsqueeze(1).to_broadcast([P, 16, 256]),
                                    ALU.add).then_inc(*k.DV.mark("masked"))
    k.stores += 32


def conv_norm(k, x, sq):
    nc, C = k.nc, k.C
    mean, r = k.R[:, 0, 0:LAT], k.R[:, 1, 0:LAT]
    with k.open("conv norm") as block:
        @block.tensor
        def _(pe):
            for d in range(KT):
                mm = nc.tensor.matmul(k.ACC[0][:, 0:LAT], C["ones"][:], x[:, d, :], start=d == 0, stop=d == KT - 1)
            mm.then_inc(*k.PE.mark("sum"))
            for d in range(KT):
                pe.wait_ge(*k.AC.after(("sq", d)))
                mm = nc.tensor.matmul(k.ACC[1][:, 0:LAT], C["ones"][:], sq[:, d, 0:LAT], start=d == 0, stop=d == KT - 1)
            mm.then_inc(*k.PE.mark("squares"))

        @block.scalar
        def _(act):
            act.wait_ge(*k.PE.after("sum"))
            nc.scalar.activation(mean, k.ACC[0][:, 0:LAT], ACT.Copy, scale=1.0 / D).then_inc(*k.AC.mark("mean"))
            for d in range(KT):
                act.wait_ge(*k.DV.after(("centred", d)))
                nc.scalar.activation(sq[:, d, 0:LAT], x[:, d, :], ACT.Square).then_inc(*k.AC.mark(("sq", d)))
            act.wait_ge(*k.PE.after("squares"))
            nc.scalar.activation(r, k.ACC[1][:, 0:LAT], ACT.Sqrt, scale=1.0 / D, bias=k.EPSC[:]).then_inc(*k.AC.mark("std"))
            for d in range(KT):
                act.wait_ge(*k.DV.after(("normed", d)))
                nc.scalar.activation(x[:, d, :], x[:, d, :], ACT.Silu, scale=C["conv_ln_g"][:, d:d + 1],
                                     bias=C["conv_ln_b"][:, d:d + 1]).then_inc(*k.AC.mark(("out", d)))

        @block.vector
        def _(dve):
            dve.wait_ge(*k.AC.after("mean"))
            for d in range(KT):
                nc.vector.tensor_tensor(x[:, d, :], x[:, d, :], mean, ALU.subtract).then_inc(*k.DV.mark(("centred", d)))
            dve.wait_ge(*k.AC.after("std"))
            nc.vector.reciprocal(r, r).then_inc(*k.DV.mark("r"))
            dve.wait_ge(*k.DV.after("r"))
            for d in range(KT):
                nc.vector.tensor_tensor(x[:, d, :], x[:, d, :], r, ALU.mult).then_inc(*k.DV.mark(("normed", d)))


def ssd_prepare(k, u, xbc, dt, da, cs, dte, tmp, cb, btok):
    nc, C = k.nc, k.C
    flat = lambda t: t[:].rearrange("p a b -> p (a b)")
    state_in, state_out = lambda g: xbc[:, INNER + g, :], lambda g: xbc[:, INNER + GROUPS + g, :]
    with k.open("ssd prepare") as block:
        @block.tensor
        def _(pe):
            for t in range(2):
                for d in range(KT):
                    mm = nc.tensor.matmul(k.AUX[0][:, t * 32:(t + 1) * 32], u(d)[:, t * P:(t + 1) * P], C["w_dt"][:, d, :],
                                          start=d == 0, stop=d == KT - 1)
            mm.then_inc(*k.PE.mark("dt"))
            for g in range(GROUPS):
                for c in range(2):
                    at = slice(c * P, (c + 1) * P)
                    out = (g % 2) * 256 + c * P
                    mm = nc.tensor.matmul(k.ACC[g // 2][:, out:out + P], state_in(g)[:, at], state_out(g)[:, at], start=True,
                                          stop=True)
                if g % 2:
                    mm.then_inc(*k.PE.mark(("cb", g // 2)))
            for g in range(GROUPS):
                mm = nc.tensor.transpose(k.ACC[2][:, g * P:(g + 1) * P], state_in(g)[:, 0:P], C["ident"][:])
            mm.then_inc(*k.PE.mark("btok"))
            pe.wait_ge(*k.DV.after("da"))
            nc.tensor.matmul(k.AUX[1][:, 0:64], C["until"][:, 0, :], flat(da), start=True, stop=True)
            nc.tensor.matmul(k.AUX[1][:, 64:96], C["ones"][:], da[:, 0, :], start=True, stop=True).then_inc(*k.PE.mark("cs"))

        @block.vector
        def _(dve):
            dve.wait_ge(*k.PE.after("dt"))
            nc.vector.tensor_tensor(tmp[:, 0], k.AUX[0][:, 0:64], C["ssd_dt_bias"][:], ALU.add).then_inc(*k.DV.mark("x"))
            dve.wait_ge(*k.DV.after("x"))
            nc.vector.scalar_tensor_tensor(tmp[:, 1], tmp[:, 0], -1.0, tmp[:, 0], ALU.mult, ALU.max).then_inc(*k.DV.mark("|x|"))
            dve.wait_ge(*k.AC.after("ln"))
            nc.vector.scalar_tensor_tensor(flat(dt), tmp[:, 0], 0.0, tmp[:, 1], ALU.max, ALU.add).then_inc(*k.DV.mark("dt"))
            dve.wait_ge(*k.DV.after("dt"))
            nc.vector.scalar_tensor_tensor(flat(da), flat(dt), -1.0, C["ssd_a_log"][:], ALU.mult, ALU.mult).then_inc(*k.DV.mark("da"))
            dve.wait_ge(*k.PE.after("cs"))
            nc.vector.tensor_copy(flat(cs), k.AUX[1][:, 0:64]).then_inc(*k.DV.mark("cs"))
            dve.wait_ge(*k.DV.after("cs"))
            nc.vector.tensor_tensor(dte[:], k.AUX[1][:, 64:96], cs[:, 0, :], ALU.subtract).then_inc(*k.DV.mark("to end"))
            dve.wait_ge(*k.AC.after("dte"))
            nc.vector.tensor_tensor(dte[:], dte[:], dt[:, 0, :], ALU.mult).then_inc(*k.DV.mark("dte"))

        @block.scalar
        def _(act):
            nc.scalar.activation(C["ssd_a_log"][:], C["ssd_a_log"][:], ACT.Exp).then_inc(*k.AC.mark("a"))
            act.wait_ge(*k.DV.after("|x|"))
            nc.scalar.activation(tmp[:, 1], tmp[:, 1], ACT.Exp, scale=-1.0).then_inc(*k.AC.mark("exp"))
            act.wait_ge(*k.AC.after("exp"))
            nc.scalar.activation(tmp[:, 1], tmp[:, 1], ACT.Ln, bias=1.0).then_inc(*k.AC.mark("ln"))
            for h in range(2):
                act.wait_ge(*k.PE.after(("cb", h)))
                nc.scalar.activation(cb[:, 2 * h:2 * h + 2, :].rearrange("p g n -> p (g n)"), k.ACC[h][:],
                                     ACT.Copy).then_inc(*k.AC.mark(("cb", h)))
            act.wait_ge(*k.PE.after("btok"))
            nc.scalar.activation(flat(btok), k.ACC[2][:], ACT.Copy).then_inc(*k.AC.mark("btok"))
            act.wait_ge(*k.DV.after("to end"))
            nc.scalar.activation(dte[:], dte[:], ACT.Exp).then_inc(*k.AC.mark("dte"))


def ssd_heads(k, g, new, xbc, z, dt, da, cs, dte, cb, btok):
    nc, C = k.nc, k.C
    xh, xtok, xdt, xe = new("s_xh", LAT), new("s_xtok", 2, P), new("s_xdt", 2, 2, 64), new("s_xe", 2, 64)
    gu, dec, sct = (new("s_" + n, 4, P) for n in ("gu", "dec", "sct"))
    egb, cme, st, y = new("s_egb", 2, P), new("s_cme", 2, P), new("s_st", P), new("s_y", LAT)
    flat = lambda t: t[:].rearrange("p a b -> p (a b)")
    combos = [(hh, c) for hh in range(2) for c in range(2)]
    csb = k.AUX[1][:].rearrange("p (x t) -> p x t", x=4)
    with k.open(f"ssd heads {g}") as block:
        head = lambda i, hh: bass.ds((g * 4 + i) * 2 + hh, 1)

        @block.scalar
        def _(act):
            with k.AC.turns(act, 4) as i:
                act.wait_ge(*k.DV.after("y1", i - 1))
                nc.scalar.activation(xh[:], row(xbc, g * 4 + i), ACT.Copy).then_inc(*k.AC.mark("xh"))
                act.wait_ge(*k.PE.after("xT", i))
                nc.scalar.activation(flat(xtok), k.AUX[0][:, 0:256], ACT.Copy).then_inc(*k.AC.mark("xtok"))
                act.wait_ge(*k.PE.after("csb", i))
                for hh in range(2):
                    nc.scalar.activation(egb[:, hh, :], csb[:, hh * 2 + 1, :], ACT.Exp).then_inc(*k.AC.mark(("egb", hh)))
                act.wait_ge(*k.DV.after(("dd", 3), i))
                nc.scalar.activation(flat(dec), flat(dec), ACT.Exp).then_inc(*k.AC.mark("dec"))
                act.wait_ge(*k.PE.after("state", i))
                nc.scalar.activation(st[:], k.AUX[2][:, 0:P], ACT.Copy).then_inc(*k.AC.mark("st"))

        @block.tensor
        def _(pe):
            with k.PE.turns(pe, 4) as i:
                pe.wait_ge(*k.DV.after("gu3", i))
                nc.tensor.matmul(k.AUX[1][:], C["ones"][:], flat(gu), start=True, stop=True).then_inc(*k.PE.mark("csb"))
                pe.wait_ge(*k.AC.after("xh", i))
                for c in range(2):
                    mm = nc.tensor.transpose(k.AUX[0][:, c * P:(c + 1) * P], xh[:, c * P:(c + 1) * P], C["ident"][:])
                mm.then_inc(*k.PE.mark("xT"))
                pe.wait_ge(*k.DV.after(("xe", 1), i))
                nc.tensor.matmul(k.AUX[2][:, 0:P], btok[:, g, :], flat(xe), start=True, stop=True).then_inc(*k.PE.mark("state"))
                pe.wait_ge(*k.DV.after("cme", i))
                pe.wait_ge(*k.AC.after("st", i))
                for x, (hh, c) in enumerate(combos):
                    out = k.AUX[3][hh * 64:(hh + 1) * 64, c * P:(c + 1) * P]
                    mm = nc.tensor.matmul(out, xdt[:, c, hh, :], sct[:, x, :], start=True, stop=c == 0)
                    if c:
                        mm = nc.tensor.matmul(out, st[:, hh * 64:(hh + 1) * 64], cme[:, hh, :], start=False, stop=True)
                mm.then_inc(*k.PE.mark("y"))

        @block.vector
        def _(dve):
            with k.DV.turns(dve, 4) as i:
                for x, (hh, c) in enumerate(combos):
                    nc.vector.tensor_scalar(gu[:, x, :], C["until"][:, 0, :], da[:, c, head(i, hh)], None,
                                            ALU.mult).then_inc(*k.DV.mark(f"gu{x}"))
                dve.wait_ge(*k.AC.after("xtok", i))
                for x, (hh, c) in enumerate(combos):
                    nc.vector.tensor_scalar(xdt[:, c, hh, :], xtok[:, c, hh * 64:(hh + 1) * 64], dt[:, c, head(i, hh)], None,
                                            ALU.mult).then_inc(*k.DV.mark(("xdt", x)))
                for hh in range(2):
                    nc.vector.tensor_scalar(xe[:, hh, :], xtok[:, 0, hh * 64:(hh + 1) * 64], dte[:, head(i, hh)], None,
                                            ALU.mult).then_inc(*k.DV.mark(("xe", hh)))
                dve.wait_ge(*k.AC.after(("egb", 1), i))
                for x, (hh, c) in enumerate(combos):
                    nc.vector.scalar_tensor_tensor(dec[:, x, :], csb[:, x, :], cs[:, c, head(i, hh)], C["behind"][:, 0, :],
                                                   ALU.subtract, ALU.add).then_inc(*k.DV.mark(("dd", x)))
                dve.wait_ge(*k.AC.after("dec", i))
                for hh in range(2):
                    nc.vector.tensor_tensor(sct[:, 2 * hh:2 * hh + 2, :].rearrange("p a b -> p (a b)"),
                                            dec[:, 2 * hh:2 * hh + 2, :].rearrange("p a b -> p (a b)"), cb[:, g, :],
                                            ALU.mult).then_inc(*k.DV.mark(("sct", hh)))
                nc.vector.tensor_tensor(cme[:], egb[:], xbc[:, INNER + GROUPS + g, P:2 * P].unsqueeze(1).to_broadcast([P, 2, P]),
                                        ALU.mult).then_inc(*k.DV.mark("cme"))
                dve.wait_ge(*k.PE.after("y", i))
                nc.vector.scalar_tensor_tensor(y[:], xh[:], C["ssd_d"][:, bass.ds(g * 4 + i, 1)], k.AUX[3][:, 0:LAT], ALU.mult,
                                               ALU.add).then_inc(*k.DV.mark("y1"))
                dve.wait_ge(*k.DV.after("y1", i))
                nc.vector.tensor_tensor(row(xbc, g * 4 + i), y[:], row(z, g * 4 + i), ALU.mult).then_inc(*k.DV.mark("y2"))


def cross_heads(k, new, q, keys, v, o):
    nc = k.nc
    combos = [(h, b) for h in range(4) for b in range(2)]
    sc, pt, cols = new("x_scores", 4, 256), new("x_pt", 2, 256), new("x_cols", 4, 8)
    mx, nm, sums, rt = (cols[:, n, :] for n in range(4))
    blk = lambda b: slice(b * P, (b + 1) * P)
    with k.open("cross heads") as block:
        @block.tensor
        def _(pe):
            def score(x):
                h, b = combos[x]
                if x >= 4:
                    pe.wait_ge(*k.AC.after(("exp", x - 4)))
                for e in range(2):
                    mm = nc.tensor.matmul(k.ACC[x % 4][:, 0:256], q[:, 2 * h + e, blk(b)], keys[:, 2 * h + e, :],
                                          start=e == 0, stop=e == 1)
                mm.then_inc(*k.PE.mark(("score", x)))

            def turn_p(x):
                pe.wait_ge(*k.DV.after(("p", x)))
                if x >= 2:
                    pe.wait_ge(*k.AC.after(("pt", x - 2)))
                for t in range(2):
                    mm = nc.tensor.transpose(k.AUX[x % 2][:, blk(t)], sc[:, x % 4, blk(t)], k.C["ident"][:])
                mm.then_inc(*k.PE.mark(("pT", x)))

            def output(x):
                h, b = combos[x]
                pe.wait_ge(*k.AC.after(("pt", x)))
                if x >= 2:
                    pe.wait_ge(*k.AC.after(("ev", x - 2)))
                for e in range(2):
                    for t in range(2):
                        at = (2 * h + e) * P
                        mm = nc.tensor.matmul(k.AUX[2 + x % 2][:, blk(e)], v[:, t, at:at + P], pt[:, x % 2, blk(t)],
                                              start=t == 0, stop=t == 1)
                mm.then_inc(*k.PE.mark(("o", x)))

            for x in range(4):
                score(x)
            for x in range(9):
                if x < 8:
                    turn_p(x)
                if 1 <= x:
                    output(x - 1)
                if x + 4 < 8:
                    score(x + 4)

        @block.scalar
        def _(act):
            for x in range(9):
                if x < 8:
                    act.wait_ge(*k.DV.after(("nm", x)))
                    if x >= 4:
                        act.wait_ge(*k.PE.after(("pT", x - 4)))
                    nc.scalar.activation(sc[:, x % 4, :], k.ACC[x % 4][:, 0:256], ACT.Exp, bias=nm[:, x:x + 1],
                                         accum_out=sums[:, x:x + 1]).then_inc(*k.AC.mark(("exp", x)))
                if x >= 1:
                    y = x - 1
                    h, b = combos[y]
                    act.wait_ge(*k.PE.after(("pT", y)))
                    if y >= 2:
                        act.wait_ge(*k.PE.after(("o", y - 2)))
                    nc.scalar.activation(pt[:, y % 2, :], k.AUX[y % 2][:, 0:256], ACT.Copy).then_inc(*k.AC.mark(("pt", y)))
                    act.wait_ge(*k.PE.after(("o", y)))
                    nc.scalar.activation(o[:, 2 * h:2 * h + 2, blk(b)],
                                         k.AUX[2 + y % 2][:, 0:256].rearrange("p (e t) -> p e t", e=2),
                                         ACT.Copy).then_inc(*k.AC.mark(("ev", y)))

        @block.vector
        def _(dve):
            def maximum(x):
                dve.wait_ge(*k.PE.after(("score", x)))
                nc.vector.reduce_max(mx[:, x:x + 1], k.ACC[x % 4][:, 0:256], AX_X).then_inc(*k.DV.mark(("max", x)))
                dve.wait_ge(*k.DV.after(("max", x)))
                nc.vector.tensor_scalar(nm[:, x:x + 1], mx[:, x:x + 1], -1.0, None, ALU.mult).then_inc(*k.DV.mark(("nm", x)))

            for x in range(2):
                maximum(x)
            for x in range(8):
                dve.wait_ge(*k.AC.after(("exp", x)))
                nc.vector.reciprocal(rt[:, x:x + 1], sums[:, x:x + 1]).then_inc(*k.DV.mark(("rt", x)))
                dve.wait_ge(*k.DV.after(("rt", x)))
                nc.vector.tensor_scalar(sc[:, x % 4, :], sc[:, x % 4, :], rt[:, x:x + 1], None, ALU.mult).then_inc(*k.DV.mark(("p", x)))
                if x + 2 < 8:
                    maximum(x + 2)


def memory_values(k, w, mem, v, ahead):
    nc = k.nc
    with k.open("cross v") as block:
        @block.sync
        def _(sp):
            for s in range(2):
                sp.wait_ge(*k.PE.after(("v", s, 1)))
                load_unit(k, sp, ahead, s, s)

        @block.tensor
        def _(pe):
            for s in range(2):
                weights_here(k, pe, s, 0, 2)
                for t in range(2):
                    for d in range(KT):
                        mm = nc.tensor.matmul(k.ACC[2 * s + t][:], mem[:, d, t * P:(t + 1) * P], k.W[:, s, d * 512:(d + 1) * 512],
                                              start=d == 0, stop=d == KT - 1)
                    mm.then_inc(*k.PE.mark(("v", s, t)))

        @block.scalar
        def _(act):
            for s in range(2):
                for t in range(2):
                    act.wait_ge(*k.PE.after(("v", s, t)))
                    nc.scalar.activation(v[:, t, s * 512:(s + 1) * 512], k.ACC[2 * s + t][:], ACT.Copy).then_inc(*k.AC.mark(("v", s, t)))
    close_stream(k, 2)


def second(k, new_in, w):
    nc, C = k.nc, k.C
    X = lambda d: k.X[:, d, CTX:TOK]
    u = lambda d: k.H[:, d, 0:LAT]
    column = lambda t: lambda d: t[:, d:d + 1]
    parts = lambda name: [(0, LAT, column(C[name]), None)]

    with ExitStack() as c:
        new = new_in(c)
        late_constants(k, new, SECOND_CONSTANTS)
        merged = new("merged", KT, LAT)
        with ExitStack() as cc:
            norm(k, "norm mix", X, u, LAT, parts("norm_mix"), new_in(cc)("squares", KT, LAT))
        with ExitStack() as cm:
            mixing = new_in(cm)
            gates, cv = mixing("gates", 24, LAT), mixing("cv", KT, LAT)

            def branch(name, weights, src, first_gate, ahead, tmp):
                def write(dve, n, at, i):
                    gate_tile, bank = row(gates, first_gate + at), k.ACC[n % 4][:, 0:LAT]
                    if first_gate == 16:
                        nc.vector.tensor_tensor(row(merged, at), gate_tile, bank, ALU.mult).then_inc(*k.DV.mark(("ev", n)))
                        return
                    nc.vector.tensor_tensor(tmp[:, n % 2, 0:LAT], gate_tile, bank, ALU.mult).then_inc(*k.DV.mark(("ev", n)))
                    dve.wait_ge(*k.DV.after(("ev", n), i))
                    nc.vector.tensor_tensor(row(merged, at), row(merged, at), tmp[:, n % 2, 0:LAT], ALU.add).then_inc(*k.DV.mark(("add", n)))
                to_residual(k, name, weights, src, LAT, write, ahead)

            with ExitStack() as cg:
                gl = new_in(cg)("gl", KT, LAT)
                with ExitStack() as cc:
                    glu(k, w["w_conv"], u, gl, new_in(cc)("sig", 4, LAT), w["w_gate"])

                def conv_beside(first, count):
                    def engine(block):
                        @block.vector
                        def _(dve):
                            long_conv(k, dve, first, count, gl, cv)
                    return engine

                sigmoid = lambda act, n, at: nc.scalar.activation(row(gates, at), k.ACC[n % 4][:, 0:LAT], ACT.Sigmoid,
                                                                  bias=C["gate_bias"][:, bass.ds(at, 1)])
                project(k, "gates", w["w_gate"], u, LAT, sigmoid, w["w_q"], engine=conv_beside(0, 5))
                with ExitStack() as cc:
                    local = new_in(cc)
                    q, keys, v, o = local("q2", KT, LAT), local("k2", 2, LAT), local("v2", 2, 256), local("o2", KT, LAT)
                    copy = lambda act, n, at: nc.scalar.activation(row(q, at), k.ACC[n % 4][:, 0:LAT], ACT.Copy)
                    project(k, "q", w["w_q"], u, LAT, copy, w["w_kv"], engine=conv_beside(5, 3))
                    project_kv(k, "kv", w["w_kv"], u, LAT, keys, v, w["w_attn_out"])
                    gains = C["attn_gains"]
                    biasm = local("biasm", 16, 256)
                    with ExitStack() as c3:
                        band_bias(k, new_in(c3), biasm)
                    with ExitStack() as c3:
                        norm_heads(k, "keys", [[keys[:, 0, :]], [keys[:, 1, :]]], LAT, lambda n: gains[:, 1:2], C["ones64"],
                                   HEAD, new_in(c3))
                    for pair in range(2):
                        with ExitStack() as c3:
                            window_heads(k, f"heads {pair}", pair, new_in(c3), q, keys, v, o, gains[:, 0:1],
                                         [(0, P), (0, LAT)], None, (C["attn_sinks"], biasm), False)
                    branch("attention out", w["w_attn_out"], lambda d: o[:, d, :], 16, w["w_conv_out"], None)
            conv_norm(k, cv, k.X[:, :, 0:CTX])
            branch("conv out", w["w_conv_out"], lambda d: cv[:, d, :], 0, w["w_z"], k.R)
            with ExitStack() as cc:
                local = new_in(cc)
                z, xbc = local("z2", INNER, LAT), local("xbc", INNER + 2 * GROUPS, LAT)
                silu = lambda act, n, at: nc.scalar.activation(row(z, at), k.ACC[n % 4][:, 0:LAT], ACT.Silu)
                project(k, "z", w["w_z"], u, LAT, silu, w["w_xbc"])
                with ExitStack() as c3:
                    taps = C["ssd_conv_w"]
                    conv_silu(k, "xbc", w["w_xbc"], u, 1, LAT, taps, taps.shape[2] - 1, C["ssd_conv_b"], xbc,
                              new_in(c3)("convs2", 4, LAT), w["w_ssd_out"])
                dt, da, cs, dte, tmp = local("dt", 2, 32), local("da", 2, 32), local("cs", 2, 32), local("dte", 32), local("stmp", 2, 64)
                cb, btok = local("cb", GROUPS, 256), local("btok", GROUPS, P)
                ssd_prepare(k, u, xbc, dt, da, cs, dte, tmp, cb, btok)
                for g in range(GROUPS):
                    with ExitStack() as c3:
                        ssd_heads(k, g, new_in(c3), xbc, z, dt, da, cs, dte, cb, btok)
                ssd_norm(k, xbc, k.X[:, :, 0:CTX])
                branch("ssd out", w["w_ssd_out"], lambda d: xbc[:, d, :], 8, w["w_mix"], k.R)

        def plain(dve, n, at, i):
            x = row(k.X, at)[:, CTX:TOK]
            nc.vector.tensor_tensor(x, x, k.ACC[n % 4][:, 0:LAT], ALU.add).then_inc(*k.DV.mark(("ev", n)))

        to_residual(k, "mix out", w["w_mix"], lambda d: merged[:, d, :], LAT, plain, w["w_xq"])
        with ExitStack() as cc:
            local = new_in(cc)
            sq = local("squares", KT, LAT)
            q, keys, v, o = local("xq", KT, LAT), local("xk", KT, LAT), local("xv", 2, D), local("xo", KT, LAT)
            late_constants(k, local, ["mem"])
            mem = C["mem"]
            m = lambda d: mem[:, d, :]
            norm(k, "norm xattn", X, u, LAT, parts("norm_xattn"), sq)
            norm(k, "norm mem", m, m, LAT, parts("norm_mem"), sq)
            into = lambda t: lambda act, n, at: nc.scalar.activation(row(t, at), k.ACC[n % 4][:, 0:LAT], ACT.Copy)
            project(k, "cross q", w["w_xq"], u, LAT, into(q), w["w_xk"])
            project(k, "cross k", w["w_xk"], m, LAT, into(keys), w["w_xv"])
            memory_values(k, w["w_xv"], mem, v, w["w_xo"])
            gains = C["xattn_gains"]
            heads = lambda t: [[t[:, 2 * h, :], t[:, 2 * h + 1, :]] for h in range(4)]
            with ExitStack() as c3:
                norm_heads(k, "cross q norm", heads(q), LAT, lambda n: gains[:, n:n + 1], C["ones"], 256, new_in(c3),
                           softmax_scale=256 ** -0.5, eps="eps_xattn")
            with ExitStack() as c3:
                norm_heads(k, "cross k norm", heads(keys), LAT, lambda n: gains[:, 2 + n:3 + n], C["ones"], 256, new_in(c3))
            with ExitStack() as c3:
                cross_heads(k, new_in(c3), q, keys, v, o)
            to_residual(k, "cross out", w["w_xo"], lambda d: o[:, d, :], LAT, plain, w["w_up"])
        with ExitStack() as cc:
            local = new_in(cc)
            hidden, relus = local("hidden2", 4 * KT, LAT), local("relus", 4, LAT)
            norm(k, "norm mlp", X, u, LAT, parts("norm_mlp"), hidden)
            squared_mlp_up(k, w["w_up"], u, hidden, relus, w["w_down"])
            to_residual(k, "down", w["w_down"], lambda d: hidden[:, d, :], LAT, plain, None)


def squared_mlp_up(k, w, u, hidden, relus, ahead):
    nc = k.nc
    turns = w.shape[0] // 2
    with k.open("up") as block:
        @block.sync
        def _(sp):
            stream(k, sp, w, 4, ahead)

        @block.tensor
        def _(pe):
            linear(k, pe, w, 4, KT, u, LAT, lambda n: k.DV)

        @block.scalar
        def _(act):
            with k.AC.turns(act, turns) as i:
                for n in range(8):
                    act.wait_ge(*k.PE.after(("acc", n), i))
                    act.wait_ge(*(k.DV.after(("ev", n - 4), i) if n >= 4 else k.DV.after(("ev", n + 4), i - 1)))
                    nc.scalar.activation(relus[:, n % 4, :], k.ACC[n % 4][:, 0:LAT], ACT.Relu).then_inc(*k.AC.mark(("relu", n)))

        @block.vector
        def _(dve):
            with k.DV.turns(dve, turns) as i:
                for n in range(8):
                    dve.wait_ge(*k.AC.after(("relu", n), i))
                    nc.vector.tensor_tensor(row(hidden, i * 8 + n), relus[:, n % 4, :], k.ACC[n % 4][:, 0:LAT],
                                            ALU.mult).then_inc(*k.DV.mark(("ev", n)))
    close_stream(k, w.shape[0])


def ssd_norm(k, y, sq):
    nc = k.nc
    r = lambda g: k.R[:, g // 2, (g % 2) * LAT:(g % 2 + 1) * LAT]
    with k.open("ssd norm") as block:
        @block.scalar
        def _(act):
            for t in range(INNER):
                if t >= KT:
                    act.wait_ge(*k.PE.after(("sum", (t - KT) // 4)))
                nc.scalar.activation(sq[:, t % KT, :], y[:, t, :], ACT.Square).then_inc(*k.AC.mark(("sq", t)))
            for g in range(GROUPS):
                act.wait_ge(*k.PE.after(("sum", g)))
                nc.scalar.activation(r(g), k.ACC[g][:, 0:LAT], ACT.Sqrt, scale=1.0 / 512, bias=k.EPSC[:]).then_inc(*k.AC.mark(("rms", g)))

        @block.tensor
        def _(pe):
            for t in range(INNER):
                pe.wait_ge(*k.AC.after(("sq", t)))
                mm = nc.tensor.matmul(k.ACC[t // 4][:, 0:LAT], k.C["ones"][:], sq[:, t % KT, :], start=t % 4 == 0, stop=t % 4 == 3)
                if t % 4 == 3:
                    mm.then_inc(*k.PE.mark(("sum", t // 4)))

        @block.vector
        def _(dve):
            for g in range(GROUPS):
                dve.wait_ge(*k.AC.after(("rms", g)))
                nc.vector.reciprocal(r(g), r(g)).then_inc(*k.DV.mark(("r", g)))
                dve.wait_ge(*k.DV.after(("r", g)))
                for t in range(4 * g, 4 * g + 4):
                    nc.vector.scalar_tensor_tensor(y[:, t, :], y[:, t, :], k.C["ssd_norm_g"][:, t:t + 1], r(g), ALU.mult,
                                                   ALU.mult).then_inc(*k.DV.mark(("out", t)))


def layout_second(I, t):
    import numpy as np
    I = {n[:-2]: (a if n in ("mem_2", "rel_table_2") else a[0]) for n, a in I.items() if n.endswith("_2")}
    win = I["w_in"]
    cuts = np.cumsum([0, 2048, 2048, 3072, 32, 1024, 256, 256, 3072])
    conv, z, xbc, dt, q, kk, v, gate = (win[:, a:b] for a, b in zip(cuts[:-1], cuts[1:]))
    order = np.concatenate([np.arange(h * HEAD, (h + 1) * HEAD) for h in Q_HEADS])
    t["w_conv"] = pack(conv.reshape(D, 2, KT, P).transpose(0, 2, 1, 3).reshape(D, 2 * D), 4)
    t["w_gate"], t["w_z"], t["w_xbc"] = pack(gate, 4), pack(z, 4), pack(xbc, 4)
    t["w_q"], t["w_kv"] = pack(q[:, order], 4), pack_kv(kk, v)
    t["w_attn_out"] = pack(I["w_attn_out"][order], 4)
    t["w_conv_out"], t["w_ssd_out"], t["w_mix"] = pack(I["w_conv_out"], 4), pack(I["w_ssd_out"], 2), pack(I["w_mix_out"], 4)
    t["w_xq"], t["w_xk"], t["w_xo"] = pack(I["w_xq"], 4), pack(I["w_xkv"][:, :D], 4), pack(I["w_xo"], 4)
    t["w_xv"] = I["w_xkv"][:, D:].reshape(KT, P, 2, 512).transpose(2, 1, 0, 3).reshape(2, P, 4096)
    t["w_up"], t["w_down"] = pack(I["w_mlp_up"], 4), pack(I["w_mlp_down"], 1)
    t["late_w_dt"] = dt.reshape(KT, P, 32).transpose(1, 0, 2)
    for name in ("norm_mix", "conv_dw_b", "conv_ln_g", "conv_ln_b", "ssd_conv_b", "ssd_norm_g", "norm_xattn", "norm_mem",
                 "norm_mlp"):
        t["late_" + name] = columns(I[name])
    t["late_gate_bias"] = columns(I["gate_bias"].reshape(-1))
    t["late_conv_dw_w"] = columns(I["conv_dw_w"]).transpose(0, 2, 1)
    t["late_ssd_conv_w"] = columns(I["ssd_conv_w"]).transpose(0, 2, 1)
    t["late_ssd_dt_bias"] = rows(np.tile(I["ssd_dt_bias"], 2), 64)
    t["late_ssd_a_log"] = rows(np.tile(I["ssd_A_log"], 2), 64)
    t["late_ssd_d"] = columns(np.repeat(I["ssd_D"], 64))
    t["late_attn_gains"] = np.stack([np.tile(I[n], 2) for n in ("attn_q_norm", "attn_k_norm")], 1)
    t["late_attn_sinks"] = rows(I["attn_sinks"][Q_HEADS], 16)
    t["late_rel_table"] = I["rel_table"][:, Q_HEADS]
    t["late_xattn_gains"] = np.concatenate([columns(I["xattn_q_norm"]), columns(I["xattn_k_norm"])], 1)
    t["late_mem"] = feature_major(I["mem"][0])
    t["late_eps_xattn"] = np.full((P, 1), EPS * 256, np.float32)



def build(nc, dram, out, steps, counted):
    with ExitStack() as ctx:
        k = Kit(nc, ctx, dram, steps, counted)
        X, H = k.X, k.H
        number = count()
        new_in = lambda c: lambda name, *shape: c.enter_context(nc.sbuf_tensor(f"{name}_{next(number)}", [P, *shape], F32))
        new = new_in(ctx)
        w = dram
        scale, gate, mod = new("scale", 2, 3, 16), new("gate", 2, 3, 16), new("mod", 288)
        col = lambda t, l, n: lambda d, c: t[:, l, n, bass.ds(d * 2 + c, 1)]
        shift = lambda l, n: lambda d, c: mod[:, bass.ds(((l * 9 + n * 3) * KT + d) * 2 + c, 1)]
        ffn1, ffn2 = w["w_ffn1"], w["w_ffn2"]
        mlp1 = lambda l, n: ffn1[(l * 2 + n) * FT:(l * 2 + n + 1) * FT]
        mlp2 = lambda l, n: ffn2[(l * 2 + n) * KT:(l * 2 + n + 1) * KT]

        def modulated(l, n, squares, first=0):
            parts = [(a - first, b - first, (lambda c: lambda d: col(scale, l, n)(d, c))(c),
                      (lambda c: lambda d: shift(l, n)(d, c))(c))
                     for c, (a, b) in enumerate(((0, CTX), (CTX, TOK))) if b > first]
            norm(k, f"norm {l} {n}", lambda d: X[:, d, first:TOK], lambda d: H[:, d, first:TOK], TOK - first, parts, squares)

        def mlp(l, n, first, ahead):
            with ExitStack() as c:
                local = new_in(c)
                hidden, silus = local("hidden", FT, TOK), local("silus", 2, TOK)
                modulated(l, 2 * n, hidden, first)
                gated_mlp(k, f"mlp {l} {n}", mlp1(l, n), mlp2(l, n), first, col(gate, l, 2 * n), hidden, silus, ahead)

        start(k, w["w_ada"])
        modulation(k, mod, gate, scale, mlp1(0, 0))
        mlp(0, 0, 0, w["w_dn_qkv"])
        with ExitStack() as c:
            local = new_in(c)
            qkv, z = local("qkv", 24, TOK), local("z", KT, TOK)
            modulated(0, 1, z)
            with ExitStack() as cc:
                taps = k.C["dn_conv"]
                conv_silu(k, "delta qkv", w["w_dn_qkv"], lambda d: H[:, d, :], 2, CTX, taps, taps.shape[2] // 2, None, qkv,
                          new_in(cc)("convs", 4, TOK), w["w_dn_z"])
            g, beta, gc, eg_neg, ekd, ea = (local(f"gates{n}", 8, 8) for n in range(6))
            tmp = local("gates_tmp", 4, 8, 8)
            delta_gates(k, z, g, beta, gc, eg_neg, ekd, ea, tmp, w["w_dn_out"])
            with ExitStack() as cc:
                delta_heads(k, new_in(cc), qkv, z, g, beta, gc, eg_neg, ekd, ea)
            to_residual(k, "delta out", w["w_dn_out"], lambda d: qkv[:, d, :], TOK,
                        lambda dve, n, at, i: gated_residual(k, dve, n, at, 0, col(gate, 0, 1)), mlp1(0, 1))
        mlp(0, 1, 0, mlp1(1, 0))
        mlp(1, 0, 0, w["w_swa_q"])
        swa(k, new_in, modulated, col(gate, 1, 1), mlp1(1, 1))
        mlp(1, 1, CTX, w["w_conv"])
        second(k, new_in, w)
        return finish(k, out)


def finish(k, out):
    with k.open("finish") as block:
        @block.sync
        def _(sp):
            sp.dma_start(out, k.X[:, :, CTX:TOK]).then_inc(k.stored, 16)
            sp.wait_ge(k.stored, k.stores + 16)


def shape_constants():
    import numpy as np
    f = np.float32
    j, i = np.arange(P)[:, None], np.arange(P)[None, :]
    ahead = [j <= i, j >= i]
    level = []
    for d in range(2):
        for s in range(LEVELS):
            b = 1 << s
            late, early = (i, j) if d == 0 else (j, i)
            level.append((i // (2 * b) == j // (2 * b)) & (late // b % 2 == 1) & (early // b % 2 == 0))
    c = {
        "ident": np.eye(P, dtype=f),
        "ones": np.ones((P, P), f),
        "until": np.stack([a.astype(f) for a in ahead], 1),
        "behind": np.stack([np.where(a, f(0), f(-1e30)) for a in ahead], 1),
        "level": np.stack([a.astype(f) for a in level], 1),
    }
    half = 64
    c["late_ones64"] = (j // half == i // half).astype(f)
    rot = np.zeros((P, P), f)
    for m in range(P):
        rot[(m + 32, m) if m % half < 32 else (m - 32, m)] = -1 if m % half < 32 else 1
    c["late_rot"] = rot
    t = np.arange(LAT)
    inv = (f(10000.0) ** (-np.arange(16, dtype=f) / f(16))).astype(f)
    ang = np.concatenate([(t // 64).astype(f)[:, None] * inv, (t % 64).astype(f)[:, None] * inv], 1)
    cos, sin = (np.tile(fn(ang).astype(f).T, (4, 1)) for fn in (np.cos, np.sin))
    c["late_cos"] = np.concatenate([np.ones((P, CTX), f), cos], 1)
    c["late_sin"] = np.concatenate([np.zeros((P, CTX), f), sin], 1)
    q, key = np.arange(P)[:, None], np.arange(LAT)[None, :]
    window = [np.where(np.abs(q + P * b - key) <= 128, f(0), f(-1e30)) for b in range(2)]
    c["late_window"] = np.stack([np.concatenate([np.zeros((P, CTX), f), m], 1) for m in window], 1)
    dist = q + P - key
    c["late_band"] = np.where((dist >= 0) & (dist < 128), f(0), f(-1e30))
    x = np.arange(384)
    dist = 255 - x
    large = 16 + (np.log(np.maximum(dist, 1).astype(f) / f(16)) / f(np.log(128 / 16)) * f(16)).astype(np.int32)
    bucket = np.where(dist < 16, np.maximum(dist, 0), np.minimum(large, 31))
    c["late_bucket"] = (np.arange(32)[:, None] == bucket[None, :]).astype(f)
    return {n if n.startswith("late_") else "c_" + n: np.ascontiguousarray(a, dtype=f) for n, a in c.items()}


def pack(w, group):
    depth, n = w.shape[0] // P, w.shape[1] // P // group
    return w.reshape(depth, P, n, group, P).transpose(2, 1, 3, 0, 4).reshape(n, P, group * depth * P)


def columns(a):
    import numpy as np
    a = a.reshape(*a.shape[:-1], a.shape[-1] // P, P)
    return np.moveaxis(a, -1, 0)


def feature_major(a):
    return a.T.reshape(a.shape[1] // P, P, a.shape[0]).transpose(1, 0, 2)


def rows(a, *shape):
    import numpy as np
    return np.broadcast_to(a.reshape(shape), (P, *shape))


def layout(I):
    import numpy as np
    t = {}
    two = lambda a: np.stack([a, a], -1)
    t["w_ada"] = np.concatenate([I["ada_w"][l].reshape(KT, P, 18, 512).transpose(2, 1, 0, 3).reshape(18, P, KT * 512)
                                 for l in range(2)])
    t["w_ffn1"] = np.concatenate([
        pack(I["ffn_w1"][l, n].reshape(D, 2, FT, P).transpose(0, 2, 1, 3).reshape(D, 2 * FFN), 2)
        for l in range(2) for n in range(2)])
    t["w_ffn2"] = np.concatenate([pack(I["ffn_w2"][l, n], 1) for l in range(2) for n in range(2)])
    dn = I["dn_w_in"][0]
    t["w_dn_qkv"], t["w_dn_z"] = pack(dn[:, :3072], 4), pack(dn[:, 3072:4096], 4)
    t["c_w_dn_ab"] = dn[:, 4096:].reshape(KT, P, 32).transpose(1, 0, 2)
    t["w_dn_out"] = pack(I["dn_w_out"][0], 4)
    t["c_cond"] = columns(np.stack([I["c_ctx"], I["c"][0]])).transpose(0, 2, 1)
    t["c_ada_b"] = two(columns(I["ada_b"])).reshape(P, 288)
    t["c_norm_g"] = two(columns(I["norm_g"])).reshape(P, 2, 3, 16)
    t["c_dn_conv"] = columns(I["dn_conv"][0]).transpose(0, 2, 1)
    t["c_dn_dt_bias"] = rows(np.tile(I["dn_dt_bias"][0], (4, 1)), 8, 8)
    t["c_dn_a_log"] = rows(np.tile(I["dn_a_log"][0], (4, 1)), 8, 8)
    t["c_dn_o_gain"] = I["dn_o_gain"][0].reshape(P, 1)
    t["tokens"] = feature_major(np.concatenate([I["ctx"][0], I["x"][0]]))
    layout_swa(I, t)
    layout_second(I, t)
    t = {n: np.ascontiguousarray(a) for n, a in t.items()}
    t.update(shape_constants())
    return t


def kernel(**inputs):
    import numpy as np
    import concourse.bacc as bacc
    from concourse.bass_utils import run_bass_kernel_spmd

    arrays = layout({n: np.asarray(a) for n, a in inputs.items()})
    steps = {}
    for counted in (False, True):
        nc = bacc.Bacc("TRN2", target_bir_lowering=False, num_devices=1)
        dram = {n: nc.dram_tensor(n, list(a.shape), F32, kind="ExternalInput").ap() for n, a in arrays.items()}
        out = nc.dram_tensor("out", [P, KT, LAT], F32, kind="ExternalOutput").ap()
        build(nc, dram, out, steps, counted)
    got = run_bass_kernel_spmd(nc, [arrays], core_ids=[0]).results[0]["out"]
    return got.transpose(2, 1, 0).reshape(1, LAT, D)
```

```python
from contextlib import ExitStack, contextmanager
from itertools import count

import concourse.bass as bass
from concourse import mybir

F32 = mybir.dt.float32
F32R = mybir.dt.float32r
ACT = mybir.ActivationFunctionType
ALU = mybir.AluOpType
AX_X = mybir.AxisListType.X

P = 128
D = 1024
KT = D // P
CTX, LAT = 256, 256
TOK = CTX + LAT
FFN = 2816
FT = FFN // P
EPS = 1e-6
BANK = 512
SEED = 2000


class Progress:

    def __init__(self, sem, steps, stage):
        self.sem, self.steps, self.stage = sem, steps, stage
        self.count, self.open = SEED, None

    def mark(self, name):
        self.count += 1
        key = (self.stage[0], name)
        assert self.steps.get(key, (self.count, 0))[0] == self.count, f"two steps are called {key}"
        self.steps.setdefault(key, (self.count, 0))
        if self.open is not None:
            self.open.append(key)
        return self.sem, 1

    def after(self, name, i=None, stage=None):
        key = (stage or self.stage[0], name)
        if key not in self.steps:
            assert not self.stage[1], f"nothing makes {key}"
            return self.sem, 1
        first, per_turn = self.steps[key]
        return self.sem, first if i is None or not per_turn else (first - per_turn) + (i + 1) * per_turn

    @contextmanager
    def turns(self, engine, times):
        start, self.open = self.count, []
        if times == 1:
            yield 0
        else:
            with engine.Fori(0, times) as i:
                yield i
        per_turn = self.count - start
        for key in self.open:
            self.steps[key] = (self.steps[key][0], per_turn)
        self.open, self.count = None, start + per_turn * times


def row(t, i):
    return t[:, bass.ds(i, 1), :].rearrange("p a n -> p (a n)")


class Kit:

    def __init__(self, nc, ctx, dram, steps, counted):
        self.nc, self.ctx, self.dram = nc, ctx, dram
        self.stage = ["start", counted]
        sem = lambda name: ctx.enter_context(nc.semaphore(name))
        self.PE, self.AC, self.DV, self.PO = (
            Progress(sem(name), steps.setdefault(name, {}), self.stage)
            for name in ("pe_done", "act_done", "dve_done", "pool_done"))
        self.landed = [sem("weights_landed_0"), sem("weights_landed_1")]
        self.landings = [0, 0]
        self.consts_landed = sem("consts_landed")
        self.stored = sem("stored")
        self.stores = 0
        f = lambda name, *shape: ctx.enter_context(nc.sbuf_tensor(name, [P, *shape], F32))
        self.W = f("weights_landing", 2, 2048)
        self.X = f("residual", KT, TOK)
        self.R = f("norm_r", 2, BANK)
        self.EPSC = f("eps", 1)
        self.banks = [ctx.enter_context(nc.psum_tensor(f"bank{b}", [P, BANK], F32)) for b in range(8)]
        self.ACC, self.AUX = self.banks[:4], self.banks[4:]
        self.C = {}
        for name, a in dram.items():
            if name.startswith("c_"):
                self.C[name[2:]] = ctx.enter_context(nc.sbuf_tensor("k" + name, list(a.shape), F32))

    def open(self, name):
        self.stage[0] = name
        return self.nc.Block()



HALF = 1024
HALVES = ((" first half", slice(0, HALF)), ("", slice(HALF, 2 * HALF)))


class Layer:

    def __init__(self, w, ahead, group=2, parts=1, split=False, fresh=False):
        self.w, self.ahead, self.group, self.parts = w, ahead, group, parts
        self.split, self.fresh = split or fresh, fresh
        self.units, self.width = w.shape[0], w.shape[2]
        self.per_unit = self.width // P // group
        self.body = 4 * parts // group
        self.turns = self.units // self.body

    def made(self, s):
        if self.parts > 1:
            return [s // self.parts] if s % self.parts == self.parts - 1 else []
        return list(range(s * self.group, (s + 1) * self.group))

    def last(self, s):
        return ("acc", self.made(s)[-1]) if self.made(s) else ("part", s)


def load_unit(k, sp, weights, u, slot):
    n = weights.shape[2]
    sp.dma_start(k.W[:, slot, 0:n], weights[bass.ds(u, 1)].rearrange("a p n -> (a p) n")).then_inc(k.landed[slot], 16)


def stream(k, sp, w, ahead, body, read):
    units = w.shape[0]
    turns = units // body
    if turns > 1:
        with sp.Fori(0, turns - 1) as i:
            for s in range(body):
                sp.wait_ge(*read(s, i))
                load_unit(k, sp, w, i * body + s + 2, s % 2)
    for s in range(body if ahead is not None else body - 2):
        sp.wait_ge(*read(s, turns - 1))
        u = (turns - 1) * body + s + 2
        if u < units:
            load_unit(k, sp, w, u, s % 2)
        else:
            load_unit(k, sp, ahead, u - units, s % 2)


def feed(k, block, L):
    nc = k.nc
    if not L.split:
        @block.sync
        def _(sp):
            stream(k, sp, L.w, L.ahead, L.body, lambda s, i: k.PE.after(L.last(s), i))
        return

    @block.sync
    def _(sp):
        if L.fresh:
            sp.wait_ge(*k.PO.after("wl first"))
        stream(k, sp, L.w, L.ahead, L.body,
               lambda s, i: k.PO.after(("wl", s), i) if s else k.PO.after(("wl", L.body), i - 1))

    @block.gpsimd
    def _(pool):
        if L.fresh:
            pool.wait_ge(*k.AC.after("wh first"))
            nc.gpsimd.tensor_tensor(k.WL[:, 0, :], k.W[:, 0, :], k.WH[:, 0, :].bitcast(F32),
                                    ALU.subtract).then_inc(*k.PO.mark("wl first"))
        with k.PO.turns(pool, L.turns) as i:
            for s in range(1, L.body + 1):
                for half, at in HALVES:
                    pool.wait_ge(*k.AC.after(("wh" + half, s), i))
                    nc.gpsimd.tensor_tensor(k.WL[:, s % 2, at], k.W[:, s % 2, at], k.WH[:, s % 2, at].bitcast(F32),
                                            ALU.subtract).then_inc(*k.PO.mark(("wl" + half, s)))


def split_hi(k, act, L, s, i):
    n = s + 1
    act.wait_ge(k.landed[n % 2], k.landings[n % 2] + 16 * (n // 2 + 1) + i * (8 * L.body))
    act.wait_ge(*(k.PE.after(L.last(s - 1), i) if s else k.PE.after(L.last(L.body - 1), i - 1)))
    for half, at in HALVES:
        k.nc.scalar.activation(k.WH[:, n % 2, at], k.W[:, n % 2, at], ACT.Copy).then_inc(*k.AC.mark(("wh" + half, n)))


def scalar_loop(k, act, L, evict=None, first=None):
    if L.fresh:
        act.wait_ge(k.landed[0], k.landings[0] + 16)
        k.nc.scalar.activation(k.WH[:, 0, :], k.W[:, 0, :], ACT.Copy).then_inc(*k.AC.mark("wh first"))
    with k.AC.turns(act, L.turns) as i:
        for s in range(L.body):
            if L.split:
                split_hi(k, act, L, s, i)
            for n in L.made(s):
                if evict is not None:
                    evict(n, i)


def close_stream(k, units):
    for s in range(2):
        k.landings[s] += 16 * (units // 2)


def three(nc, out, lhs, rhs, start, stop):
    (lh, ll), (rh, rl) = lhs, rhs
    nc.tensor.matmul(out, ll, rh, start=start, stop=False)
    nc.tensor.matmul(out, lh, rl, start=False, stop=False)
    return nc.tensor.matmul(out, lh, rh, start=False, stop=stop)


def parts_at(k, slot, at, n=P):
    return k.WH[:, slot, at:at + n], k.WL[:, slot, at:at + n]


def low_part(k, L, s, i, half):
    return k.PO.after(("wl" + half, s), i) if s else k.PO.after(("wl" + half, L.body), i - 1)


def unit_here(k, pe, L, s, i):
    if not L.split:
        pe.wait_ge(k.landed[s % 2], k.landings[s % 2] + 16 * (s // 2 + 1) + i * (8 * L.body))
        return
    pe.wait_ge(*low_part(k, L, s, i, " first half"))


def linear(k, pe, L, rhs, tokens, evictor):
    if L.fresh:
        pe.wait_ge(*k.PO.after("wl first"))
    with k.PE.turns(pe, L.turns) as i:
        for s in range(L.body):
            unit_here(k, pe, L, s, i)
            half = s % L.parts
            tiles = L.made(s) or [s // L.parts]
            for m, n in enumerate(tiles):
                if half == 0:
                    pe.wait_ge(*evictor(n).after(("ev", n), i - 1))
                for d in range(L.per_unit):
                    at, x, out = (m * L.per_unit + d) * P, rhs(half * L.per_unit + d), k.ACC[n][:, 0:tokens]
                    start, stop = half == 0 and d == 0, half == L.parts - 1 and d == L.per_unit - 1
                    if L.split:
                        if at == HALF:
                            pe.wait_ge(*low_part(k, L, s, i, ""))
                        mm = three(k.nc, out, parts_at(k, s % 2, at), x, start, stop)
                    else:
                        mm = k.nc.tensor.matmul(out, k.W[:, s % 2, at:at + P], x, start=start, stop=stop)
                mm.then_inc(*k.PE.mark(("acc", n) if L.made(s) else ("part", s)))



def norm(k, name, src, dst, tokens, parts, squares):
    nc = k.nc
    with k.open(name) as block:
        @block.scalar
        def _(act):
            for d in range(KT):
                nc.scalar.activation(squares[:, d, 0:tokens], src(d), ACT.Square).then_inc(*k.AC.mark(("sq", d)))
            act.wait_ge(*k.PE.after("sum"))
            nc.scalar.activation(k.R[:, 0, 0:tokens], k.AUX[0][:, 0:tokens], ACT.Sqrt, scale=1.0 / D,
                                 bias=k.EPSC[:]).then_inc(*k.AC.mark("rms"))
            for d in range(KT):
                act.wait_ge(*k.DV.after(("x", d)))
                for n, (a, b, scale, shift) in enumerate(parts):
                    nc.scalar.activation(dst(d)[:, a:b], dst(d)[:, a:b], ACT.Identity, scale=scale(d),
                                         bias=shift(d) if shift else 0.0).then_inc(*k.AC.mark(("out", d, n)))

        @block.tensor
        def _(pe):
            for d in range(KT):
                pe.wait_ge(*k.AC.after(("sq", d)))
                mm = nc.tensor.matmul(k.AUX[0][:, 0:tokens], k.C["ones"][:], squares[:, d, 0:tokens],
                                      start=d == 0, stop=d == KT - 1)
            mm.then_inc(*k.PE.mark("sum"))

        @block.vector
        def _(dve):
            dve.wait_ge(*k.AC.after("rms"))
            nc.vector.reciprocal(k.R[:, 1, 0:tokens], k.R[:, 0, 0:tokens]).then_inc(*k.DV.mark("r"))
            dve.wait_ge(*k.DV.after("r"))
            for d in range(KT):
                nc.vector.tensor_tensor(dst(d), src(d), k.R[:, 1, 0:tokens], ALU.mult).then_inc(*k.DV.mark(("x", d)))


def norm_split(k, name, src, hi, lo, tokens, parts, work):
    nc = k.nc
    with k.open(name) as block:
        @block.scalar
        def _(act):
            for d in range(KT):
                nc.scalar.activation(work[:, d, 0:tokens], src(d), ACT.Square).then_inc(*k.AC.mark(("sq", d)))
            act.wait_ge(*k.PE.after("sum"))
            nc.scalar.activation(k.R[:, 0, 0:tokens], k.AUX[0][:, 0:tokens], ACT.Sqrt, scale=1.0 / D,
                                 bias=k.EPSC[:]).then_inc(*k.AC.mark("rms"))
            for d in range(KT):
                act.wait_ge(*k.DV.after(("x", d)))
                for n, (a, b, scale, shift) in enumerate(parts):
                    nc.scalar.activation(hi(d)[:, a:b], work[:, d, a:b], ACT.Identity, scale=scale(d),
                                         bias=shift(d) if shift else 0.0).then_inc(*k.AC.mark(("hi", d, n)))

        @block.tensor
        def _(pe):
            for d in range(KT):
                pe.wait_ge(*k.AC.after(("sq", d)))
                mm = nc.tensor.matmul(k.AUX[0][:, 0:tokens], k.C["ones"][:], work[:, d, 0:tokens],
                                      start=d == 0, stop=d == KT - 1)
            mm.then_inc(*k.PE.mark("sum"))

        @block.vector
        def _(dve):
            dve.wait_ge(*k.AC.after("rms"))
            nc.vector.reciprocal(k.R[:, 1, 0:tokens], k.R[:, 0, 0:tokens]).then_inc(*k.DV.mark("r"))
            dve.wait_ge(*k.DV.after("r"))
            for d in range(KT):
                nc.vector.tensor_tensor(work[:, d, 0:tokens], src(d), k.R[:, 1, 0:tokens], ALU.mult).then_inc(*k.DV.mark(("x", d)))
            for d in range(KT):
                dve.wait_ge(*k.AC.after(("hi", d, len(parts) - 1)))
                for n, (a, b, scale, shift) in enumerate(parts):
                    nc.vector.tensor_scalar(work[:, d, a:b], work[:, d, a:b], scale(d), shift(d) if shift else None, ALU.mult,
                                            *((ALU.add,) if shift else ())).then_inc(*k.DV.mark(("scaled", d, n)))
                dve.wait_ge(*k.DV.after(("scaled", d, len(parts) - 1)))
                nc.vector.tensor_tensor(lo(d), work[:, d, 0:tokens], hi(d).bitcast(F32), ALU.subtract).then_inc(*k.DV.mark(("lo", d)))



def start(k, ahead):
    nc = k.nc
    with k.open("start") as block:
        @block.sync
        def _(sp):
            n = 0
            for name, t in k.C.items():
                sp.dma_start(t[:], k.dram["c_" + name]).then_inc(k.consts_landed, 16)
                n += 16
            sp.dma_start(k.X[:], k.dram["tokens"]).then_inc(k.consts_landed, 16)
            for s in range(2):
                load_unit(k, sp, ahead, s, s)
            sp.wait_ge(k.consts_landed, n + 16)

        @block.tensor
        def _(pe):
            nc.tensor.nop().then_inc(k.PE.sem, SEED)

        @block.scalar
        def _(act):
            nc.scalar.nop().then_inc(k.AC.sem, SEED)

        @block.vector
        def _(dve):
            nc.vector.memset(k.EPSC[:], EPS).then_inc(k.DV.sem, SEED)

        @block.gpsimd
        def _(pool):
            nc.gpsimd.nop().then_inc(k.PO.sem, SEED)


def modulation(k, mod, gate, scale, pieces, ahead):
    nc, w = k.nc, k.dram["w_ada"]
    units, body = w.shape[0], 4
    cond = k.C["cond"]
    with k.open("modulation") as block:
        @block.sync
        def _(sp):
            stream(k, sp, w, ahead, body, lambda s, i: k.PE.after(("acc", s), i))

        @block.scalar
        def _(act):
            nc.scalar.activation(cond[:], cond[:], ACT.Silu).then_inc(*k.AC.mark("silu"))
            with k.AC.turns(act, units // body) as i:
                for s in range(body):
                    act.wait_ge(*k.PE.after(("acc", s), i))
                    nc.scalar.activation(pieces[0:2, s, :], k.ACC[s][0:2, 0:256], ACT.Copy).then_inc(*k.AC.mark(("ev", s)))

        @block.tensor
        def _(pe):
            pe.wait_ge(*k.AC.after("silu"))

            def turn(s, i):
                pe.wait_ge(*k.AC.after(("ev", s), i))
                pe.wait_ge(*k.DV.after(("mod", s), i - 1))
                for m in range(2):
                    mm = nc.tensor.matmul(k.AUX[s][:, 2 * m:2 * m + 2], pieces[0:2, s, m * P:(m + 1) * P],
                                          k.C["ident"][0:2, 0:2], start=True, stop=True)
                mm.then_inc(*k.PE.mark(("turned", s)))

            with k.PE.turns(pe, units // body) as i:
                for s in range(body):
                    pe.wait_ge(k.landed[s % 2], k.landings[s % 2] + 16 * (s // 2 + 1) + i * (8 * body))
                    pe.wait_ge(*k.AC.after(("ev", s), i - 1))
                    for d in range(KT):
                        mm = nc.tensor.matmul(k.ACC[s][0:2, 0:256], cond[:, d, :], k.W[:, s % 2, d * 256:(d + 1) * 256],
                                              start=d == 0, stop=d == KT - 1)
                    mm.then_inc(*k.PE.mark(("acc", s)))
                    if s:
                        turn(s - 1, i)
                turn(body - 1, i)

        @block.vector
        def _(dve):
            with k.DV.turns(dve, units // body) as i:
                for s in range(body):
                    dve.wait_ge(*k.PE.after(("turned", s), i))
                    at = bass.ds((i * body + s) * 4, 4)
                    nc.vector.tensor_tensor(mod[:, at], k.AUX[s][:, 0:4], k.C["ada_b"][:, at],
                                            ALU.add).then_inc(*k.DV.mark(("mod", s)))
            dve.wait_ge(*k.DV.after(("mod", body - 1), units // body - 1))
            m = mod[:].rearrange("p (l i j f) -> p l i j f", l=2, i=3, j=3)
            for l in range(2):
                for n in range(3):
                    nc.vector.scalar_tensor_tensor(scale[:, l, n, :], m[:, l, n, 1, :], 1.0, k.C["norm_g"][:, l, n, :],
                                                   ALU.add, ALU.mult).then_inc(*k.DV.mark(("scale", l, n)))
                    nc.vector.tensor_scalar(gate[:, l, n, :], m[:, l, n, 2, :], 1.0 if n == 1 else 0.5, None,
                                            ALU.mult).then_inc(*k.DV.mark(("gate", l, n)))
    close_stream(k, units)


def gated_residual(k, dve, n, at, first, gate):
    for c, (a, b) in enumerate(((0, CTX), (CTX, TOK))):
        if b <= first:
            continue
        x = row(k.X, at)[:, a:b]
        ins = k.nc.vector.scalar_tensor_tensor(x, k.ACC[n][:, a - first:b - first], gate(at, c), x, ALU.mult, ALU.add)
        ins.then_inc(*k.DV.mark(("ev", n) if c == 1 else ("ev ctx", n)))


def gated_mlp(k, name, up, down, first, gate, hid, silus, raw):
    nc, tokens = k.nc, TOK - first
    hi, lo = hid
    cut = lambda t: t[:, 0:tokens]
    with k.open(name + " up") as block:
        feed(k, block, up)

        @block.tensor
        def _(pe):
            linear(k, pe, up, lambda d: (k.HH[:, d, first:TOK], k.HL[:, d, first:TOK]), tokens,
                   lambda n: k.DV if n % 2 else k.AC)

        @block.scalar
        def _(act):
            def evict(n, i):
                if n % 2:
                    return
                s = n // 2
                act.wait_ge(*k.PE.after(("acc", n), i))
                act.wait_ge(*k.DV.after(("ev", n + 1), i - 1))
                nc.scalar.activation(cut(silus[:, s, :]), cut(k.ACC[n]), ACT.Silu).then_inc(*k.AC.mark(("ev", n)))
                act.wait_ge(*k.DV.after(("ev", n + 1), i))
                nc.scalar.activation(cut(row(hi, i * 2 + s)), cut(raw[:, s, :]), ACT.Copy).then_inc(*k.AC.mark(("hi", s)))
            scalar_loop(k, act, up, evict)

        @block.vector
        def _(dve):
            with k.DV.turns(dve, FT // 2) as i:
                for s in range(2):
                    dve.wait_ge(*k.PE.after(("acc", 2 * s + 1), i))
                    dve.wait_ge(*k.AC.after(("ev", 2 * s), i))
                    nc.vector.tensor_tensor(cut(raw[:, s, :]), cut(silus[:, s, :]), cut(k.ACC[2 * s + 1]),
                                            ALU.mult).then_inc(*k.DV.mark(("ev", 2 * s + 1)))
                    dve.wait_ge(*k.AC.after(("hi", s), i))
                    nc.vector.tensor_tensor(cut(row(lo, i * 2 + s)), cut(raw[:, s, :]), cut(row(hi, i * 2 + s)).bitcast(F32),
                                            ALU.subtract).then_inc(*k.DV.mark(("lo", s)))
    close_stream(k, up.units)
    to_residual(k, name + " down", down, lambda d: (cut(hi[:, d, :]), cut(lo[:, d, :])), tokens,
                lambda dve, n, at, i: gated_residual(k, dve, n, at, first, gate))


def to_residual(k, name, L, src, tokens, write, split=None):
    nc = k.nc
    with k.open(name) as block:
        feed(k, block, L)

        @block.tensor
        def _(pe):
            if split is not None:
                pe.wait_ge(*k.DV.after(("src lo", len(split[0]) - 1)))
            linear(k, pe, L, src, tokens, lambda n: k.DV)

        @block.scalar
        def _(act):
            if split is not None:
                for d, (x, (hi, lo)) in enumerate(zip(*split)):
                    nc.scalar.activation(hi, x, ACT.Copy).then_inc(*k.AC.mark(("src hi", d)))
            scalar_loop(k, act, L)

        @block.vector
        def _(dve):
            if split is not None:
                for d, (x, (hi, lo)) in enumerate(zip(*split)):
                    dve.wait_ge(*k.AC.after(("src hi", d)))
                    nc.vector.tensor_tensor(lo, x, hi.bitcast(F32), ALU.subtract).then_inc(*k.DV.mark(("src lo", d)))
            with k.DV.turns(dve, L.turns) as i:
                for n in range(4):
                    dve.wait_ge(*k.PE.after(("acc", n), i))
                    write(dve, n, i * 4 + n, i)
    close_stream(k, L.units)



DN_HEADS = D // P
CHUNKS = TOK // P
LEVELS = 7
ORDER = ((0, 1, 2, 3), (1, 0, 3, 2))


def conv_silu(k, name, L, src, seqs, length, taps, mid, bias, out, convs):
    nc = k.nc
    width, tokens = taps.shape[2], seqs * length
    with k.open(name) as block:
        feed(k, block, L)

        @block.tensor
        def _(pe):
            linear(k, pe, L, src, tokens, lambda n: k.DV)

        @block.vector
        def _(dve):
            with k.DV.turns(dve, L.turns) as i:
                for n in range(4):
                    x = k.ACC[n][:, 0:tokens].rearrange("p (s t) -> p s t", s=seqs)
                    y = convs[:, n, 0:tokens].rearrange("p (s t) -> p s t", s=seqs)
                    tap = lambda j: taps[:, bass.ds(i * 4 + n, 1), j:j + 1].rearrange("p a b -> p (a b)")
                    dve.wait_ge(*k.PE.after(("acc", n), i))
                    dve.wait_ge(*k.AC.after(("silu", n), i - 1))
                    nc.vector.tensor_scalar(y, x, tap(mid), None, ALU.mult).then_inc(*k.DV.mark(("tap", n, mid)))
                    last = ("tap", n, mid)
                    others = [j for j in range(width) if j != mid]
                    for j in others:
                        shift = j - mid
                        a, b = max(0, -shift), length - max(0, shift)
                        dve.wait_ge(*k.DV.after(last, i))
                        last = ("ev", n) if j == others[-1] else ("tap", n, j)
                        nc.vector.scalar_tensor_tensor(y[:, :, a:b], x[:, :, a + shift:b + shift], tap(j),
                                                       y[:, :, a:b], ALU.mult, ALU.add).then_inc(*k.DV.mark(last))

        @block.scalar
        def _(act):
            def silu(n, i):
                act.wait_ge(*k.DV.after(("ev", n), i))
                nc.scalar.activation(row(out, i * 4 + n), convs[:, n, 0:tokens], ACT.Silu,
                                     bias=bias[:, bass.ds(i * 4 + n, 1)] if bias is not None else 0.0
                                     ).then_inc(*k.AC.mark(("silu", n)))
            scalar_loop(k, act, L, silu)
    close_stream(k, L.units)


def delta_gates(k, L, z, ab_parts, g, beta, gc, eg_neg, ekd, ea, tmp):
    nc = k.nc
    ab = k.AUX[0][:, 0:CHUNKS * 32].rearrange("p (x w h) -> p x w h", w=2, h=8)
    per_dir = lambda t, d: t[:].rearrange("p (c d) h -> p c d h", d=2)[:, :, d, :]
    sums, totals = k.AUX[1][:, 0:64], k.AUX[1][:, 64:128]
    flat = lambda t: t[:].rearrange("p a b -> p (a b)")
    with k.open("delta gates") as block:
        feed(k, block, L)

        @block.tensor
        def _(pe):
            pe.wait_ge(*k.DV.after("w lo"))
            for c in range(CHUNKS):
                at = slice(c * P, (c + 1) * P)
                for d in range(KT):
                    mm = three(nc, k.AUX[0][:, c * 32:c * 32 + 32], (k.HH[:, d, at], k.HL[:, d, at]),
                               [t[:, d, :] for t in ab_parts], d == 0, d == KT - 1)
            mm.then_inc(*k.PE.mark("ab"))
            linear(k, pe, L, lambda d: (k.HH[:, d, :], k.HL[:, d, :]), TOK, lambda n: k.AC)
            pe.wait_ge(*k.DV.after("g"))
            for d in range(2):
                nc.tensor.matmul(sums[:, d * 32:d * 32 + 32], k.C["until"][:, d, :], per_dir(g, d), start=True, stop=True)
                mm = nc.tensor.matmul(totals[:, d * 32:d * 32 + 32], k.C["ones"][:], per_dir(g, d), start=True, stop=True)
            mm.then_inc(*k.PE.mark("sums"))

        @block.vector
        def _(dve):
            dve.wait_ge(*k.AC.after("w hi"))
            nc.vector.tensor_tensor(ab_parts[1][:], k.C["w_dn_ab"][:], ab_parts[0][:].bitcast(F32),
                                    ALU.subtract).then_inc(*k.DV.mark("w lo"))
            dve.wait_ge(*k.PE.after("ab"))
            nc.vector.tensor_tensor(tmp[:, 0], ab[:, :, 0, :], k.C["dn_dt_bias"][:], ALU.add).then_inc(*k.DV.mark("x"))
            dve.wait_ge(*k.DV.after("x"))
            nc.vector.scalar_tensor_tensor(tmp[:, 1], tmp[:, 0], -1.0, tmp[:, 0], ALU.mult, ALU.max).then_inc(*k.DV.mark("|x|"))
            dve.wait_ge(*k.AC.after("ln"))
            nc.vector.scalar_tensor_tensor(tmp[:, 3], tmp[:, 0], 0.0, tmp[:, 2], ALU.max, ALU.add).then_inc(*k.DV.mark("softplus"))
            dve.wait_ge(*k.DV.after("softplus"))
            nc.vector.scalar_tensor_tensor(g[:], tmp[:, 3], -1.0, k.C["dn_a_log"][:], ALU.mult, ALU.mult).then_inc(*k.DV.mark("g"))
            dve.wait_ge(*k.PE.after("sums"))
            nc.vector.tensor_copy(flat(gc), sums).then_inc(*k.DV.mark("gc"))
            dve.wait_ge(*k.DV.after("gc"))
            nc.vector.tensor_tensor(flat(ekd), totals, flat(gc), ALU.subtract).then_inc(*k.DV.mark("to end"))
            dve.wait_ge(*k.AC.after("eg"))
            nc.vector.tensor_scalar(flat(eg_neg), flat(eg_neg), -1.0, None, ALU.mult).then_inc(*k.DV.mark("-eg"))

        @block.scalar
        def _(act):
            nc.scalar.activation(ab_parts[0][:], k.C["w_dn_ab"][:], ACT.Copy).then_inc(*k.AC.mark("w hi"))
            act.wait_ge(*k.DV.after("|x|"))
            nc.scalar.activation(k.C["dn_a_log"][:], k.C["dn_a_log"][:], ACT.Exp).then_inc(*k.AC.mark("a"))
            nc.scalar.activation(tmp[:, 2], tmp[:, 1], ACT.Exp, scale=-1.0).then_inc(*k.AC.mark("exp"))
            act.wait_ge(*k.AC.after("exp"))
            nc.scalar.activation(tmp[:, 2], tmp[:, 2], ACT.Ln, bias=1.0).then_inc(*k.AC.mark("ln"))
            nc.scalar.activation(beta[:], ab[:, :, 1, :], ACT.Sigmoid).then_inc(*k.AC.mark("beta"))

            def silu(n, i):
                act.wait_ge(*k.PE.after(("acc", n), i))
                nc.scalar.activation(row(z, i * 4 + n), k.ACC[n][:], ACT.Silu).then_inc(*k.AC.mark(("ev", n)))
            scalar_loop(k, act, L, silu)
            act.wait_ge(*k.DV.after("to end"))
            nc.scalar.activation(flat(eg_neg), sums, ACT.Exp).then_inc(*k.AC.mark("eg"))
            nc.scalar.activation(flat(ea), totals, ACT.Exp).then_inc(*k.AC.mark("ea"))
            nc.scalar.activation(flat(ekd), flat(ekd), ACT.Exp).then_inc(*k.AC.mark("ekd"))
    close_stream(k, L.units)


def delta_heads(k, new, qkv, z, g, beta, gc, eg_neg, ekd, ea):
    nc, B = k.nc, k.banks
    head, kh, qh, vh = new("dn_squares", 2, TOK), new("dn_k", TOK), new("dn_q", TOK), new("dn_v", TOK)
    ktok, vtok = new("dn_ktok", CHUNKS, P), new("dn_vtok", CHUNKS, P)
    pair = lambda name, *shape: [new(f"dn_{name}{d}", *(shape or (CHUNKS, P))) for d in range(2)]
    gu, dec, egb, kd, Y = (pair(n) for n in "gu dec egb kd y".split())
    at, qkt, qg, kbg = (pair(n) for n in "at qkt qg kbg".split())
    ps, wt, X = gu, dec, egb
    lm = [pair(f"lm{s}_") for s in range(2)]
    vnew, S = pair("vnew", P), pair("state", P)
    oh = new("dn_o", TOK)
    r = k.R
    C = k.C
    ck = lambda t, c: t[:, c * P:(c + 1) * P]
    tc = lambda t, c, d, i: t[:, c * 2 + d, bass.ds(i, 1)]
    td = lambda t, c, d, i: t[:, d * 4 + c, bass.ds(i, 1)]
    w4 = lambda t: t[:, :, :].rearrange("p c n -> p (c n)")
    wide = lambda m: m.unsqueeze(1).to_broadcast([P, CHUNKS, P])

    with k.open("delta heads") as block:
        @block.scalar
        def _(act):
            with k.AC.turns(act, DN_HEADS) as i:
                act.wait_ge(*k.PE.after("sum_o", i - 1))
                nc.scalar.activation(head[:, 0, :], row(qkv, i), ACT.Square).then_inc(*k.AC.mark("sq_q"))
                nc.scalar.activation(head[:, 1, :], row(qkv, i + 8), ACT.Square).then_inc(*k.AC.mark("sq_k"))
                nc.scalar.activation(vh[:], row(qkv, i + 16), ACT.Copy).then_inc(*k.AC.mark("vh"))
                act.wait_ge(*k.PE.after("sum_q", i))
                act.wait_ge(*k.DV.after("out", i - 1))
                nc.scalar.activation(r[:, 0, :], B[0][:], ACT.Sqrt, bias=k.EPSC[:]).then_inc(*k.AC.mark("norm_q"))
                act.wait_ge(*k.PE.after("sum_k", i))
                nc.scalar.activation(r[:, 1, :], B[1][:], ACT.Sqrt, bias=k.EPSC[:]).then_inc(*k.AC.mark("norm_k"))
                act.wait_ge(*k.PE.after("vT", i))
                nc.scalar.activation(w4(vtok), B[3][:], ACT.Copy).then_inc(*k.AC.mark("vtok"))
                act.wait_ge(*k.PE.after("kT", i))
                nc.scalar.activation(w4(ktok), B[2][:], ACT.Copy).then_inc(*k.AC.mark("ktok"))
                for d in range(2):
                    act.wait_ge(*k.PE.after(("gcb", d), i))
                    nc.scalar.activation(w4(egb[d]), B[6 + d][:], ACT.Exp).then_inc(*k.AC.mark(("egb", d)))
                    act.wait_ge(*k.DV.after(("dd", d, 3), i))
                    nc.scalar.activation(w4(dec[d]), w4(dec[d]), ACT.Exp).then_inc(*k.AC.mark(("dec", d)))
                for s in range(LEVELS):
                    for d in range(2 if s else 0):
                        act.wait_ge(*k.PE.after(("p", s, d), i))
                        nc.scalar.activation(w4(ps[d]), B[d][:], ACT.Copy).then_inc(*k.AC.mark(("ps", s, d)))
                    for d in range(2 if s < LEVELS - 1 else 0):
                        if s == 0:
                            act.wait_ge(*k.DV.after(("qg", d), i))
                        act.wait_ge(*k.PE.after(("yT", s, d), i))
                        nc.scalar.activation(w4(X[d]), B[2 + d][:], ACT.Copy).then_inc(*k.AC.mark(("x", s, d)))
                for d in range(2):
                    act.wait_ge(*k.PE.after(("wT", d), i))
                    nc.scalar.activation(w4(wt[d]), B[d][:], ACT.Copy).then_inc(*k.AC.mark(("wt", d)))
                act.wait_ge(*k.DV.after(("o", 3, 1), i))
                nc.scalar.activation(head[:, 0, :], oh[:], ACT.Square).then_inc(*k.AC.mark("sq_o"))
                act.wait_ge(*k.PE.after("sum_o", i))
                nc.scalar.activation(r[:, 0, :], B[0][:], ACT.Sqrt, scale=1.0 / P, bias=k.EPSC[:]).then_inc(*k.AC.mark("norm_o"))

        @block.tensor
        def _(pe):
            def four(bank, lhs, rhs, name):
                for c in range(CHUNKS):
                    mm = nc.tensor.matmul(ck(bank, c), lhs[:, c, :], rhs[:, c, :], start=True, stop=True)
                mm.then_inc(*k.PE.mark(name))

            with k.PE.turns(pe, DN_HEADS) as i:
                pe.wait_ge(*k.AC.after("sq_q", i))
                nc.tensor.matmul(B[0][:], C["ones"][:], head[:, 0, :], start=True, stop=True).then_inc(*k.PE.mark("sum_q"))
                pe.wait_ge(*k.AC.after("sq_k", i))
                nc.tensor.matmul(B[1][:], C["ones"][:], head[:, 1, :], start=True, stop=True).then_inc(*k.PE.mark("sum_k"))
                pe.wait_ge(*k.AC.after("vh", i))
                for c in range(CHUNKS):
                    mm = nc.tensor.transpose(ck(B[3], c), ck(vh, c), C["ident"][:])
                mm.then_inc(*k.PE.mark("vT"))
                for d in range(2):
                    pe.wait_ge(*k.DV.after(("gu", d, 3), i))
                    nc.tensor.matmul(B[6 + d][:], C["ones"][:], w4(gu[d]), start=True, stop=True).then_inc(*k.PE.mark(("gcb", d)))
                pe.wait_ge(*k.DV.after("kh", i))
                for c in range(CHUNKS):
                    mm = nc.tensor.transpose(ck(B[2], c), ck(kh, c), C["ident"][:])
                mm.then_inc(*k.PE.mark("kT"))
                for c in range(CHUNKS):
                    mm = nc.tensor.matmul(ck(B[4], c), ck(kh, c), ck(kh, c), start=True, stop=True)
                mm.then_inc(*k.PE.mark("kk"))
                for c in range(CHUNKS):
                    mm = nc.tensor.matmul(ck(B[5], c), ck(kh, c), ck(qh, c), start=True, stop=True)
                mm.then_inc(*k.PE.mark("kq"))
                for s in range(LEVELS):
                    for d in range(2 if s else 0):
                        pe.wait_ge(*k.PO.after(("lm", s, d), i))
                        pe.wait_ge(*k.AC.after(("x", s - 1, d), i))
                        four(B[d], lm[s % 2][d], X[d], ("p", s, d))
                    for d in range(2 if s else 0):
                        pe.wait_ge(*k.AC.after(("ps", s, d), i))
                        four(B[4 + d], ps[d], Y[d], ("dy", s, d))
                    for d in range(2 if s < LEVELS - 1 else 0):
                        if s:
                            pe.wait_ge(*k.DV.after(("y", s, d), i))
                        else:
                            pe.wait_ge(*k.PO.after(("y", d), i))
                            pe.wait_ge(*k.DV.after(("kd", 1, 3), i))
                        for c in range(CHUNKS):
                            mm = nc.tensor.transpose(ck(B[2 + d], c), Y[d][:, c, :], C["ident"][:])
                        mm.then_inc(*k.PE.mark(("yT", s, d)))
                for d in range(2):
                    pe.wait_ge(*k.DV.after(("y", LEVELS - 1, d), i))
                    four(B[d], kbg[d], Y[d], ("wT", d))
                for t in range(CHUNKS):
                    for d in range(2):
                        c = ORDER[d][t]
                        mm = nc.tensor.matmul(B[2 + d][:, 0:P], Y[d][:, c, :], vtok[:, c, :], start=True, stop=t == 0)
                        if t:
                            pe.wait_ge(*k.AC.after(("wt", d), i))
                            pe.wait_ge(*k.DV.after(("state", t - 1, d), i))
                            mm = nc.tensor.matmul(B[2 + d][:, 0:P], wt[d][:, c, :], S[d][:], start=False, stop=True)
                        mm.then_inc(*k.PE.mark(("vn", t, d)))
                    for d in range(2):
                        c = ORDER[d][t]
                        if t:
                            pe.wait_ge(*k.DV.after(("o", t - 1, d), i))
                            nc.tensor.matmul(B[4 + d][:, 0:P], S[d][:], qg[d][:, c, :], start=True, stop=False)
                        pe.wait_ge(*k.DV.after(("vnew", t, d), i))
                        nc.tensor.matmul(B[4 + d][:, 0:P], vnew[d][:], qkt[d][:, c, :], start=t == 0,
                                         stop=True).then_inc(*k.PE.mark(("o", t, d)))
                        if t < CHUNKS - 1:
                            nc.tensor.matmul(B[6 + d][:, 0:P], kd[d][:, c, :], vnew[d][:], start=True,
                                             stop=True).then_inc(*k.PE.mark(("ds", t, d)))
                pe.wait_ge(*k.AC.after("sq_o", i))
                nc.tensor.matmul(B[0][:], C["ones"][:], head[:, 0, :], start=True, stop=True).then_inc(*k.PE.mark("sum_o"))

        @block.gpsimd
        def _(pool):
            with k.PO.turns(pool, DN_HEADS) as i:
                for s in range(LEVELS):
                    for d in range(2):
                        pool.wait_ge(*k.DV.after(("at", d, 3), i))
                        if s >= 3:
                            pool.wait_ge(*k.PE.after(("p", s - 2, d), i))
                        if s == 2:
                            pool.wait_ge(*k.PO.after(("y", d), i))
                        nc.gpsimd.tensor_tensor(lm[s % 2][d][:], at[d][:], wide(C["level"][:, d * LEVELS + s, :]),
                                                ALU.mult).then_inc(*k.PO.mark(("lm", s, d)))
                    if s == 0:
                        for d in range(2):
                            pool.wait_ge(*k.PE.after(("vn", 3, d), i - 1))
                            pool.wait_ge(*k.PO.after(("lm", 0, d), i))
                            nc.gpsimd.tensor_tensor(Y[d][:], wide(C["ident"][:]), lm[0][d][:],
                                                    ALU.subtract).then_inc(*k.PO.mark(("y", d)))

        @block.vector
        def _(dve):
            with k.DV.turns(dve, DN_HEADS) as i:
                for d in range(2):
                    for c in range(CHUNKS):
                        nc.vector.tensor_scalar(gu[d][:, c, :], C["until"][:, d, :], tc(g, c, d, i), None,
                                                ALU.mult).then_inc(*k.DV.mark(("gu", d, c)))
                dve.wait_ge(*k.AC.after("norm_q", i))
                nc.vector.reciprocal(r[:, 0, :], r[:, 0, :]).then_inc(*k.DV.mark("r_q"))
                dve.wait_ge(*k.AC.after("norm_k", i))
                nc.vector.reciprocal(r[:, 1, :], r[:, 1, :]).then_inc(*k.DV.mark("r_k"))
                dve.wait_ge(*k.DV.after("r_q", i))
                nc.vector.scalar_tensor_tensor(qh[:], row(qkv, i), P ** -0.5, r[:, 0, :], ALU.mult,
                                               ALU.mult).then_inc(*k.DV.mark("qh"))
                dve.wait_ge(*k.DV.after("r_k", i))
                nc.vector.tensor_tensor(kh[:], row(qkv, i + 8), r[:, 1, :], ALU.mult).then_inc(*k.DV.mark("kh"))
                for d in range(2):
                    dve.wait_ge(*k.AC.after(("egb", d), i))
                    for c in range(CHUNKS):
                        nc.vector.scalar_tensor_tensor(dec[d][:, c, :], ck(B[6 + d], c), td(gc, c, d, i),
                                                       C["behind"][:, d, :], ALU.subtract,
                                                       ALU.add).then_inc(*k.DV.mark(("dd", d, c)))
                for d in range(2):
                    dve.wait_ge(*k.AC.after(("dec", d), i))
                    dve.wait_ge(*k.PE.after("kk", i))
                    for c in range(CHUNKS):
                        nc.vector.scalar_tensor_tensor(at[d][:, c, :], ck(B[4], c), tc(beta, c, d, i), dec[d][:, c, :],
                                                       ALU.mult, ALU.mult).then_inc(*k.DV.mark(("at", d, c)))
                for d in range(2):
                    dve.wait_ge(*k.PE.after("kq", i))
                    nc.vector.tensor_tensor(w4(qkt[d]), B[5][:], w4(dec[d]), ALU.mult).then_inc(*k.DV.mark(("qkt", d)))
                    dve.wait_ge(*k.AC.after(("egb", d), i))
                    nc.vector.tensor_tensor(w4(qg[d]), qh[:], w4(egb[d]), ALU.mult).then_inc(*k.DV.mark(("qg", d)))
                    dve.wait_ge(*k.AC.after("ktok", i))
                    for c in range(CHUNKS):
                        nc.vector.tensor_scalar(kbg[d][:, c, :], ktok[:, c, :], td(eg_neg, c, d, i), None,
                                                ALU.mult).then_inc(*k.DV.mark(("kbg", d, c)))
                        nc.vector.tensor_scalar(kd[d][:, c, :], ktok[:, c, :], td(ekd, c, d, i), None,
                                                ALU.mult).then_inc(*k.DV.mark(("kd", d, c)))
                for s in range(1, LEVELS):
                    for d in range(2):
                        dve.wait_ge(*k.PE.after(("dy", s, d), i))
                        nc.vector.tensor_tensor(w4(Y[d]), w4(Y[d]), B[4 + d][:], ALU.subtract).then_inc(*k.DV.mark(("y", s, d)))
                seen = set()
                for t in range(CHUNKS):
                    for d in range(2):
                        dve.wait_ge(*k.PE.after(("vn", t, d), i))
                        nc.vector.tensor_scalar(vnew[d][:], B[2 + d][:, 0:P], tc(beta, ORDER[d][t], d, i), None,
                                                ALU.mult).then_inc(*k.DV.mark(("vnew", t, d)))
                    for d in range(2):
                        c = ORDER[d][t]
                        dve.wait_ge(*k.PE.after(("o", t, d), i))
                        if c in seen:
                            dve.wait_ge(*k.DV.after(("o", ORDER[1 - d].index(c), 1 - d), i))
                            ins = nc.vector.tensor_tensor(ck(oh, c), ck(oh, c), B[4 + d][:, 0:P], ALU.add)
                        else:
                            ins = nc.vector.tensor_copy(ck(oh, c), B[4 + d][:, 0:P])
                            seen.add(c)
                        ins.then_inc(*k.DV.mark(("o", t, d)))
                        if t < CHUNKS - 1:
                            dve.wait_ge(*k.PE.after(("ds", t, d), i))
                            if t:
                                ins = nc.vector.scalar_tensor_tensor(S[d][:], S[d][:], td(ea, c, d, i), B[6 + d][:, 0:P],
                                                                     ALU.mult, ALU.add)
                            else:
                                ins = nc.vector.tensor_copy(S[d][:], B[6 + d][:, 0:P])
                            ins.then_inc(*k.DV.mark(("state", t, d)))
                dve.wait_ge(*k.AC.after("norm_o", i))
                nc.vector.reciprocal(r[:, 0, :], r[:, 0, :]).then_inc(*k.DV.mark("r_o"))
                dve.wait_ge(*k.DV.after("r_o", i))
                nc.vector.tensor_tensor(oh[:], oh[:], r[:, 0, :], ALU.mult).then_inc(*k.DV.mark("oh"))
                dve.wait_ge(*k.DV.after("oh", i))
                nc.vector.scalar_tensor_tensor(row(qkv, i), oh[:], C["dn_o_gain"][:], row(z, i), ALU.mult,
                                               ALU.mult).then_inc(*k.DV.mark("out"))





HEAD = 64
Q_HEADS = [h for pair in range(2) for i in range(4) for h in (8 * pair + i, 8 * pair + 4 + i)]


def late_constants(k, new, names):
    with k.open("load " + names[0]) as block:
        @block.sync
        def _(sp):
            for name in names:
                a = k.dram["late_" + name]
                k.C[name] = new("k" + name, *a.shape[1:])
                sp.dma_start(k.C[name][0:a.shape[0]], a).then_inc(k.stored, 16)
            k.stores += 16 * len(names)
            sp.wait_ge(k.stored, k.stores)


def norm_heads(k, name, tiles, tokens, gain, ones, width, new, rope=False, softmax_scale=1.0, eps="eps"):
    nc = k.nc
    sq, r, t = new("nh_sq", sum(map(len, tiles)), tokens), new("nh_r", len(tiles), tokens), new("nh_t", 2, tokens)
    flat = [(g, n, tile) for g, group in enumerate(tiles) for n, tile in enumerate(group)]
    a, b = 1.0 / (width * softmax_scale ** 2), k.C[eps]
    with k.open(name) as block:
        @block.scalar
        def _(act):
            for m, (g, n, tile) in enumerate(flat):
                nc.scalar.activation(sq[:, m, :], tile, ACT.Square).then_inc(*k.AC.mark(("sq", m)))
            for g in range(len(tiles)):
                act.wait_ge(*k.PE.after(("sum", g)))
                nc.scalar.activation(r[:, g, :], k.ACC[g][:, 0:tokens], ACT.Sqrt, scale=a, bias=b[:, 0:1]).then_inc(*k.AC.mark(("rms", g)))

        @block.tensor
        def _(pe):
            for m, (g, n, tile) in enumerate(flat):
                pe.wait_ge(*k.AC.after(("sq", m)))
                mm = nc.tensor.matmul(k.ACC[g][:, 0:tokens], ones[:], sq[:, m, :], start=n == 0, stop=n == len(tiles[g]) - 1)
                if n == len(tiles[g]) - 1:
                    mm.then_inc(*k.PE.mark(("sum", g)))
            if rope:
                for m, (g, n, tile) in enumerate(flat):
                    pe.wait_ge(*k.DV.after(("n", m)))
                    nc.tensor.matmul(k.AUX[m][:, 0:tokens], k.C["rot"][:], tile, start=True, stop=True).then_inc(*k.PE.mark(("rot", m)))

        @block.vector
        def _(dve):
            for g in range(len(tiles)):
                dve.wait_ge(*k.AC.after(("rms", g)))
                nc.vector.reciprocal(r[:, g, :], r[:, g, :]).then_inc(*k.DV.mark(("r", g)))
            for m, (g, n, tile) in enumerate(flat):
                dve.wait_ge(*k.DV.after(("r", g)))
                nc.vector.scalar_tensor_tensor(tile, tile, gain(n), r[:, g, :], ALU.mult, ALU.mult).then_inc(*k.DV.mark(("n", m)))
            if rope:
                for m, (g, n, tile) in enumerate(flat):
                    dve.wait_ge(*k.PE.after(("rot", m)))
                    nc.vector.tensor_tensor(t[:, m, :], k.AUX[m][:, 0:tokens], k.C["sin"][:], ALU.mult).then_inc(*k.DV.mark(("s", m)))
                    nc.vector.tensor_tensor(tile, tile, k.C["cos"][:], ALU.mult).then_inc(*k.DV.mark(("c", m)))
                    dve.wait_ge(*k.DV.after(("c", m)))
                    nc.vector.tensor_tensor(tile, tile, t[:, m, :], ALU.add).then_inc(*k.DV.mark(("roped", m)))


def window_heads(k, name, pair, new, q, ks, v, o, gain, keys, mask, sink, rope):
    nc, C = k.nc, k.C
    sq, r, qn, qs, qr = (new("wh_" + n, LAT) for n in ("sq", "r", "qn", "qs", "qr"))
    sc, pt = new("wh_scores", 4, BANK), new("wh_pt", 2, BANK)
    cols = new("wh_cols", 8, 4)
    mx, nm, sums, es, tot, rt, sk = (cols[:, n, :] for n in range(7))
    bias = new("wh_bias", 2, 256) if mask is None else None
    combos = [(hh, b) for hh in range(2) for b in range(2)]
    n_keys = [keys[b][1] - keys[b][0] for hh, b in combos]
    half = lambda t, hh: t[hh * HEAD:(hh + 1) * HEAD]
    blk = lambda b: slice(b * P, (b + 1) * P)
    with k.open(name) as block:
        @block.scalar
        def _(act):
            def copy_p(x, i):
                act.wait_ge(*k.PE.after(("pT", x), i))
                if x >= 2:
                    act.wait_ge(*k.PE.after(("o", x - 2), i))
                nc.scalar.activation(pt[:, x % 2, 0:n_keys[x]], k.AUX[x % 2][:, 0:n_keys[x]], ACT.Copy).then_inc(*k.AC.mark(("pt", x)))

            with k.AC.turns(act, 4) as i:
                nc.scalar.activation(sq[:], row(q, pair * 4 + i), ACT.Square).then_inc(*k.AC.mark("sq"))
                if bias is not None:
                    act.wait_ge(*k.DV.after(("max", 3), i - 1))
                    b_in = sink[1][:, bass.ds((pair * 4 + i) * 2, 2), :]
                    nc.scalar.activation(bias[:], b_in, ACT.Copy).then_inc(*k.AC.mark("bias"))
                act.wait_ge(*k.PE.after("sum", i))
                nc.scalar.activation(r[:], k.AUX[3][:, 0:LAT], ACT.Sqrt, scale=1.0,
                                     bias=C["eps_width"][:, 0:1]).then_inc(*k.AC.mark("rms"))
                for x in range(4):
                    act.wait_ge(*k.DV.after(("nm", x), i))
                    nc.scalar.activation(sc[:, x, 0:n_keys[x]], sc[:, x, 0:n_keys[x]], ACT.Exp, bias=nm[:, x:x + 1],
                                         accum_out=sums[:, x:x + 1]).then_inc(*k.AC.mark(("exp", x)))
                    nc.scalar.activation(es[:, x:x + 1], sk[:, combos[x][0]:combos[x][0] + 1], ACT.Exp,
                                         bias=nm[:, x:x + 1]).then_inc(*k.AC.mark(("es", x)))
                    if x:
                        copy_p(x - 1, i)
                copy_p(3, i)
                act.wait_ge(*k.PE.after(("o", 3), i))
                nc.scalar.activation(row(o, pair * 4 + i)[:, 0:LAT], k.AUX[2][:, 0:LAT], ACT.Copy).then_inc(*k.AC.mark("ev"))

        @block.vector
        def _(dve):
            with k.DV.turns(dve, 4) as i:
                dve.wait_ge(*k.AC.after(("es", 3), i - 1))
                nc.vector.tensor_copy(sk[:, 0:2], sink[0][:, bass.ds((pair * 4 + i) * 2, 2)]).then_inc(*k.DV.mark("sink"))
                dve.wait_ge(*k.AC.after("rms", i))
                nc.vector.reciprocal(r[:], r[:]).then_inc(*k.DV.mark("r"))
                dve.wait_ge(*k.DV.after("r", i))
                nc.vector.scalar_tensor_tensor((qn if rope else qs)[:], row(q, pair * 4 + i), gain, r[:], ALU.mult,
                                               ALU.mult).then_inc(*k.DV.mark("qn" if rope else "qs"))
                if rope:
                    dve.wait_ge(*k.PE.after("rot", i))
                    nc.vector.tensor_tensor(qr[:], k.AUX[3][:, LAT:2 * LAT], C["sin"][:, CTX:TOK], ALU.mult).then_inc(*k.DV.mark("qr"))
                    nc.vector.tensor_tensor(qn[:], qn[:], C["cos"][:, CTX:TOK], ALU.mult).then_inc(*k.DV.mark("qc"))
                    dve.wait_ge(*k.DV.after("qc", i))
                    nc.vector.tensor_tensor(qs[:], qn[:], qr[:], ALU.add).then_inc(*k.DV.mark("qs"))
                dve.wait_ge(*k.DV.after("sink", i))
                if bias is not None:
                    dve.wait_ge(*k.AC.after("bias", i))
                for x, (hh, b) in enumerate(combos):
                    dve.wait_ge(*k.PE.after(("score", x), i))
                    nc.vector.memset(cols[:, 7, x:x + 1], 0.0).then_inc(*k.DV.mark(("scored", x)))
                    m = mask(b) if mask else bias[:, hh, 256 - n_keys[x]:256]
                    nc.vector.tensor_tensor_reduce(sc[:, x, 0:n_keys[x]], k.ACC[x][:, 0:n_keys[x]], m, 1.0, sk[:, hh:hh + 1],
                                                   ALU.add, ALU.max, mx[:, x:x + 1]).then_inc(*k.DV.mark(("max", x)))
                    dve.wait_ge(*k.DV.after(("max", x), i))
                    nc.vector.tensor_scalar(nm[:, x:x + 1], mx[:, x:x + 1], -1.0, None, ALU.mult).then_inc(*k.DV.mark(("nm", x)))
                for x in range(4):
                    dve.wait_ge(*k.AC.after(("es", x), i))
                    nc.vector.tensor_tensor(tot[:, x:x + 1], sums[:, x:x + 1], es[:, x:x + 1], ALU.add).then_inc(*k.DV.mark(("tot", x)))
                    dve.wait_ge(*k.DV.after(("tot", x), i))
                    nc.vector.reciprocal(rt[:, x:x + 1], tot[:, x:x + 1]).then_inc(*k.DV.mark(("rt", x)))
                    dve.wait_ge(*k.DV.after(("rt", x), i))
                    nc.vector.tensor_scalar(sc[:, x, 0:n_keys[x]], sc[:, x, 0:n_keys[x]], rt[:, x:x + 1], None,
                                            ALU.mult).then_inc(*k.DV.mark(("p", x)))

        @block.tensor
        def _(pe):
            def turn_p(x, i):
                pe.wait_ge(*k.DV.after(("p", x), i))
                if x >= 2:
                    pe.wait_ge(*k.AC.after(("pt", x - 2), i))
                for kt in range(n_keys[x] // P):
                    mm = nc.tensor.transpose(k.AUX[x % 2][:, blk(kt)], sc[:, x, blk(kt)], C["ident"][:])
                mm.then_inc(*k.PE.mark(("pT", x)))

            def output(x, i):
                hh, b = combos[x]
                pe.wait_ge(*k.AC.after(("pt", x), i))
                n = n_keys[x] // P
                at = (2 * pair + hh) * HEAD
                for kt in range(n):
                    mm = nc.tensor.matmul(half(k.AUX[2], hh)[:, blk(b)], v[:, keys[b][0] // P + kt, at:at + HEAD],
                                          pt[:, x % 2, blk(kt)], start=kt == 0, stop=kt == n - 1)
                mm.then_inc(*k.PE.mark(("o", x)))

            with k.PE.turns(pe, 4) as i:
                pe.wait_ge(*k.AC.after("sq", i))
                nc.tensor.matmul(k.AUX[3][:, 0:LAT], C["ones64"][:], sq[:], start=True, stop=True).then_inc(*k.PE.mark("sum"))
                if rope:
                    pe.wait_ge(*k.DV.after("qn", i))
                    nc.tensor.matmul(k.AUX[3][:, LAT:2 * LAT], C["rot"][:], qn[:], start=True, stop=True).then_inc(*k.PE.mark("rot"))
                pe.wait_ge(*k.DV.after("qs", i))
                for x, (hh, b) in enumerate(combos):
                    nc.tensor.matmul(k.ACC[x][:, 0:n_keys[x]], half(qs, hh)[:, blk(b)],
                                     half(ks, hh)[:, pair, keys[b][0]:keys[b][1]], start=True,
                                     stop=True).then_inc(*k.PE.mark(("score", x)))
                pe.wait_ge(*k.AC.after("ev", i - 1))
                turn_p(0, i)
                for x in range(1, 4):
                    turn_p(x, i)
                    output(x - 1, i)
                output(3, i)


def project(k, name, L, src, tokens, evict, engine=None):
    with k.open(name) as block:
        feed(k, block, L)

        @block.tensor
        def _(pe):
            linear(k, pe, L, src, tokens, lambda n: k.AC)

        @block.scalar
        def _(act):
            def read(n, i):
                act.wait_ge(*k.PE.after(("acc", n), i))
                evict(act, n, i * 4 + n).then_inc(*k.AC.mark(("ev", n)))
            scalar_loop(k, act, L, read)
        if engine is not None:
            engine(block)
    close_stream(k, L.units)


def project_kv(k, name, w, src, tokens, keys, v, ahead):
    nc = k.nc
    spots = tokens // P
    with k.open(name) as block:
        @block.sync
        def _(sp):
            for s in range(2):
                sp.wait_ge(*k.PE.after(("kv", s)))
                load_unit(k, sp, ahead, s, s)

        @block.tensor
        def _(pe):
            pe.wait_ge(k.landed[0], k.landings[0] + 16)
            for m in range(2):
                for d in range(KT):
                    at = (m * KT + d) * P
                    mm = nc.tensor.matmul(k.ACC[m][:, 0:tokens], k.W[:, 0, at:at + P], src(d), start=d == 0, stop=d == KT - 1)
            mm.then_inc(*k.PE.mark(("kv", 0)))
            pe.wait_ge(k.landed[1], k.landings[1] + 16)
            for t in range(spots):
                for d in range(KT):
                    mm = nc.tensor.matmul(k.AUX[t][:, 0:256], src(d)[:, t * P:(t + 1) * P], k.W[:, 1, d * 256:(d + 1) * 256],
                                          start=d == 0, stop=d == KT - 1)
            mm.then_inc(*k.PE.mark(("kv", 1)))

        @block.scalar
        def _(act):
            act.wait_ge(*k.PE.after(("kv", 0)))
            for m in range(2):
                nc.scalar.activation(keys[:, m, :], k.ACC[m][:, 0:tokens], ACT.Copy).then_inc(*k.AC.mark(("k", m)))

        @block.vector
        def _(dve):
            dve.wait_ge(*k.PE.after(("kv", 1)))
            for t in range(spots):
                nc.vector.tensor_copy(v[:, t, :], k.AUX[t][:, 0:256]).then_inc(*k.DV.mark(("v", t)))
    close_stream(k, 2)


def swa(k, new_in, modulated, gate, ahead):
    nc, w = k.nc, k.dram
    with ExitStack() as c:
        new = new_in(c)
        late_constants(k, new, ["cos", "sin", "window", "rot", "ones64", "swa_gains", "swa_sink", "eps_width", "eps"])
        q, keys, v = new("swa_q", KT, LAT), new("swa_k", 2, TOK), new("swa_v", 4, 256)
        H = new("swa_normed", KT, TOK)
        with ExitStack() as cc:
            squares = new_in(cc)("squares", KT, TOK)
            modulated(1, 1, lambda name, src, tokens, parts: norm(k, name, src, lambda d: H[:, d, :], tokens, parts, squares))
        copy = lambda act, n, at: nc.scalar.activation(row(q, at), k.ACC[n][:, 0:LAT], ACT.Copy)
        project(k, "swa q", Layer(w["w_swa_q"], w["w_swa_kv"]), lambda d: H[:, d, CTX:TOK], LAT, copy)
        project_kv(k, "swa kv", w["w_swa_kv"], lambda d: H[:, d, :], TOK, keys, v, w["w_swa_out"])
        gains = k.C["swa_gains"]
        with ExitStack() as cc:
            norm_heads(k, "swa keys", [[keys[:, 0, :]], [keys[:, 1, :]]], TOK, lambda n: gains[:, 1:2], k.C["ones64"],
                       HEAD, new_in(cc), rope=True)
        for pair in range(2):
            with ExitStack() as cc:
                window_heads(k, f"swa heads {pair}", pair, new_in(cc), q, keys, v, H, gains[:, 0:1],
                             [(0, TOK)] * 2, lambda b: k.C["window"][:, b, :], (k.C["swa_sink"],), True)
        to_residual(k, "swa out", Layer(w["w_swa_out"], ahead), lambda d: H[:, d, 0:LAT], LAT,
                    lambda dve, n, at, i: gated_residual(k, dve, n, at, CTX, gate))


def layout_swa(I, t):
    import numpy as np
    wq = I["swa_w_qkv"][0]
    order = np.concatenate([np.arange(h * HEAD, (h + 1) * HEAD) for h in Q_HEADS])
    t["w_swa_q"] = pack(wq[:, :1024][:, order], 2)
    t["w_swa_kv"] = pack_kv(wq[:, 1024:1280], wq[:, 1280:])
    t["w_swa_out"] = pack(I["swa_w_out"][0][order], 2)
    t["late_swa_gains"] = np.stack([np.tile(I[n][0], 2) for n in ("swa_q_gain", "swa_k_gain")], 1)
    t["late_swa_sink"] = rows(I["swa_sink"][0][Q_HEADS], 16)
    t["late_eps_width"] = np.full((P, 1), EPS * HEAD, np.float32)
    t["late_eps"] = np.full((P, 1), EPS, np.float32)


def pack_kv(wk, wv):
    import numpy as np
    return np.stack([pack(wk, 2)[0], wv.reshape(KT, P, 256).transpose(1, 0, 2).reshape(P, 2048)])



SSD_HEADS = 32
GROUPS = 4
INNER = 16
CONV = 31
SECOND_CONSTANTS = ["norm_mix", "gate_bias", "conv_dw_w", "conv_dw_b", "conv_ln_g", "conv_ln_b", "ssd_conv_w",
                    "ssd_conv_b", "w_dt", "ssd_dt_bias", "ssd_a_log", "ssd_d", "ssd_norm_g", "attn_gains",
                    "attn_sinks", "norm_xattn", "norm_mem", "xattn_gains", "norm_mlp", "ones64", "eps_width",
                    "eps", "eps_xattn"]


def long_conv(k, dve, first, count, x, y):
    nc, w = k.nc, k.C["conv_dw_w"]
    with k.DV.turns(dve, count) as i:
        at = i + first
        tap = lambda j: w[:, bass.ds(at, 1), j:j + 1].rearrange("p a b -> p (a b)")
        nc.vector.tensor_scalar(row(y, at), row(x, at), tap(CONV - 1), k.C["conv_dw_b"][:, bass.ds(at, 1)], ALU.mult,
                                ALU.add).then_inc(*k.DV.mark(("tap", CONV - 1)))
        for j in reversed(range(CONV - 1)):
            a = CONV - 1 - j
            dve.wait_ge(*k.DV.after(("tap", j + 1), i))
            nc.vector.scalar_tensor_tensor(row(y, at)[:, a:LAT], row(x, at)[:, 0:LAT - a], tap(j), row(y, at)[:, a:LAT],
                                           ALU.mult, ALU.add).then_inc(*k.DV.mark(("tap", j)))


def glu(k, L, src, out, sig):
    nc = k.nc
    with k.open("glu") as block:
        feed(k, block, L)

        @block.tensor
        def _(pe):
            linear(k, pe, L, src, LAT, lambda n: k.AC if n % 2 else k.DV)

        @block.scalar
        def _(act):
            def sigmoid(n, i):
                if n % 2:
                    act.wait_ge(*k.PE.after(("acc", n), i))
                    act.wait_ge(*k.DV.after(("ev", n - 1), i - 1))
                    nc.scalar.activation(sig[:, n // 2, :], k.ACC[n][:, 0:LAT], ACT.Sigmoid).then_inc(*k.AC.mark(("ev", n)))
            scalar_loop(k, act, L, sigmoid)

        @block.vector
        def _(dve):
            with k.DV.turns(dve, L.turns) as i:
                for n in (0, 2):
                    dve.wait_ge(*k.AC.after(("ev", n + 1), i))
                    nc.vector.tensor_tensor(row(out, i * 2 + n // 2), sig[:, n // 2, :], k.ACC[n][:, 0:LAT],
                                            ALU.mult).then_inc(*k.DV.mark(("ev", n)))
    close_stream(k, L.units)


def band_bias(k, new, biasm):
    nc = k.nc
    late_constants(k, new, ["bucket", "rel_table", "band"])
    by_dist = new("by_dist", 384)
    skew = nc.dram_tensor(f"skew{int(k.stage[1])}", [P, 16, 384], F32, kind="Internal").ap()
    with k.open("band bias") as block:
        @block.tensor
        def _(pe):
            nc.tensor.matmul(k.ACC[0][0:16, 0:384], k.C["rel_table"][0:32, :], k.C["bucket"][0:32, :], start=True,
                             stop=True).then_inc(*k.PE.mark("by_dist"))

        @block.scalar
        def _(act):
            act.wait_ge(*k.PE.after("by_dist"))
            nc.scalar.activation(by_dist[0:16, :], k.ACC[0][0:16, 0:384], ACT.Copy).then_inc(*k.AC.mark("by_dist"))

        @block.sync
        def _(sp):
            sp.wait_ge(*k.AC.after("by_dist"))
            sp.dma_start(skew.rearrange("i h x -> h i x"),
                         by_dist[0:16, :].unsqueeze(1).to_broadcast([16, P, 384])).then_inc(k.stored, 16)
            sp.wait_ge(k.stored, k.stores + 16)
            shifted = bass.AP(tensor=skew.tensor, offset=P - 1, ap=[[16 * 384 - 1, P], [384, 16], [1, 256]])
            sp.dma_start(biasm[:], shifted).then_inc(k.stored, 16)
            sp.wait_ge(k.stored, k.stores + 32)

        @block.vector
        def _(dve):
            dve.wait_ge(k.stored, k.stores + 32)
            nc.vector.tensor_tensor(biasm[:], biasm[:], k.C["band"][:].unsqueeze(1).to_broadcast([P, 16, 256]),
                                    ALU.add).then_inc(*k.DV.mark("masked"))
    k.stores += 32


def conv_norm(k, x, sq):
    nc, C = k.nc, k.C
    mean, r = k.R[:, 0, 0:LAT], k.R[:, 1, 0:LAT]
    with k.open("conv norm") as block:
        @block.tensor
        def _(pe):
            for d in range(KT):
                mm = nc.tensor.matmul(k.ACC[0][:, 0:LAT], C["ones"][:], x[:, d, :], start=d == 0, stop=d == KT - 1)
            mm.then_inc(*k.PE.mark("sum"))
            for d in range(KT):
                pe.wait_ge(*k.AC.after(("sq", d)))
                mm = nc.tensor.matmul(k.ACC[1][:, 0:LAT], C["ones"][:], sq[:, d, 0:LAT], start=d == 0, stop=d == KT - 1)
            mm.then_inc(*k.PE.mark("squares"))

        @block.scalar
        def _(act):
            act.wait_ge(*k.PE.after("sum"))
            nc.scalar.activation(mean, k.ACC[0][:, 0:LAT], ACT.Copy, scale=1.0 / D).then_inc(*k.AC.mark("mean"))
            for d in range(KT):
                act.wait_ge(*k.DV.after(("centred", d)))
                nc.scalar.activation(sq[:, d, 0:LAT], x[:, d, :], ACT.Square).then_inc(*k.AC.mark(("sq", d)))
            act.wait_ge(*k.PE.after("squares"))
            nc.scalar.activation(r, k.ACC[1][:, 0:LAT], ACT.Sqrt, scale=1.0 / D, bias=k.EPSC[:]).then_inc(*k.AC.mark("std"))
            for d in range(KT):
                act.wait_ge(*k.DV.after(("normed", d)))
                nc.scalar.activation(x[:, d, :], x[:, d, :], ACT.Silu, scale=C["conv_ln_g"][:, d:d + 1],
                                     bias=C["conv_ln_b"][:, d:d + 1]).then_inc(*k.AC.mark(("out", d)))

        @block.vector
        def _(dve):
            dve.wait_ge(*k.AC.after("mean"))
            for d in range(KT):
                nc.vector.tensor_tensor(x[:, d, :], x[:, d, :], mean, ALU.subtract).then_inc(*k.DV.mark(("centred", d)))
            dve.wait_ge(*k.AC.after("std"))
            nc.vector.reciprocal(r, r).then_inc(*k.DV.mark("r"))
            dve.wait_ge(*k.DV.after("r"))
            for d in range(KT):
                nc.vector.tensor_tensor(x[:, d, :], x[:, d, :], r, ALU.mult).then_inc(*k.DV.mark(("normed", d)))


def ssd_prepare(k, u, xbc, dt, da, cs, dte, tmp, cb, btok):
    nc, C = k.nc, k.C
    flat = lambda t: t[:].rearrange("p a b -> p (a b)")
    state_in, state_out = lambda g: xbc[:, INNER + g, :], lambda g: xbc[:, INNER + GROUPS + g, :]
    with k.open("ssd prepare") as block:
        @block.tensor
        def _(pe):
            for t in range(2):
                for d in range(KT):
                    mm = nc.tensor.matmul(k.AUX[0][:, t * 32:(t + 1) * 32], u(d)[:, t * P:(t + 1) * P], C["w_dt"][:, d, :],
                                          start=d == 0, stop=d == KT - 1)
            mm.then_inc(*k.PE.mark("dt"))
            for g in range(GROUPS):
                for c in range(2):
                    at = slice(c * P, (c + 1) * P)
                    out = (g % 2) * 256 + c * P
                    mm = nc.tensor.matmul(k.ACC[g // 2][:, out:out + P], state_in(g)[:, at], state_out(g)[:, at], start=True,
                                          stop=True)
                if g % 2:
                    mm.then_inc(*k.PE.mark(("cb", g // 2)))
            for g in range(GROUPS):
                mm = nc.tensor.transpose(k.ACC[2][:, g * P:(g + 1) * P], state_in(g)[:, 0:P], C["ident"][:])
            mm.then_inc(*k.PE.mark("btok"))
            pe.wait_ge(*k.DV.after("da"))
            nc.tensor.matmul(k.AUX[1][:, 0:64], C["until"][:, 0, :], flat(da), start=True, stop=True)
            nc.tensor.matmul(k.AUX[1][:, 64:96], C["ones"][:], da[:, 0, :], start=True, stop=True).then_inc(*k.PE.mark("cs"))

        @block.vector
        def _(dve):
            dve.wait_ge(*k.PE.after("dt"))
            nc.vector.tensor_tensor(tmp[:, 0], k.AUX[0][:, 0:64], C["ssd_dt_bias"][:], ALU.add).then_inc(*k.DV.mark("x"))
            dve.wait_ge(*k.DV.after("x"))
            nc.vector.scalar_tensor_tensor(tmp[:, 1], tmp[:, 0], -1.0, tmp[:, 0], ALU.mult, ALU.max).then_inc(*k.DV.mark("|x|"))
            dve.wait_ge(*k.AC.after("ln"))
            nc.vector.scalar_tensor_tensor(flat(dt), tmp[:, 0], 0.0, tmp[:, 1], ALU.max, ALU.add).then_inc(*k.DV.mark("dt"))
            dve.wait_ge(*k.DV.after("dt"))
            nc.vector.scalar_tensor_tensor(flat(da), flat(dt), -1.0, C["ssd_a_log"][:], ALU.mult, ALU.mult).then_inc(*k.DV.mark("da"))
            dve.wait_ge(*k.PE.after("cs"))
            nc.vector.tensor_copy(flat(cs), k.AUX[1][:, 0:64]).then_inc(*k.DV.mark("cs"))
            dve.wait_ge(*k.DV.after("cs"))
            nc.vector.tensor_tensor(dte[:], k.AUX[1][:, 64:96], cs[:, 0, :], ALU.subtract).then_inc(*k.DV.mark("to end"))
            dve.wait_ge(*k.AC.after("dte"))
            nc.vector.tensor_tensor(dte[:], dte[:], dt[:, 0, :], ALU.mult).then_inc(*k.DV.mark("dte"))

        @block.scalar
        def _(act):
            nc.scalar.activation(C["ssd_a_log"][:], C["ssd_a_log"][:], ACT.Exp).then_inc(*k.AC.mark("a"))
            act.wait_ge(*k.DV.after("|x|"))
            nc.scalar.activation(tmp[:, 1], tmp[:, 1], ACT.Exp, scale=-1.0).then_inc(*k.AC.mark("exp"))
            act.wait_ge(*k.AC.after("exp"))
            nc.scalar.activation(tmp[:, 1], tmp[:, 1], ACT.Ln, bias=1.0).then_inc(*k.AC.mark("ln"))
            for h in range(2):
                act.wait_ge(*k.PE.after(("cb", h)))
                nc.scalar.activation(cb[:, 2 * h:2 * h + 2, :].rearrange("p g n -> p (g n)"), k.ACC[h][:],
                                     ACT.Copy).then_inc(*k.AC.mark(("cb", h)))
            act.wait_ge(*k.PE.after("btok"))
            nc.scalar.activation(flat(btok), k.ACC[2][:], ACT.Copy).then_inc(*k.AC.mark("btok"))
            act.wait_ge(*k.DV.after("to end"))
            nc.scalar.activation(dte[:], dte[:], ACT.Exp).then_inc(*k.AC.mark("dte"))


def ssd_heads(k, g, new, xbc, z, dt, da, cs, dte, cb, btok):
    nc, C = k.nc, k.C
    xh, xtok, xdt, xe = new("s_xh", LAT), new("s_xtok", 2, P), new("s_xdt", 2, 2, 64), new("s_xe", 2, 64)
    gu, dec, sct = (new("s_" + n, 4, P) for n in ("gu", "dec", "sct"))
    egb, cme, st, y = new("s_egb", 2, P), new("s_cme", 2, P), new("s_st", P), new("s_y", LAT)
    flat = lambda t: t[:].rearrange("p a b -> p (a b)")
    combos = [(hh, c) for hh in range(2) for c in range(2)]
    csb = k.AUX[1][:].rearrange("p (x t) -> p x t", x=4)
    with k.open(f"ssd heads {g}") as block:
        head = lambda i, hh: bass.ds((g * 4 + i) * 2 + hh, 1)

        @block.scalar
        def _(act):
            with k.AC.turns(act, 4) as i:
                act.wait_ge(*k.DV.after("y1", i - 1))
                nc.scalar.activation(xh[:], row(xbc, g * 4 + i), ACT.Copy).then_inc(*k.AC.mark("xh"))
                act.wait_ge(*k.PE.after("xT", i))
                nc.scalar.activation(flat(xtok), k.AUX[0][:, 0:256], ACT.Copy).then_inc(*k.AC.mark("xtok"))
                act.wait_ge(*k.PE.after("csb", i))
                for hh in range(2):
                    nc.scalar.activation(egb[:, hh, :], csb[:, hh * 2 + 1, :], ACT.Exp).then_inc(*k.AC.mark(("egb", hh)))
                act.wait_ge(*k.DV.after(("dd", 3), i))
                nc.scalar.activation(flat(dec), flat(dec), ACT.Exp).then_inc(*k.AC.mark("dec"))
                act.wait_ge(*k.PE.after("state", i))
                nc.scalar.activation(st[:], k.AUX[2][:, 0:P], ACT.Copy).then_inc(*k.AC.mark("st"))

        @block.tensor
        def _(pe):
            with k.PE.turns(pe, 4) as i:
                pe.wait_ge(*k.DV.after("gu3", i))
                nc.tensor.matmul(k.AUX[1][:], C["ones"][:], flat(gu), start=True, stop=True).then_inc(*k.PE.mark("csb"))
                pe.wait_ge(*k.AC.after("xh", i))
                for c in range(2):
                    mm = nc.tensor.transpose(k.AUX[0][:, c * P:(c + 1) * P], xh[:, c * P:(c + 1) * P], C["ident"][:])
                mm.then_inc(*k.PE.mark("xT"))
                pe.wait_ge(*k.DV.after(("xe", 1), i))
                nc.tensor.matmul(k.AUX[2][:, 0:P], btok[:, g, :], flat(xe), start=True, stop=True).then_inc(*k.PE.mark("state"))
                pe.wait_ge(*k.DV.after("cme", i))
                pe.wait_ge(*k.AC.after("st", i))
                for x, (hh, c) in enumerate(combos):
                    out = k.AUX[3][hh * 64:(hh + 1) * 64, c * P:(c + 1) * P]
                    mm = nc.tensor.matmul(out, xdt[:, c, hh, :], sct[:, x, :], start=True, stop=c == 0)
                    if c:
                        mm = nc.tensor.matmul(out, st[:, hh * 64:(hh + 1) * 64], cme[:, hh, :], start=False, stop=True)
                mm.then_inc(*k.PE.mark("y"))

        @block.vector
        def _(dve):
            with k.DV.turns(dve, 4) as i:
                for x, (hh, c) in enumerate(combos):
                    nc.vector.tensor_scalar(gu[:, x, :], C["until"][:, 0, :], da[:, c, head(i, hh)], None,
                                            ALU.mult).then_inc(*k.DV.mark(f"gu{x}"))
                dve.wait_ge(*k.AC.after("xtok", i))
                for x, (hh, c) in enumerate(combos):
                    nc.vector.tensor_scalar(xdt[:, c, hh, :], xtok[:, c, hh * 64:(hh + 1) * 64], dt[:, c, head(i, hh)], None,
                                            ALU.mult).then_inc(*k.DV.mark(("xdt", x)))
                for hh in range(2):
                    nc.vector.tensor_scalar(xe[:, hh, :], xtok[:, 0, hh * 64:(hh + 1) * 64], dte[:, head(i, hh)], None,
                                            ALU.mult).then_inc(*k.DV.mark(("xe", hh)))
                dve.wait_ge(*k.AC.after(("egb", 1), i))
                for x, (hh, c) in enumerate(combos):
                    nc.vector.scalar_tensor_tensor(dec[:, x, :], csb[:, x, :], cs[:, c, head(i, hh)], C["behind"][:, 0, :],
                                                   ALU.subtract, ALU.add).then_inc(*k.DV.mark(("dd", x)))
                dve.wait_ge(*k.AC.after("dec", i))
                for hh in range(2):
                    nc.vector.tensor_tensor(sct[:, 2 * hh:2 * hh + 2, :].rearrange("p a b -> p (a b)"),
                                            dec[:, 2 * hh:2 * hh + 2, :].rearrange("p a b -> p (a b)"), cb[:, g, :],
                                            ALU.mult).then_inc(*k.DV.mark(("sct", hh)))
                nc.vector.tensor_tensor(cme[:], egb[:], xbc[:, INNER + GROUPS + g, P:2 * P].unsqueeze(1).to_broadcast([P, 2, P]),
                                        ALU.mult).then_inc(*k.DV.mark("cme"))
                dve.wait_ge(*k.PE.after("y", i))
                nc.vector.scalar_tensor_tensor(y[:], xh[:], C["ssd_d"][:, bass.ds(g * 4 + i, 1)], k.AUX[3][:, 0:LAT], ALU.mult,
                                               ALU.add).then_inc(*k.DV.mark("y1"))
                dve.wait_ge(*k.DV.after("y1", i))
                nc.vector.tensor_tensor(row(xbc, g * 4 + i), y[:], row(z, g * 4 + i), ALU.mult).then_inc(*k.DV.mark("y2"))


def cross_heads(k, new, q, keys, v, o):
    nc = k.nc
    combos = [(h, b) for h in range(4) for b in range(2)]
    sc, pt, cols = new("x_scores", 4, 256), new("x_pt", 2, 256), new("x_cols", 4, 8)
    mx, nm, sums, rt = (cols[:, n, :] for n in range(4))
    blk = lambda b: slice(b * P, (b + 1) * P)
    with k.open("cross heads") as block:
        @block.tensor
        def _(pe):
            def score(x):
                h, b = combos[x]
                if x >= 4:
                    pe.wait_ge(*k.AC.after(("exp", x - 4)))
                for e in range(2):
                    mm = nc.tensor.matmul(k.ACC[x % 4][:, 0:256], q[:, 2 * h + e, blk(b)], keys[:, 2 * h + e, :],
                                          start=e == 0, stop=e == 1)
                mm.then_inc(*k.PE.mark(("score", x)))

            def turn_p(x):
                pe.wait_ge(*k.DV.after(("p", x)))
                if x >= 2:
                    pe.wait_ge(*k.AC.after(("pt", x - 2)))
                for t in range(2):
                    mm = nc.tensor.transpose(k.AUX[x % 2][:, blk(t)], sc[:, x % 4, blk(t)], k.C["ident"][:])
                mm.then_inc(*k.PE.mark(("pT", x)))

            def output(x):
                h, b = combos[x]
                pe.wait_ge(*k.AC.after(("pt", x)))
                if x >= 2:
                    pe.wait_ge(*k.AC.after(("ev", x - 2)))
                for e in range(2):
                    for t in range(2):
                        at = (2 * h + e) * P
                        mm = nc.tensor.matmul(k.AUX[2 + x % 2][:, blk(e)], v[:, t, at:at + P], pt[:, x % 2, blk(t)],
                                              start=t == 0, stop=t == 1)
                mm.then_inc(*k.PE.mark(("o", x)))

            for x in range(4):
                score(x)
            for x in range(9):
                if x < 8:
                    turn_p(x)
                if 1 <= x:
                    output(x - 1)
                if x + 4 < 8:
                    score(x + 4)

        @block.scalar
        def _(act):
            for x in range(9):
                if x < 8:
                    act.wait_ge(*k.DV.after(("nm", x)))
                    if x >= 4:
                        act.wait_ge(*k.PE.after(("pT", x - 4)))
                    nc.scalar.activation(sc[:, x % 4, :], k.ACC[x % 4][:, 0:256], ACT.Exp, bias=nm[:, x:x + 1],
                                         accum_out=sums[:, x:x + 1]).then_inc(*k.AC.mark(("exp", x)))
                if x >= 1:
                    y = x - 1
                    h, b = combos[y]
                    act.wait_ge(*k.PE.after(("pT", y)))
                    if y >= 2:
                        act.wait_ge(*k.PE.after(("o", y - 2)))
                    nc.scalar.activation(pt[:, y % 2, :], k.AUX[y % 2][:, 0:256], ACT.Copy).then_inc(*k.AC.mark(("pt", y)))
                    act.wait_ge(*k.PE.after(("o", y)))
                    nc.scalar.activation(o[:, 2 * h:2 * h + 2, blk(b)],
                                         k.AUX[2 + y % 2][:, 0:256].rearrange("p (e t) -> p e t", e=2),
                                         ACT.Copy).then_inc(*k.AC.mark(("ev", y)))

        @block.vector
        def _(dve):
            def maximum(x):
                dve.wait_ge(*k.PE.after(("score", x)))
                nc.vector.reduce_max(mx[:, x:x + 1], k.ACC[x % 4][:, 0:256], AX_X).then_inc(*k.DV.mark(("max", x)))
                dve.wait_ge(*k.DV.after(("max", x)))
                nc.vector.tensor_scalar(nm[:, x:x + 1], mx[:, x:x + 1], -1.0, None, ALU.mult).then_inc(*k.DV.mark(("nm", x)))

            for x in range(2):
                maximum(x)
            for x in range(8):
                dve.wait_ge(*k.AC.after(("exp", x)))
                nc.vector.reciprocal(rt[:, x:x + 1], sums[:, x:x + 1]).then_inc(*k.DV.mark(("rt", x)))
                dve.wait_ge(*k.DV.after(("rt", x)))
                nc.vector.tensor_scalar(sc[:, x % 4, :], sc[:, x % 4, :], rt[:, x:x + 1], None, ALU.mult).then_inc(*k.DV.mark(("p", x)))
                if x + 2 < 8:
                    maximum(x + 2)


def memory_values(k, w, mem, v, ahead):
    nc = k.nc
    units = w.shape[0]
    with k.open("cross v") as block:
        @block.sync
        def _(sp):
            stream(k, sp, w, ahead, units, lambda s, i: k.PE.after(("v", s)))

        @block.tensor
        def _(pe):
            for s in range(units):
                weights_here = k.landings[s % 2] + 16 * (s // 2 + 1)
                pe.wait_ge(k.landed[s % 2], weights_here)
                for t in range(2):
                    for d in range(KT):
                        mm = nc.tensor.matmul(k.banks[s][:, t * 256:(t + 1) * 256], mem[:, d, t * P:(t + 1) * P],
                                              k.W[:, s % 2, d * 256:(d + 1) * 256], start=d == 0, stop=d == KT - 1)
                mm.then_inc(*k.PE.mark(("v", s)))

        @block.scalar
        def _(act):
            for s in range(units):
                act.wait_ge(*k.PE.after(("v", s)))
                nc.scalar.activation(v[:, :, s * 256:(s + 1) * 256], k.banks[s][:].rearrange("p (t n) -> p t n", t=2),
                                     ACT.Copy).then_inc(*k.AC.mark(("v", s)))
    close_stream(k, units)


def second(k, new_in, w):
    nc, C = k.nc, k.C
    X = lambda d: k.X[:, d, CTX:TOK]
    column = lambda t: lambda d: t[:, d:d + 1]
    parts = lambda name: [(0, LAT, column(C[name]), None)]

    with ExitStack() as c:
        new = new_in(c)
        late_constants(k, new, SECOND_CONSTANTS)
        merged, H = new("merged", KT, LAT), new("normed", KT, LAT)
        u = lambda d: H[:, d, :]
        k.WH, k.WL = (new(n, 2, 2048, dtype=F32R) for n in ("weights_hi", "weights_lo"))
        k.HH, k.HL = (new(n, KT, LAT, dtype=F32R) for n in ("normed_hi", "normed_lo"))
        hi, lo = lambda d: k.HH[:, d, :], lambda d: k.HL[:, d, :]
        both = lambda d: (hi(d), lo(d))
        norm_split(k, "norm mix", X, hi, lo, LAT, parts("norm_mix"), H)
        with ExitStack() as cm:
            mixing = new_in(cm)
            gates, cv = mixing("gates", 24, LAT), mixing("cv", KT, LAT)

            def branch(name, L, src, first_gate, tmp):
                def write(dve, n, at, i):
                    gate_tile, bank = row(gates, first_gate + at), k.ACC[n][:, 0:LAT]
                    if first_gate == 16:
                        nc.vector.tensor_tensor(row(merged, at), gate_tile, bank, ALU.mult).then_inc(*k.DV.mark(("ev", n)))
                        return
                    nc.vector.tensor_tensor(tmp[:, n % 2, 0:LAT], gate_tile, bank, ALU.mult).then_inc(*k.DV.mark(("ev", n)))
                    dve.wait_ge(*k.DV.after(("ev", n), i))
                    nc.vector.tensor_tensor(row(merged, at), row(merged, at), tmp[:, n % 2, 0:LAT], ALU.add).then_inc(*k.DV.mark(("add", n)))
                to_residual(k, name, L, src, LAT, write)

            with ExitStack() as cg:
                gl = new_in(cg)("gl", KT, LAT)
                with ExitStack() as cc:
                    glu(k, Layer(w["w_conv"], w["w_gate"], fresh=True), both, gl, new_in(cc)("sig", 2, LAT))

                def conv_beside(first, count):
                    def engine(block):
                        @block.vector
                        def _(dve):
                            long_conv(k, dve, first, count, gl, cv)
                    return engine

                sigmoid = lambda act, n, at: nc.scalar.activation(row(gates, at), k.ACC[n][:, 0:LAT], ACT.Sigmoid,
                                                                  bias=C["gate_bias"][:, bass.ds(at, 1)])
                project(k, "gates", Layer(w["w_gate"], w["w_q"], split=True), both, LAT, sigmoid, engine=conv_beside(0, 5))
                with ExitStack() as cc:
                    local = new_in(cc)
                    q, keys, v, o = local("q2", KT, LAT), local("k2", 2, LAT), local("v2", 2, 256), local("o2", KT, LAT)
                    copy = lambda act, n, at: nc.scalar.activation(row(q, at), k.ACC[n][:, 0:LAT], ACT.Copy)
                    project(k, "q", Layer(w["w_q"], w["w_kv"], split=True), both, LAT, copy, engine=conv_beside(5, 3))
                    project_kv(k, "kv", w["w_kv"], u, LAT, keys, v, w["w_attn_out"])
                    gains = C["attn_gains"]
                    biasm = local("biasm", 16, 256)
                    with ExitStack() as c3:
                        band_bias(k, new_in(c3), biasm)
                    with ExitStack() as c3:
                        norm_heads(k, "keys", [[keys[:, 0, :]], [keys[:, 1, :]]], LAT, lambda n: gains[:, 1:2], C["ones64"],
                                   HEAD, new_in(c3))
                    for pair in range(2):
                        with ExitStack() as c3:
                            window_heads(k, f"heads {pair}", pair, new_in(c3), q, keys, v, o, gains[:, 0:1],
                                         [(0, P), (0, LAT)], None, (C["attn_sinks"], biasm), False)
                    branch("attention out", Layer(w["w_attn_out"], w["w_conv_out"]), lambda d: o[:, d, :], 16, None)
            conv_norm(k, cv, k.X[:, :, 0:CTX])
            branch("conv out", Layer(w["w_conv_out"], w["w_z"]), lambda d: cv[:, d, :], 0, k.R)
            with ExitStack() as cc:
                local = new_in(cc)
                z, xbc = local("z2", INNER, LAT), local("xbc", INNER + 2 * GROUPS, LAT)
                silu = lambda act, n, at: nc.scalar.activation(row(z, at), k.ACC[n][:, 0:LAT], ACT.Silu)
                project(k, "z", Layer(w["w_z"], w["w_xbc"], fresh=True), both, LAT, silu)
                with ExitStack() as c3:
                    taps = C["ssd_conv_w"]
                    conv_silu(k, "xbc", Layer(w["w_xbc"], w["w_ssd_out"], split=True), both, 1, LAT, taps, taps.shape[2] - 1,
                              C["ssd_conv_b"], xbc, new_in(c3)("convs2", 4, LAT))
                dt, da, cs, dte, tmp = local("dt", 2, 32), local("da", 2, 32), local("cs", 2, 32), local("dte", 32), local("stmp", 2, 64)
                cb, btok = local("cb", GROUPS, 256), local("btok", GROUPS, P)
                ssd_prepare(k, u, xbc, dt, da, cs, dte, tmp, cb, btok)
                for g in range(GROUPS):
                    with ExitStack() as c3:
                        ssd_heads(k, g, new_in(c3), xbc, z, dt, da, cs, dte, cb, btok)
                ssd_norm(k, xbc, k.X[:, :, 0:CTX])
                branch("ssd out", Layer(w["w_ssd_out"], w["w_mix"], group=1), lambda d: xbc[:, d, :], 8, k.R)

        def plain(dve, n, at, i):
            x = row(k.X, at)[:, CTX:TOK]
            nc.vector.tensor_tensor(x, x, k.ACC[n][:, 0:LAT], ALU.add).then_inc(*k.DV.mark(("ev", n)))

        to_residual(k, "mix out", Layer(w["w_mix"], w["w_xq"]), lambda d: merged[:, d, :], LAT, plain)
        with ExitStack() as cc:
            local = new_in(cc)
            sq = local("squares", KT, LAT)
            q, keys, v, o = local("xq", KT, LAT), local("xk", KT, LAT), local("xv", 2, D), local("xo", KT, LAT)
            late_constants(k, local, ["mem"])
            mem = C["mem"]
            m = lambda d: mem[:, d, :]
            norm_split(k, "norm xattn", X, hi, lo, LAT, parts("norm_xattn"), sq)
            norm(k, "norm mem", m, m, LAT, parts("norm_mem"), sq)
            into = lambda t: lambda act, n, at: nc.scalar.activation(row(t, at), k.ACC[n][:, 0:LAT], ACT.Copy)
            project(k, "cross q", Layer(w["w_xq"], w["w_xk"], fresh=True), both, LAT, into(q))
            project(k, "cross k", Layer(w["w_xk"], w["w_xv"]), m, LAT, into(keys))
            memory_values(k, w["w_xv"], mem, v, w["w_xo"])
            gains = C["xattn_gains"]
            heads = lambda t: [[t[:, 2 * h, :], t[:, 2 * h + 1, :]] for h in range(4)]
            with ExitStack() as c3:
                norm_heads(k, "cross q norm", heads(q), LAT, lambda n: gains[:, n:n + 1], C["ones"], 256, new_in(c3),
                           softmax_scale=256 ** -0.5, eps="eps_xattn")
            with ExitStack() as c3:
                norm_heads(k, "cross k norm", heads(keys), LAT, lambda n: gains[:, 2 + n:3 + n], C["ones"], 256, new_in(c3))
            with ExitStack() as c3:
                cross_heads(k, new_in(c3), q, keys, v, o)
            to_residual(k, "cross out", Layer(w["w_xo"], w["w_up"]), lambda d: o[:, d, :], LAT, plain)
        with ExitStack() as cc:
            local = new_in(cc)
            hidden = [local(f"hidden2_{part}", 4 * KT, LAT, dtype=F32R) for part in ("hi", "lo")]
            relus, squares = local("relus", 4, LAT), local("squares", 4, LAT)
            norm_split(k, "norm mlp", X, hi, lo, LAT, parts("norm_mlp"), H)
            squared_mlp_up(k, Layer(w["w_up"], w["w_down"], fresh=True), both, hidden, relus, squares)
            to_residual(k, "down", Layer(w["w_down"], w["w_down"], group=1, parts=2, split=True),
                        lambda d: (hidden[0][:, d, :], hidden[1][:, d, :]), LAT, plain)
            drain_stream(k)


def drain_stream(k):
    with k.open("drain stream") as block:
        @block.sync
        def _(sp):
            for s in range(2):
                sp.wait_ge(k.landed[s], k.landings[s] + 16)


def squared_mlp_up(k, L, u, hidden, relus, squares):
    nc = k.nc
    hi, lo = hidden
    with k.open("up") as block:
        feed(k, block, L)

        @block.tensor
        def _(pe):
            linear(k, pe, L, u, LAT, lambda n: k.DV)

        @block.scalar
        def _(act):
            def relu(n, i):
                act.wait_ge(*k.PE.after(("acc", n), i))
                act.wait_ge(*k.DV.after(("ev", n), i - 1))
                nc.scalar.activation(relus[:, n, :], k.ACC[n][:, 0:LAT], ACT.Relu).then_inc(*k.AC.mark(("relu", n)))
                act.wait_ge(*k.DV.after(("ev", n), i))
                nc.scalar.activation(row(hi, i * 4 + n), squares[:, n, :], ACT.Copy).then_inc(*k.AC.mark(("hi", n)))
            scalar_loop(k, act, L, relu)

        @block.vector
        def _(dve):
            with k.DV.turns(dve, L.turns) as i:
                for n in range(4):
                    dve.wait_ge(*k.AC.after(("relu", n), i))
                    nc.vector.tensor_tensor(squares[:, n, :], relus[:, n, :], k.ACC[n][:, 0:LAT],
                                            ALU.mult).then_inc(*k.DV.mark(("ev", n)))
                    dve.wait_ge(*k.AC.after(("hi", n), i))
                    nc.vector.tensor_tensor(row(lo, i * 4 + n), squares[:, n, :], row(hi, i * 4 + n).bitcast(F32),
                                            ALU.subtract).then_inc(*k.DV.mark(("lo", n)))
    close_stream(k, L.units)


def ssd_norm(k, y, sq):
    nc = k.nc
    r = lambda g: k.R[:, g // 2, (g % 2) * LAT:(g % 2 + 1) * LAT]
    with k.open("ssd norm") as block:
        @block.scalar
        def _(act):
            for t in range(INNER):
                if t >= KT:
                    act.wait_ge(*k.PE.after(("sum", (t - KT) // 4)))
                nc.scalar.activation(sq[:, t % KT, :], y[:, t, :], ACT.Square).then_inc(*k.AC.mark(("sq", t)))
            for g in range(GROUPS):
                act.wait_ge(*k.PE.after(("sum", g)))
                nc.scalar.activation(r(g), k.ACC[g][:, 0:LAT], ACT.Sqrt, scale=1.0 / 512, bias=k.EPSC[:]).then_inc(*k.AC.mark(("rms", g)))

        @block.tensor
        def _(pe):
            for t in range(INNER):
                pe.wait_ge(*k.AC.after(("sq", t)))
                mm = nc.tensor.matmul(k.ACC[t // 4][:, 0:LAT], k.C["ones"][:], sq[:, t % KT, :], start=t % 4 == 0, stop=t % 4 == 3)
                if t % 4 == 3:
                    mm.then_inc(*k.PE.mark(("sum", t // 4)))

        @block.vector
        def _(dve):
            for g in range(GROUPS):
                dve.wait_ge(*k.AC.after(("rms", g)))
                nc.vector.reciprocal(r(g), r(g)).then_inc(*k.DV.mark(("r", g)))
                dve.wait_ge(*k.DV.after(("r", g)))
                for t in range(4 * g, 4 * g + 4):
                    nc.vector.scalar_tensor_tensor(y[:, t, :], y[:, t, :], k.C["ssd_norm_g"][:, t:t + 1], r(g), ALU.mult,
                                                   ALU.mult).then_inc(*k.DV.mark(("out", t)))


def layout_second(I, t):
    import numpy as np
    I = {n[:-2]: (a if n in ("mem_2", "rel_table_2") else a[0]) for n, a in I.items() if n.endswith("_2")}
    win = I["w_in"]
    cuts = np.cumsum([0, 2048, 2048, 3072, 32, 1024, 256, 256, 3072])
    conv, z, xbc, dt, q, kk, v, gate = (win[:, a:b] for a, b in zip(cuts[:-1], cuts[1:]))
    order = np.concatenate([np.arange(h * HEAD, (h + 1) * HEAD) for h in Q_HEADS])
    t["w_conv"] = pack(conv.reshape(D, 2, KT, P).transpose(0, 2, 1, 3).reshape(D, 2 * D), 2)
    t["w_gate"], t["w_z"], t["w_xbc"] = pack(gate, 2), pack(z, 2), pack(xbc, 2)
    t["w_q"], t["w_kv"] = pack(q[:, order], 2), pack_kv(kk, v)
    t["w_attn_out"] = pack(I["w_attn_out"][order], 2)
    t["w_conv_out"], t["w_ssd_out"], t["w_mix"] = pack(I["w_conv_out"], 2), pack(I["w_ssd_out"], 1), pack(I["w_mix_out"], 2)
    t["w_xq"], t["w_xk"], t["w_xo"] = pack(I["w_xq"], 2), pack(I["w_xkv"][:, :D], 2), pack(I["w_xo"], 2)
    t["w_xv"] = as_moving(I["w_xkv"][:, D:])
    t["w_up"], t["w_down"] = pack(I["w_mlp_up"], 2), halves(pack(I["w_mlp_down"], 1))
    t["late_w_dt"] = dt.reshape(KT, P, 32).transpose(1, 0, 2)
    for name in ("norm_mix", "conv_dw_b", "conv_ln_g", "conv_ln_b", "ssd_conv_b", "ssd_norm_g", "norm_xattn", "norm_mem",
                 "norm_mlp"):
        t["late_" + name] = columns(I[name])
    t["late_gate_bias"] = columns(I["gate_bias"].reshape(-1))
    t["late_conv_dw_w"] = columns(I["conv_dw_w"]).transpose(0, 2, 1)
    t["late_ssd_conv_w"] = columns(I["ssd_conv_w"]).transpose(0, 2, 1)
    t["late_ssd_dt_bias"] = rows(np.tile(I["ssd_dt_bias"], 2), 64)
    t["late_ssd_a_log"] = rows(np.tile(I["ssd_A_log"], 2), 64)
    t["late_ssd_d"] = columns(np.repeat(I["ssd_D"], 64))
    t["late_attn_gains"] = np.stack([np.tile(I[n], 2) for n in ("attn_q_norm", "attn_k_norm")], 1)
    t["late_attn_sinks"] = rows(I["attn_sinks"][Q_HEADS], 16)
    t["late_rel_table"] = I["rel_table"][:, Q_HEADS]
    t["late_xattn_gains"] = np.concatenate([columns(I["xattn_q_norm"]), columns(I["xattn_k_norm"])], 1)
    t["late_mem"] = feature_major(I["mem"][0])
    t["late_eps_xattn"] = np.full((P, 1), EPS * 256, np.float32)



def build(nc, dram, out, steps, counted):
    with ExitStack() as ctx:
        k = Kit(nc, ctx, dram, steps, counted)
        X = k.X
        number = count()
        new_in = lambda c: lambda name, *shape, dtype=F32: c.enter_context(
            nc.sbuf_tensor(f"{name}_{next(number)}", [P, *shape], dtype))
        new = new_in(ctx)
        w = dram
        scale, gate, mod = new("scale", 2, 3, 16), new("gate", 2, 3, 16), new("mod", 288)
        col = lambda t, l, n: lambda d, c: t[:, l, n, bass.ds(d * 2 + c, 1)]
        shift = lambda l, n: lambda d, c: mod[:, bass.ds(((l * 9 + n * 3) * KT + d) * 2 + c, 1)]
        ffn1, ffn2 = w["w_ffn1"], w["w_ffn2"]
        mlp1 = lambda l, n: ffn1[(l * 2 + n) * FT:(l * 2 + n + 1) * FT]
        mlp2 = lambda l, n: ffn2[(l * 2 + n) * 2 * KT:(l * 2 + n + 1) * 2 * KT]

        def modulated(l, n, make, first=0):
            parts = [(a - first, b - first, (lambda c: lambda d: col(scale, l, n)(d, c))(c),
                      (lambda c: lambda d: shift(l, n)(d, c))(c))
                     for c, (a, b) in enumerate(((0, CTX), (CTX, TOK))) if b > first]
            make(f"norm {l} {n}", lambda d: X[:, d, first:TOK], TOK - first, parts)

        @contextmanager
        def split_region():
            with ExitStack() as c:
                local = new_in(c)
                k.WH, k.WL = (local(n, 2, 2048, dtype=F32R) for n in ("weights_hi", "weights_lo"))
                k.HH, k.HL = (local(n, KT, TOK, dtype=F32R) for n in ("normed_hi", "normed_lo"))
                yield local

        def modulated_split(l, n, first=0):
            with ExitStack() as c:
                work = new_in(c)("work", KT, TOK)
                modulated(l, n, lambda name, src, tokens, parts: norm_split(
                    k, name, src, lambda d: k.HH[:, d, first:TOK], lambda d: k.HL[:, d, first:TOK], tokens, parts, work), first)

        def mlp(l, n, first, ahead, fresh):
            modulated_split(l, 2 * n, first)
            with ExitStack() as c:
                local = new_in(c)
                hid = [local(f"hidden_{part}", FT, TOK, dtype=F32R) for part in ("hi", "lo")]
                silus, raw = local("silus", 2, TOK), local("gated", 2, TOK)
                gated_mlp(k, f"mlp {l} {n}", Layer(mlp1(l, n), mlp2(l, n), split=True, fresh=fresh),
                          Layer(mlp2(l, n), ahead, group=1, parts=2, split=True), first, col(gate, l, 2 * n), hid, silus, raw)

        start(k, w["w_ada"])
        with ExitStack() as c:
            modulation(k, mod, gate, scale, new_in(c)("pieces", 4, 256), mlp1(0, 0))
        with split_region():
            mlp(0, 0, 0, w["w_dn_qkv"], True)
        with ExitStack() as c:
            local = new_in(c)
            qkv, z = local("qkv", 24, TOK), local("z", KT, TOK)
            g, beta, gc, eg_neg, ekd, ea = (local(f"gates{n}", 8, 8) for n in range(6))
            both = lambda d: (k.HH[:, d, :], k.HL[:, d, :])
            with split_region() as region:
                modulated_split(0, 1)
                taps = k.C["dn_conv"]
                with ExitStack() as cc:
                    conv_silu(k, "delta qkv", Layer(w["w_dn_qkv"], w["w_dn_z"], fresh=True), both, 2, CTX, taps,
                              taps.shape[2] // 2, None, qkv, new_in(cc)("convs", 4, TOK))
                tmp = region("gates_tmp", 4, 8, 8)
                ab_parts = [region(f"w_ab_{part}", KT, 32, dtype=F32R) for part in ("hi", "lo")]
                delta_gates(k, Layer(w["w_dn_z"], w["w_dn_out"], split=True), z, ab_parts, g, beta, gc, eg_neg, ekd, ea, tmp)
            with ExitStack() as cc:
                late_constants(k, new_in(cc), ["level"])
                delta_heads(k, new_in(cc), qkv, z, g, beta, gc, eg_neg, ekd, ea)
            with split_region():
                to_residual(k, "delta out", Layer(w["w_dn_out"], mlp1(0, 1), fresh=True), both, TOK,
                            lambda dve, n, at, i: gated_residual(k, dve, n, at, 0, col(gate, 0, 1)),
                            split=([qkv[:, d, :] for d in range(KT)], [both(d) for d in range(KT)]))
        with split_region():
            mlp(0, 1, 0, mlp1(1, 0), True)
            mlp(1, 0, 0, w["w_swa_q"], False)
        swa(k, new_in, modulated, col(gate, 1, 1), mlp1(1, 1))
        with split_region():
            mlp(1, 1, CTX, w["w_conv"], True)
        second(k, new_in, w)
        return finish(k, out)


def finish(k, out):
    with k.open("finish") as block:
        @block.sync
        def _(sp):
            sp.dma_start(out, k.X[:, :, CTX:TOK]).then_inc(k.stored, 16)
            sp.wait_ge(k.stored, k.stores + 16)


def shape_constants():
    import numpy as np
    f = np.float32
    j, i = np.arange(P)[:, None], np.arange(P)[None, :]
    ahead = [j <= i, j >= i]
    level = []
    for d in range(2):
        for s in range(LEVELS):
            b = 1 << s
            late, early = (i, j) if d == 0 else (j, i)
            level.append((i // (2 * b) == j // (2 * b)) & (late // b % 2 == 1) & (early // b % 2 == 0))
    c = {
        "ident": np.eye(P, dtype=f),
        "ones": np.ones((P, P), f),
        "until": np.stack([a.astype(f) for a in ahead], 1),
        "behind": np.stack([np.where(a, f(0), f(-1e30)) for a in ahead], 1),
        "late_level": np.stack([a.astype(f) for a in level], 1),
    }
    half = 64
    c["late_ones64"] = (j // half == i // half).astype(f)
    rot = np.zeros((P, P), f)
    for m in range(P):
        rot[(m + 32, m) if m % half < 32 else (m - 32, m)] = -1 if m % half < 32 else 1
    c["late_rot"] = rot
    t = np.arange(LAT)
    inv = (f(10000.0) ** (-np.arange(16, dtype=f) / f(16))).astype(f)
    ang = np.concatenate([(t // 64).astype(f)[:, None] * inv, (t % 64).astype(f)[:, None] * inv], 1)
    cos, sin = (np.tile(fn(ang).astype(f).T, (4, 1)) for fn in (np.cos, np.sin))
    c["late_cos"] = np.concatenate([np.ones((P, CTX), f), cos], 1)
    c["late_sin"] = np.concatenate([np.zeros((P, CTX), f), sin], 1)
    q, key = np.arange(P)[:, None], np.arange(LAT)[None, :]
    window = [np.where(np.abs(q + P * b - key) <= 128, f(0), f(-1e30)) for b in range(2)]
    c["late_window"] = np.stack([np.concatenate([np.zeros((P, CTX), f), m], 1) for m in window], 1)
    dist = q + P - key
    c["late_band"] = np.where((dist >= 0) & (dist < 128), f(0), f(-1e30))
    x = np.arange(384)
    dist = 255 - x
    large = 16 + (np.log(np.maximum(dist, 1).astype(f) / f(16)) / f(np.log(128 / 16)) * f(16)).astype(np.int32)
    bucket = np.where(dist < 16, np.maximum(dist, 0), np.minimum(large, 31))
    c["late_bucket"] = (np.arange(32)[:, None] == bucket[None, :]).astype(f)
    return {n if n.startswith("late_") else "c_" + n: np.ascontiguousarray(a, dtype=f) for n, a in c.items()}


def pack(w, group):
    depth, n = w.shape[0] // P, w.shape[1] // P // group
    return w.reshape(depth, P, n, group, P).transpose(2, 1, 3, 0, 4).reshape(n, P, group * depth * P)


def halves(units):
    import numpy as np
    n, p, width = units.shape
    return units.reshape(n, p, 2, width // 2).transpose(0, 2, 1, 3).reshape(2 * n, p, width // 2)


def as_moving(w):
    n = w.shape[1] // 256
    return w.reshape(KT, P, n, 256).transpose(2, 1, 0, 3).reshape(n, P, KT * 256)


def columns(a):
    import numpy as np
    a = a.reshape(*a.shape[:-1], a.shape[-1] // P, P)
    return np.moveaxis(a, -1, 0)


def feature_major(a):
    return a.T.reshape(a.shape[1] // P, P, a.shape[0]).transpose(1, 0, 2)


def rows(a, *shape):
    import numpy as np
    return np.broadcast_to(a.reshape(shape), (P, *shape))


def layout(I):
    import numpy as np
    t = {}
    two = lambda a: np.stack([a, a], -1)
    t["w_ada"] = np.concatenate([as_moving(I["ada_w"][l]) for l in range(2)])
    t["w_ffn1"] = np.concatenate([
        pack(I["ffn_w1"][l, n].reshape(D, 2, FT, P).transpose(0, 2, 1, 3).reshape(D, 2 * FFN), 2)
        for l in range(2) for n in range(2)])
    t["w_ffn2"] = np.concatenate([halves(pack(I["ffn_w2"][l, n], 1)) for l in range(2) for n in range(2)])
    dn = I["dn_w_in"][0]
    t["w_dn_qkv"], t["w_dn_z"] = pack(dn[:, :3072], 2), pack(dn[:, 3072:4096], 2)
    t["c_w_dn_ab"] = dn[:, 4096:].reshape(KT, P, 32).transpose(1, 0, 2)
    t["w_dn_out"] = pack(I["dn_w_out"][0], 2)
    t["c_cond"] = columns(np.stack([I["c_ctx"], I["c"][0]])).transpose(0, 2, 1)
    t["c_ada_b"] = two(columns(I["ada_b"])).reshape(P, 288)
    t["c_norm_g"] = two(columns(I["norm_g"])).reshape(P, 2, 3, 16)
    t["c_dn_conv"] = columns(I["dn_conv"][0]).transpose(0, 2, 1)
    t["c_dn_dt_bias"] = rows(np.tile(I["dn_dt_bias"][0], (4, 1)), 8, 8)
    t["c_dn_a_log"] = rows(np.tile(I["dn_a_log"][0], (4, 1)), 8, 8)
    t["c_dn_o_gain"] = I["dn_o_gain"][0].reshape(P, 1)
    t["tokens"] = feature_major(np.concatenate([I["ctx"][0], I["x"][0]]))
    layout_swa(I, t)
    layout_second(I, t)
    t = {n: np.ascontiguousarray(a) for n, a in t.items()}
    t.update(shape_constants())
    return t


def kernel(**inputs):
    import numpy as np
    import concourse.bacc as bacc
    from concourse.bass_utils import run_bass_kernel_spmd

    arrays = layout({n: np.asarray(a) for n, a in inputs.items()})
    steps = {}
    for counted in (False, True):
        nc = bacc.Bacc("TRN2", target_bir_lowering=False, num_devices=1)
        dram = {n: nc.dram_tensor(n, list(a.shape), F32, kind="ExternalInput").ap() for n, a in arrays.items()}
        out = nc.dram_tensor("out", [P, KT, LAT], F32, kind="ExternalOutput").ap()
        build(nc, dram, out, steps, counted)
    got = run_bass_kernel_spmd(nc, [arrays], core_ids=[0]).results[0]["out"]
    return got.transpose(2, 1, 0).reshape(1, LAT, D)
```
